# Optimizing a Trainium2 kernel written in Bass

```python
import math
import jax, jax.numpy as jnp
from jax import lax
import numpy as np
import jax
import jax.numpy as jnp

D_MODEL = 1024
BATCH = 1
SEQ = 512
DEPTH = 2

CHUNK = 64
N_EVEN = (DEPTH + 1) // 2
N_ODD = DEPTH // 2
EPS = 1e-6

POOL_WIDTH = D_MODEL // 2
POOL_WINDOWS = (2, 4, 8, 16)
POOL_N_GROUPS = len(POOL_WINDOWS)
POOL_GROUP = POOL_WIDTH // POOL_N_GROUPS
ATT_HEAD_DIM = 64
ATT_HEADS = (D_MODEL // 2) // ATT_HEAD_DIM
ATT_WIDTH = ATT_HEADS * ATT_HEAD_DIM
ATT_PREV_CHUNKS = 8
REL_CLIP = 256
MIX_IN = POOL_WIDTH + 3 * ATT_WIDTH
MIX_OUT = POOL_WIDTH + ATT_WIDTH

SSM_EXPAND = 2
SSM_D_INNER = SSM_EXPAND * D_MODEL
SSM_HEAD_DIM = 64
SSM_HEADS = SSM_D_INNER // SSM_HEAD_DIM
SSM_GROUPS = 8
SSM_HEADS_PER_GROUP = SSM_HEADS // SSM_GROUPS
SSM_D_STATE = 128
SSM_D_CONV = 4
SSM_CONV_DIM = SSM_D_INNER + 2 * SSM_GROUPS * SSM_D_STATE
SSM_IN = SSM_D_INNER + SSM_CONV_DIM + SSM_HEADS
DT_MIN = 0.001
DT_MAX = 0.1

MOE_GROUPS = 4
MOE_EXPERTS_PER_GROUP = 8
MOE_EXPERTS = MOE_GROUPS * MOE_EXPERTS_PER_GROUP
MOE_TOP_K = 2
MOE_D_FF = D_MODEL // 8


def rmsnorm(x, w):
    xf = x.astype(jnp.float32)
    y = xf * lax.rsqrt(jnp.mean(xf * xf, axis=-1, keepdims=True) + EPS)
    return (y * w.astype(jnp.float32)).astype(x.dtype)

def modulate(h, shift, scale):
    return h * (1 + scale[:, None, :]) + shift[:, None, :]

def pool_mixer(u, pool_w, pool_scale):
    b, s, _ = u.shape
    uf = u.astype(jnp.float32)
    cs = jnp.pad(jnp.cumsum(uf, axis=1), ((0, 0), (1, 0), (0, 0)))
    pos = jnp.arange(1, s + 1, dtype=jnp.float32)
    outs = []
    for g, w in enumerate(POOL_WINDOWS):
        lo, hi = g * POOL_GROUP, (g + 1) * POOL_GROUP
        upper = cs[:, 1:, lo:hi]
        lower = jnp.pad(cs[:, :s + 1 - w, lo:hi], ((0, 0), (w - 1, 0), (0, 0)))
        count = jnp.minimum(pos, w)[None, :, None]
        outs.append((upper - lower) / count - uf[:, :, lo:hi])
    pooled = jnp.stack(outs, axis=2).astype(u.dtype)
    y = jnp.einsum('bsgc,gcd->bsgd', pooled, pool_w).reshape(b, s, POOL_WIDTH)
    return y * pool_scale

def chunk_attention(q, k, v, rel_bias):
    b, s, _ = q.shape
    nc = s // CHUNK
    band = (ATT_PREV_CHUNKS + 1) * CHUNK
    q = q.reshape(b, nc, CHUNK, ATT_HEADS, ATT_HEAD_DIM)
    k = k.reshape(b, nc, CHUNK, ATT_HEADS, ATT_HEAD_DIM)
    v = v.reshape(b, nc, CHUNK, ATT_HEADS, ATT_HEAD_DIM)
    pad = ((0, 0), (ATT_PREV_CHUNKS, 0), (0, 0), (0, 0), (0, 0))
    kp = jnp.pad(k, pad)
    vp = jnp.pad(v, pad)
    k_band = jnp.concatenate([kp[:, j:j + nc] for j in range(ATT_PREV_CHUNKS + 1)], axis=2)
    v_band = jnp.concatenate([vp[:, j:j + nc] for j in range(ATT_PREV_CHUNKS + 1)], axis=2)
    q_off = jnp.arange(CHUNK)[:, None] + ATT_PREV_CHUNKS * CHUNK
    k_off = jnp.arange(band)[None, :]
    rel_idx = jnp.clip(q_off - k_off, -REL_CLIP, REL_CLIP) + REL_CLIP
    bias = rel_bias[:, rel_idx].astype(jnp.float32)
    key_chunk = jnp.arange(nc)[:, None] - ATT_PREV_CHUNKS + jnp.arange(band)[None, :] // CHUNK
    valid = key_chunk >= 0
    scores = jnp.einsum('bclhd,bcshd->bchls', q, k_band).astype(jnp.float32) * (ATT_HEAD_DIM ** -0.5)
    scores = scores + bias[None, None]
    scores = jnp.where(valid[None, :, None, None, :], scores, -1e30)
    p = jax.nn.softmax(scores, axis=-1).astype(v.dtype)
    o = jnp.einsum('bchls,bcshd->bclhd', p, v_band)
    return o.reshape(b, s, ATT_WIDTH)

def mamba2_mixer(h, w_in, conv_w, conv_b, dt_bias, A_log, D_skip, norm_w, w_out):
    b, s, _ = h.shape
    nc = s // CHUNK
    G, R, P, N = SSM_GROUPS, SSM_HEADS_PER_GROUP, SSM_HEAD_DIM, SSM_D_STATE
    f32 = jnp.float32
    zxbcdt = h @ w_in
    z, xbc, dt = jnp.split(zxbcdt, [SSM_D_INNER, SSM_D_INNER + SSM_CONV_DIM], axis=-1)
    xp = jnp.pad(xbc, ((0, 0), (SSM_D_CONV - 1, 0), (0, 0)))
    conv = xp[:, 0:s] * conv_w[0]
    for tap in range(1, SSM_D_CONV):
        conv = conv + xp[:, tap:tap + s] * conv_w[tap]
    xbc = jax.nn.silu(conv + conv_b)
    xs, Bm, Cm = jnp.split(xbc, [SSM_D_INNER, SSM_D_INNER + G * N], axis=-1)
    dt = jax.nn.softplus(dt.astype(f32) + dt_bias.astype(f32))
    A = -jnp.exp(A_log.astype(f32))
    a = (dt * A).reshape(b, nc, CHUNK, G, R)
    xs = xs.astype(f32).reshape(b, nc, CHUNK, G, R, P)
    x_dt = xs * dt.reshape(b, nc, CHUNK, G, R)[..., None]
    Bm = Bm.astype(f32).reshape(b, nc, CHUNK, G, N)
    Cm = Cm.astype(f32).reshape(b, nc, CHUNK, G, N)
    a_cs = jnp.moveaxis(jnp.cumsum(a, axis=2), 2, -1)
    tril = jnp.tril(jnp.ones((CHUNK, CHUNK), dtype=bool))
    seg = jnp.exp(jnp.where(tril, a_cs[..., :, None] - a_cs[..., None, :], -jnp.inf))
    cb = jnp.einsum('bclgn,bcsgn->bcgls', Cm, Bm)
    y_diag = jnp.einsum('bcgls,bcgrls,bcsgrp->bclgrp', cb, seg, x_dt)
    decay_states = jnp.exp(a_cs[..., -1:] - a_cs)
    states = jnp.einsum('bclgn,bcgrl,bclgrp->bcgrpn', Bm, decay_states, x_dt)
    chunk_decay = jnp.exp(a_cs[..., -1])

    def step(carry, inp):
        st, dec = inp
        return carry * dec[..., None, None] + st, carry

    init = jnp.zeros((b, G, R, P, N), f32)
    _, prev = lax.scan(step, init, (jnp.moveaxis(states, 1, 0), jnp.moveaxis(chunk_decay, 1, 0)))
    prev = jnp.moveaxis(prev, 0, 1)
    y_off = jnp.einsum('bclgn,bcgrpn,bcgrl->bclgrp', Cm, prev, jnp.exp(a_cs))
    y = y_diag + y_off + xs * D_skip.astype(f32).reshape(G, R)[:, :, None]
    y = y.reshape(b, s, SSM_D_INNER)
    g = (y * jax.nn.silu(z.astype(f32))).reshape(b, s, G, SSM_D_INNER // G)
    g = g * lax.rsqrt(jnp.mean(g * g, axis=-1, keepdims=True) + EPS)
    g = g.reshape(b, s, SSM_D_INNER) * norm_w.astype(f32)
    return g.astype(h.dtype) @ w_out

def hier_moe(h, w_group, b_group, w_expert, b_expert, w1, w3, w2):
    b, s, d = h.shape
    t = h.reshape(b * s, d)
    tf = t.astype(jnp.float32)
    g_prob = jax.nn.softmax(tf @ w_group.astype(jnp.float32) + b_group.astype(jnp.float32), axis=-1)
    g_val, g_idx = lax.top_k(g_prob, 1)
    e_logits = jnp.einsum('td,dge->tge', tf, w_expert.astype(jnp.float32)) + b_expert.astype(jnp.float32)
    e_logits = e_logits[jnp.arange(b * s), g_idx[:, 0]]
    e_val, e_idx = lax.top_k(jax.nn.softmax(e_logits, axis=-1), MOE_TOP_K)
    e_val = e_val / jnp.sum(e_val, axis=-1, keepdims=True)
    weights = g_val * e_val
    expert_id = g_idx * MOE_EXPERTS_PER_GROUP + e_idx
    combine = jnp.sum(jax.nn.one_hot(expert_id, MOE_EXPERTS, dtype=jnp.float32) * weights[..., None], axis=1)
    hid = jax.nn.silu(jnp.einsum('td,edf->tef', t, w1)) * jnp.einsum('td,edf->tef', t, w3)
    hid = hid * combine.astype(hid.dtype)[:, :, None]
    y = jnp.einsum('tef,efd->td', hid, w2)
    return y.reshape(b, s, d)

def _normal(key, shape, scale):
    return jax.random.normal(key, shape, jnp.float32) * scale

def first_inputs(seed: int = 0) -> dict:
    key = jax.random.key(seed)
    ks = jax.random.split(key, 28)
    D = D_MODEL
    f32 = jnp.float32
    dt0 = jnp.exp(jax.random.uniform(ks[14], (N_ODD, SSM_HEADS), f32) * (math.log(DT_MAX) - math.log(DT_MIN)) + math.log(DT_MIN))
    dt0 = jnp.maximum(dt0, 1e-4)
    return {
        'x': _normal(ks[0], (BATCH, SEQ, D), 1.0),
        'c': _normal(ks[1], (BATCH, D), 1.0),
        'ada_w': _normal(ks[2], (DEPTH, D, 6 * D), 0.5 * D ** -0.5),
        'ada_b': _normal(ks[3], (DEPTH, 6 * D), 0.02),
        'norm1_w': 1.0 + _normal(ks[4], (DEPTH, D), 0.05),
        'norm2_w': 1.0 + _normal(ks[5], (DEPTH, D), 0.05),
        'mix_w_in': _normal(ks[6], (N_EVEN, D, MIX_IN), D ** -0.5),
        'pool_w': _normal(ks[7], (N_EVEN, POOL_N_GROUPS, POOL_GROUP, POOL_GROUP), POOL_GROUP ** -0.5),
        'pool_scale': 1.0 + _normal(ks[8], (N_EVEN, POOL_WIDTH), 0.05),
        'rel_bias': _normal(ks[9], (N_EVEN, ATT_HEADS, 2 * REL_CLIP + 1), 0.2),
        'mix_w_out': _normal(ks[10], (N_EVEN, MIX_OUT, D), MIX_OUT ** -0.5),
        'ssm_w_in': _normal(ks[11], (N_ODD, D, SSM_IN), D ** -0.5),
        'ssm_conv_w': _normal(ks[12], (N_ODD, SSM_D_CONV, SSM_CONV_DIM), SSM_D_CONV ** -0.5),
        'ssm_conv_b': _normal(ks[13], (N_ODD, SSM_CONV_DIM), 0.02),
        'ssm_dt_bias': dt0 + jnp.log(-jnp.expm1(-dt0)),
        'ssm_A_log': jnp.log(jax.random.uniform(ks[15], (N_ODD, SSM_HEADS), f32, 1.0, 16.0)),
        'ssm_D': 1.0 + _normal(ks[16], (N_ODD, SSM_HEADS), 0.1),
        'ssm_norm_w': 1.0 + _normal(ks[17], (N_ODD, SSM_D_INNER), 0.05),
        'ssm_w_out': _normal(ks[18], (N_ODD, SSM_D_INNER, D), SSM_D_INNER ** -0.5),
        'moe_w_group': _normal(ks[19], (DEPTH, D, MOE_GROUPS), D ** -0.5),
        'moe_b_group': _normal(ks[20], (DEPTH, MOE_GROUPS), 0.01),
        'moe_w_expert': _normal(ks[21], (DEPTH, D, MOE_GROUPS, MOE_EXPERTS_PER_GROUP), D ** -0.5),
        'moe_b_expert': _normal(ks[22], (DEPTH, MOE_GROUPS, MOE_EXPERTS_PER_GROUP), 0.01),
        'moe_w1': _normal(ks[23], (DEPTH, MOE_EXPERTS, D, MOE_D_FF), D ** -0.5),
        'moe_w3': _normal(ks[24], (DEPTH, MOE_EXPERTS, D, MOE_D_FF), D ** -0.5),
        'moe_w2': _normal(ks[25], (DEPTH, MOE_EXPERTS, MOE_D_FF, D), MOE_D_FF ** -0.5),
        'final_norm_w': 1.0 + _normal(ks[26], (D,), 0.05),
    }

def first_block(x, c, ada_w, ada_b, norm1_w, norm2_w, mix_w_in, pool_w, pool_scale, rel_bias, mix_w_out,
              ssm_w_in, ssm_conv_w, ssm_conv_b, ssm_dt_bias, ssm_A_log, ssm_D, ssm_norm_w, ssm_w_out,
              moe_w_group, moe_b_group, moe_w_expert, moe_b_expert, moe_w1, moe_w3, moe_w2, final_norm_w):
    c_act = jax.nn.silu(c)
    for layer in range(DEPTH):
        mod = c_act @ ada_w[layer] + ada_b[layer]
        shift1, scale1, gate1, shift2, scale2, gate2 = jnp.split(mod, 6, axis=-1)
        h = modulate(rmsnorm(x, norm1_w[layer]), shift1, scale1)
        i = layer // 2
        if layer % 2 == 0:
            proj = h @ mix_w_in[i]
            u, q, k, v = jnp.split(proj, [POOL_WIDTH, POOL_WIDTH + ATT_WIDTH, POOL_WIDTH + 2 * ATT_WIDTH], axis=-1)
            a_out = pool_mixer(u, pool_w[i], pool_scale[i])
            b_out = chunk_attention(q, k, v, rel_bias[i])
            mix = jnp.concatenate([a_out, b_out], axis=-1) @ mix_w_out[i]
        else:
            mix = mamba2_mixer(h, ssm_w_in[i], ssm_conv_w[i], ssm_conv_b[i], ssm_dt_bias[i], ssm_A_log[i],
                               ssm_D[i], ssm_norm_w[i], ssm_w_out[i])
        x = x + gate1[:, None, :] * mix
        h2 = modulate(rmsnorm(x, norm2_w[layer]), shift2, scale2)
        ffn = hier_moe(h2, moe_w_group[layer], moe_b_group[layer], moe_w_expert[layer], moe_b_expert[layer],
                       moe_w1[layer], moe_w3[layer], moe_w2[layer])
        x = x + gate2[:, None, :] * ffn
    return rmsnorm(x, final_norm_w)


CTX_LEN = 256
GRID_W = 64
N_BRANCH = 4
BRANCH_W = D_MODEL // 2
RET_HEADS = 4
RET_DH = BRANCH_W // RET_HEADS
RET_CHUNK = 128
SC_KERNEL = 3
CF_KERNEL = 31
ATT_HEADS_2 = 8
ATT_KV_HEADS = 2
ATT_DH = BRANCH_W // ATT_HEADS_2
ATT_KV_W = ATT_KV_HEADS * ATT_DH
ATT_BLOCK = 128
WINDOW = 128
ROPE_BASE = 10000.0
ROPE_AXIS_FREQS = ATT_DH // 4
NEG_INF = -1e30

IN_NAMES = ('ret_q', 'ret_k', 'ret_v', 'ret_z',
            'sc_b', 'sc_c', 'sc_x', 'sc_z',
            'cf_glu', 'cf_z',
            'att_q', 'att_k', 'att_v', 'att_z',
            'merge_gates')
IN_SIZES = (BRANCH_W, BRANCH_W, BRANCH_W, BRANCH_W,
            BRANCH_W, BRANCH_W, BRANCH_W, BRANCH_W,
            2 * BRANCH_W, BRANCH_W,
            BRANCH_W, ATT_KV_W, ATT_KV_W, BRANCH_W,
            N_BRANCH * D_MODEL)
IN_TOTAL = sum(IN_SIZES)


def split_proj(y):
    offsets = [int(o) for o in np.cumsum(IN_SIZES)[:-1]]
    return dict(zip(IN_NAMES, jnp.split(y, offsets, axis=-1)))

def in_cols(w, name):
    i = IN_NAMES.index(name)
    start = sum(IN_SIZES[:i])
    return w[:, start:start + IN_SIZES[i]]

def heads(t, n):
    return t.reshape(t.shape[:-1] + (n, t.shape[-1] // n))

def rmsnorm_2(x, w):
    xf = x.astype(jnp.float32)
    y = xf * lax.rsqrt(jnp.mean(xf * xf, axis=-1, keepdims=True) + EPS)
    return (y * w).astype(x.dtype)

def layer_norm(u, w, b):
    uf = u.astype(jnp.float32)
    mu = jnp.mean(uf, axis=-1, keepdims=True)
    var = jnp.mean(jnp.square(uf - mu), axis=-1, keepdims=True)
    return (uf - mu) * lax.rsqrt(var + EPS) * w + b

def head_group_norm(o, w):
    of = o.astype(jnp.float32)
    mu = jnp.mean(of, axis=-1, keepdims=True)
    var = jnp.mean(jnp.square(of - mu), axis=-1, keepdims=True)
    y = (of - mu) * lax.rsqrt(var + EPS)
    return y.reshape(o.shape[:-2] + (-1,)) * w

def ada_modulation(cvec, w, b):
    m = jax.nn.silu(cvec) @ w + b
    return jnp.split(m, 3, axis=-1)

def modulate_2(h, shift, scale):
    return h * (1 + scale) + shift

def depthwise_conv(u, w):
    K, C = w.shape
    return lax.conv_general_dilated(
        u, w[:, None, :].astype(u.dtype), window_strides=(1,), padding=[(K // 2, K // 2)],
        dimension_numbers=('NWC', 'WIO', 'NWC'), feature_group_count=C)

def axial_rope_tables(row, col):
    inv = ROPE_BASE ** (-jnp.arange(ROPE_AXIS_FREQS, dtype=jnp.float32) / ROPE_AXIS_FREQS)
    ang = jnp.concatenate([row.astype(jnp.float32)[:, None] * inv[None],
                           col.astype(jnp.float32)[:, None] * inv[None]], axis=-1)
    return jnp.cos(ang)[:, None, :], jnp.sin(ang)[:, None, :]

def axial_rope(t, cos, sin):
    half = t.shape[-1] // 2
    t1 = t[..., :half].astype(jnp.float32)
    t2 = t[..., half:].astype(jnp.float32)
    return jnp.concatenate([t1 * cos - t2 * sin, t2 * cos + t1 * sin], axis=-1).astype(t.dtype)

def retention_dir(q, k, v, log_gamma, s0, strict):
    B, N, H, d = q.shape
    C = RET_CHUNK
    nc = N // C
    qc, kc, vc = (t.reshape(B, nc, C, H, d) for t in (q, k, v))
    pos = jnp.arange(C)
    diff = pos[:, None] - pos[None, :]
    keep = (diff > 0) if strict else (diff >= 0)
    expo = jnp.where(keep, diff, 0).astype(jnp.float32)
    decay = jnp.where(keep[None], jnp.exp(expo[None] * log_gamma[:, None, None]), 0.0)
    scores = jnp.einsum('bnihd,bnjhd->bnhij', qc, kc) * decay
    intra = jnp.einsum('bnhij,bnjhe->bnihe', scores, vc)
    posf = pos.astype(jnp.float32)
    k_w = jnp.exp((C - 1 - posf)[:, None] * log_gamma[None])
    q_w = jnp.exp((posf + 1)[:, None] * log_gamma[None])
    kv = jnp.einsum('bnjhd,jh,bnjhe->nbhde', kc, k_w, vc)
    chunk_decay = jnp.exp(C * log_gamma)[None, :, None, None]

    def step(s, kv_c):
        return s * chunk_decay + kv_c, s

    s_final, s_prev = lax.scan(step, s0, kv)
    cross = jnp.einsum('bnihd,ih,nbhde->bnihe', qc, q_w, s_prev)
    return (intra + cross).reshape(B, N, H, d), s_final

def retention_bidir(q, k, v, log_gamma, s0_f, s0_b):
    out_f, s_f = retention_dir(q, k, v, log_gamma[0], s0_f, False)
    flip = lambda t: jnp.flip(t, axis=1)
    out_b, s_b = retention_dir(flip(q), flip(k), flip(v), log_gamma[1], s0_b, True)
    return out_f + flip(out_b), s_f, s_b

def retention_context_states(k, v, log_gamma):
    L = k.shape[1]
    pos = jnp.arange(L, dtype=jnp.float32)
    w_f = jnp.exp((L - 1 - pos)[:, None] * log_gamma[0][None])
    w_b = jnp.exp(pos[:, None] * log_gamma[1][None])
    s_f = jnp.einsum('blhd,lh,blhe->bhde', k, w_f, v)
    s_b = jnp.einsum('blhd,lh,blhe->bhde', k, w_b, v)
    return s_f, s_b

def windowed_gqa(q, k, v, k_ctx, v_ctx, sink):
    B, S, H, d = q.shape
    G = H // ATT_KV_HEADS
    nb = S // ATT_BLOCK
    L = k_ctx.shape[1]
    qb = q.reshape(B, nb, ATT_BLOCK, ATT_KV_HEADS, G, d)

    def band(t):
        tp = jnp.pad(t, ((0, 0), (ATT_BLOCK, ATT_BLOCK), (0, 0), (0, 0)))
        tp = tp.reshape(B, nb + 2, ATT_BLOCK, ATT_KV_HEADS, d)
        return jnp.concatenate([tp[:, :-2], tp[:, 1:-1], tp[:, 2:]], axis=2)

    kw, vw = band(k), band(v)
    qi = jnp.arange(ATT_BLOCK)
    kj = jnp.arange(3 * ATT_BLOCK) - ATT_BLOCK
    in_band = jnp.abs(kj[None, :] - qi[:, None]) <= WINDOW
    key_pos = jnp.arange(nb)[:, None] * ATT_BLOCK + kj[None, :]
    in_seq = (key_pos >= 0) & (key_pos < S)
    mask = in_band[None] & in_seq[:, None, :]
    scale = d ** -0.5
    s_loc = jnp.einsum('bnqhgd,bnkhd->bnhgqk', qb, kw).astype(jnp.float32) * scale
    s_loc = jnp.where(mask[None, :, None, None], s_loc, NEG_INF)
    s_ctx = jnp.einsum('bnqhgd,bchd->bnhgqc', qb, k_ctx).astype(jnp.float32) * scale
    s_sink = jnp.broadcast_to(sink.astype(jnp.float32).reshape(ATT_KV_HEADS, G, 1, 1),
                              s_loc.shape[:-1] + (1,))
    p = jax.nn.softmax(jnp.concatenate([s_loc, s_ctx, s_sink], axis=-1), axis=-1)
    nk = 3 * ATT_BLOCK
    p_loc = p[..., :nk].astype(v.dtype)
    p_ctx = p[..., nk:nk + L].astype(v.dtype)
    o = (jnp.einsum('bnhgqk,bnkhd->bnqhgd', p_loc, vw)
         + jnp.einsum('bnhgqc,bchd->bnqhgd', p_ctx, v_ctx))
    return o.reshape(B, S, H * d)

def context_attention(q, k, v, sink):
    B, L, H, d = q.shape
    G = H // ATT_KV_HEADS
    qg = q.reshape(B, L, ATT_KV_HEADS, G, d)
    s = jnp.einsum('bqhgd,bkhd->bhgqk', qg, k).astype(jnp.float32) * d ** -0.5
    s_sink = jnp.broadcast_to(sink.astype(jnp.float32).reshape(ATT_KV_HEADS, G, 1, 1), s.shape[:-1] + (1,))
    p = jax.nn.softmax(jnp.concatenate([s, s_sink], axis=-1), axis=-1)[..., :L]
    o = jnp.einsum('bhgqk,bkhd->bqhgd', p.astype(v.dtype), v)
    return o.reshape(B, L, H * d)

def short_conv(b_gate, c_gate, xv, w):
    return b_gate * depthwise_conv(c_gate * xv, w)

def conformer_conv(glu_in, w, bias, ln_w, ln_b):
    a, g = jnp.split(glu_in, 2, axis=-1)
    u = depthwise_conv(a * jax.nn.sigmoid(g), w) + bias
    return jax.nn.silu(layer_norm(u, ln_w, ln_b)).astype(glu_in.dtype)

def mixer_output(p, ret_o, att_o, ret_gn_w, sc_conv_w, cf_conv_w, cf_conv_b, cf_ln_w, cf_ln_b,
                 w_branch, w_out):
    dt = p['ret_z'].dtype
    r = (head_group_norm(ret_o, ret_gn_w) * jax.nn.silu(p['ret_z'])).astype(dt)
    s = short_conv(p['sc_b'], p['sc_c'], p['sc_x'], sc_conv_w) * jax.nn.silu(p['sc_z'])
    f = conformer_conv(p['cf_glu'], cf_conv_w, cf_conv_b, cf_ln_w, cf_ln_b) * jax.nn.silu(p['cf_z'])
    a = att_o * jax.nn.silu(p['att_z'])
    gates = jnp.split(p['merge_gates'], N_BRANCH, axis=-1)
    merged = sum(jax.nn.sigmoid(g) * (br @ w_branch[i])
                 for i, (g, br) in enumerate(zip(gates, (r, s, f, a))))
    return merged @ w_out

def second_inputs(seed: int = 0) -> dict:
    key = jax.random.key(seed)
    ks = jax.random.split(key, 20)
    f32 = jnp.float32
    D = D_MODEL

    def nrm(k, shape, fan_in):
        return jax.random.normal(k, shape, f32) * fan_in ** -0.5

    decay_logit = jnp.log(2.0 ** (5.0 + jnp.arange(RET_HEADS, dtype=f32)) - 1.0)
    return {
        'x': jax.random.normal(ks[0], (BATCH, SEQ, D), f32),
        'c': jax.random.normal(ks[1], (BATCH, D), f32),
        'ctx': jax.random.normal(ks[2], (BATCH, CTX_LEN, D), f32),
        'c_ctx': jax.random.normal(ks[3], (D,), f32),
        'w_mod': nrm(ks[4], (DEPTH, D, 3 * D), D),
        'b_mod': 0.02 * jax.random.normal(ks[5], (DEPTH, 3 * D), f32),
        'norm_w': 1.0 + 0.1 * jax.random.normal(ks[6], (DEPTH, D), f32),
        'w_in': nrm(ks[7], (DEPTH, D, IN_TOTAL), D),
        'ret_decay': decay_logit[None, None, :] + 0.1 * jax.random.normal(ks[8], (DEPTH, 2, RET_HEADS), f32),
        'ret_gn_w': 1.0 + 0.1 * jax.random.normal(ks[9], (DEPTH, BRANCH_W), f32),
        'sc_conv_w': nrm(ks[10], (DEPTH, SC_KERNEL, BRANCH_W), SC_KERNEL),
        'cf_conv_w': nrm(ks[11], (DEPTH, CF_KERNEL, BRANCH_W), CF_KERNEL),
        'cf_conv_b': 0.02 * jax.random.normal(ks[12], (DEPTH, BRANCH_W), f32),
        'cf_ln_w': 1.0 + 0.1 * jax.random.normal(ks[13], (DEPTH, BRANCH_W), f32),
        'cf_ln_b': 0.02 * jax.random.normal(ks[14], (DEPTH, BRANCH_W), f32),
        'att_sink': jax.random.normal(ks[15], (DEPTH, ATT_HEADS_2), f32),
        'w_branch': nrm(ks[16], (DEPTH, N_BRANCH, BRANCH_W, D), BRANCH_W),
        'w_out': nrm(ks[17], (DEPTH, D, D), D),
        'final_norm_w': 1.0 + 0.1 * jax.random.normal(ks[18], (D,), f32),
    }

def second_block(x, c, ctx, c_ctx, w_mod, b_mod, norm_w, w_in, ret_decay, ret_gn_w, sc_conv_w,
              cf_conv_w, cf_conv_b, cf_ln_w, cf_ln_b, att_sink, w_branch, w_out, final_norm_w):
    B, S, _ = x.shape
    ROWS = S // GRID_W
    row = jnp.repeat(jnp.arange(ROWS), GRID_W)
    col = jnp.tile(jnp.arange(GRID_W), ROWS)
    cos, sin = axial_rope_tables(row, col)
    k_scale = RET_DH ** -0.5
    xc = ctx
    for l in range(DEPTH):
        ctx_out_needed = l < DEPTH - 1
        log_gamma = jax.nn.log_sigmoid(ret_decay[l].astype(jnp.float32))
        shift_x, scale_x, gate_x = ada_modulation(c, w_mod[l], b_mod[l])
        shift_c, scale_c, gate_c = ada_modulation(c_ctx, w_mod[l], b_mod[l])
        hx = modulate_2(rmsnorm_2(x, norm_w[l]), shift_x[:, None], scale_x[:, None])
        hc = modulate_2(rmsnorm_2(xc, norm_w[l]), shift_c, scale_c)
        px = split_proj(hx @ w_in[l])
        if ctx_out_needed:
            pc = split_proj(hc @ w_in[l])
        else:
            pc = {n: hc @ in_cols(w_in[l], n) for n in ('ret_k', 'ret_v', 'att_k', 'att_v')}
        rk_c = heads(pc['ret_k'], RET_HEADS) * k_scale
        rv_c = heads(pc['ret_v'], RET_HEADS)
        ak_c = heads(pc['att_k'], ATT_KV_HEADS)
        av_c = heads(pc['att_v'], ATT_KV_HEADS)
        if ctx_out_needed:
            zero = jnp.zeros((B, RET_HEADS, RET_DH, RET_DH), jnp.float32)
            ret_c, s_f, s_b = retention_bidir(heads(pc['ret_q'], RET_HEADS), rk_c, rv_c, log_gamma, zero, zero)
            att_c = context_attention(heads(pc['att_q'], ATT_HEADS_2), ak_c, av_c, att_sink[l])
            out_c = mixer_output(pc, ret_c, att_c, ret_gn_w[l], sc_conv_w[l], cf_conv_w[l], cf_conv_b[l],
                                 cf_ln_w[l], cf_ln_b[l], w_branch[l], w_out[l])
        else:
            s_f, s_b = retention_context_states(rk_c, rv_c, log_gamma)
        ret_x, _, _ = retention_bidir(heads(px['ret_q'], RET_HEADS), heads(px['ret_k'], RET_HEADS) * k_scale,
                                      heads(px['ret_v'], RET_HEADS), log_gamma, s_f, s_b)
        att_x = windowed_gqa(axial_rope(heads(px['att_q'], ATT_HEADS_2), cos, sin),
                             axial_rope(heads(px['att_k'], ATT_KV_HEADS), cos, sin),
                             heads(px['att_v'], ATT_KV_HEADS), ak_c, av_c, att_sink[l])
        out_x = mixer_output(px, ret_x, att_x, ret_gn_w[l], sc_conv_w[l], cf_conv_w[l], cf_conv_b[l],
                             cf_ln_w[l], cf_ln_b[l], w_branch[l], w_out[l])
        x = x + gate_x[:, None] * out_x
        if ctx_out_needed:
            xc = xc + gate_c * out_c
    return rmsnorm_2(x, final_norm_w)


def setup_inputs(seed=0):
    out = dict(first_inputs(seed))
    for name, value in second_inputs(seed + 1).items():
        if name != "x":
            out[name + "_2"] = value
    return out


def reference(
    x, c, ada_w, ada_b, norm1_w, norm2_w, mix_w_in, pool_w, pool_scale, rel_bias, mix_w_out,
    ssm_w_in, ssm_conv_w, ssm_conv_b, ssm_dt_bias, ssm_A_log, ssm_D, ssm_norm_w, ssm_w_out,
    moe_w_group, moe_b_group, moe_w_expert, moe_b_expert, moe_w1, moe_w3, moe_w2, final_norm_w,
    c_2, ctx_2, c_ctx_2, w_mod_2, b_mod_2, norm_w_2, w_in_2, ret_decay_2, ret_gn_w_2,
    sc_conv_w_2, cf_conv_w_2, cf_conv_b_2, cf_ln_w_2, cf_ln_b_2, att_sink_2, w_branch_2,
    w_out_2, final_norm_w_2,
):
    x = first_block(
        x, c, ada_w, ada_b, norm1_w, norm2_w, mix_w_in, pool_w, pool_scale, rel_bias, mix_w_out,
        ssm_w_in, ssm_conv_w, ssm_conv_b, ssm_dt_bias, ssm_A_log, ssm_D, ssm_norm_w, ssm_w_out,
        moe_w_group, moe_b_group, moe_w_expert, moe_b_expert, moe_w1, moe_w3, moe_w2,
        final_norm_w,
    )
    return second_block(
        x, c_2, ctx_2, c_ctx_2, w_mod_2, b_mod_2, norm_w_2, w_in_2, ret_decay_2, ret_gn_w_2,
        sc_conv_w_2, cf_conv_w_2, cf_conv_b_2, cf_ln_w_2, cf_ln_b_2, att_sink_2, w_branch_2,
        w_out_2, final_norm_w_2,
    )


_drawn_inputs = setup_inputs


def setup_inputs(seed=0):
    import zlib

    import numpy as np

    out = dict(_drawn_inputs(seed))
    spreads = {}
    factors = {'rel_bias': 3.024,
     'ssm_conv_b': 3.513,
     'moe_b_group': 4.255,
     'moe_b_expert': 4.02,
     'cf_conv_b_2': 8.0,
     'cf_ln_b_2': 8.0,
     'att_sink_2': 8.0}
    for name, (base, spread) in spreads.items():
        noise = np.random.default_rng([zlib.crc32(name.encode()), seed]).standard_normal(out[name].shape)
        drawn = base * np.exp(spread * noise) if base else spread * noise
        out[name] = jnp.asarray(drawn.astype(out[name].dtype))
    for name, factor in factors.items():
        out[name] = (out[name] * factor).astype(out[name].dtype)
    return out
```

```python
from contextlib import ExitStack, contextmanager

import concourse.bass as bass
from concourse import mybir

F32 = mybir.dt.float32
ALU = mybir.AluOpType
ACT = mybir.ActivationFunctionType
AX = mybir.AxisListType.X

P = 128
S = 512
L = 256
D = 1024
KD = D // P
EPS = 1e-6
RING = 8
BANKS = 8
CW = 783
CO = S + 15

VEC_ROWS = [
    ("c", 8), ("norm1_w", 16), ("norm2_w", 16), ("final_norm_w", 8), ("pool_scale", 4), ("c_2", 8),
    ("c_ctx_2", 8), ("norm_w_2", 16), ("final_norm_w_2", 8), ("ssm_norm_w", 16), ("ssm_D", 16), ("pad0", 4),
    ("ada_b", 96), ("cf_conv_b_2", 8), ("cf_ln_w_2", 8), ("cf_ln_b_2", 8), ("ret_gn_w_2", 8),
    ("ssm_conv_w", 128),
    ("ssm_conv_b", 32), ("b_mod_2", 48), ("sc_conv_w_2", 24), ("pad1", 24),
    ("cf_conv_w_2a", 124), ("pad2", 4), ("cf_conv_w_2b", 124), ("pad3", 4),
]
VEC = {}
_row = 0
for _name, _n in VEC_ROWS:
    VEC[_name] = _row
    _row += _n
VT = _row // P

CONST_COLS = [("ident", P), ("mask_next", S), ("window", 3 * P), ("rank", 8), ("inv_count", 64),
              ("rot", P), ("cos", S), ("sin", S),
              ("dplus", 896), ("dminus", 896), ("to_end", S), ("to_start", S)]
CONST = {}
_col = 0
for _name, _n in CONST_COLS:
    CONST[_name] = (_col, _n)
    _col += _n
CONST_W = _col
CONST1_W = CONST["rot"][0]


class Count:

    def __init__(self, eng, key, sems, old, new):
        self.eng, self.key, self.sems, self.old, self.new = eng, key, sems, old, new
        self.n, self.local = {}, {}
        self.loop_name, self.i, self.last = None, None, None

    def landing(self, key, name):
        return self._bump(key, 16, name)

    def step(self, name=None):
        return self._bump(self.key, 1, name)

    def _bump(self, key, amount, name):
        book = self.n if self.loop_name is None else self.local
        book[key] = book.get(key, 0) + amount
        at = (key, self.loop_name, book[key])
        for x in name if isinstance(name, list) else [name]:
            if x is not None:
                self.new[x] = at
        if key == self.key:
            self.last = at
        return amount

    def _value(self, at, lag=0):
        key, loop, value = at
        if loop is None:
            return value
        base, per, count = self.old.get(("loop", loop, key), (0, 1, 1))
        if loop == self.loop_name:
            return self.i * per + (base + value - lag * per)
        return base + (count - 1) * per + value

    def at(self, name, lag=0):
        return self._value(self.old[name], lag) if self.old else 1

    def own(self):
        return self._value(self.last)

    def doer(self, name):
        return self.sems(self.old[name][0] if self.old else self.key)

    @contextmanager
    def loop(self, name, count):
        base = dict(self.n)
        self.local, self.last = {}, None
        with self.eng.Fori(0, count) as i:
            self.loop_name, self.i = name, i
            yield i
        for key, per in self.local.items():
            self.new[("loop", name, key)] = (base.get(key, 0), per, count)
            self.n[key] = base.get(key, 0) + per * count
        self.loop_name, self.i, self.local = None, None, {}
        self.last = (self.key, None, self.n.get(self.key, 0)) if self.n.get(self.key) else None


class Ring:

    def __init__(self, lane):
        self.lane, self.n, self.l, self.parts = lane, 0, 0, []

    def next(self):
        if self.lane.loop_name is None:
            n = self.n
            self.n += 1
            return n % RING, ("use", n), self._flat(n - RING), 0
        loop, l = self.lane.loop_name, self.l
        self.l += 1
        per = self.lane.old.get(("ring", loop), RING)
        back, lag = (l - RING, 0) if l >= RING else (l - RING + per, 1)
        return (self.n + l) % RING, ("use", loop, l), ("use", loop, back), lag

    def _flat(self, n):
        for start, per, count, loop in self.parts:
            if start <= n < start + per * count:
                return ("use", loop, (n - start) % per)
        return ("use", n) if n >= 0 else None

    def enter(self):
        self.l = 0

    def leave(self, loop, count):
        self.lane.new[("ring", loop)] = self.l
        assert self.l % RING == 0
        self.parts.append((self.n, self.l, count, loop))
        self.n += self.l * count


def program(nc, a, out, upto, old, new):
    ctx = ExitStack()
    with ctx:
        def sb(name, shape, dt=F32):
            return ctx.enter_context(nc.sbuf_tensor(name, shape, dt))

        semaphores = {}

        def sems(key):
            if key not in semaphores:
                semaphores[key] = ctx.enter_context(nc.semaphore(key))
            return semaphores[key]

        xT = sb("xT", [P, KD, S])
        cT = sb("cT", [P, KD, L])
        hT = sb("hT", [P, KD, S + L])
        ring = sb("ring", [P, RING, KD, P])
        vec = sb("vec", [P, VT * P])
        const = sb("const", [P, CONST1_W])
        ones = sb("ones", [P, P])
        cols = sb("cols", [P, 640])
        square = sb("square", [P, 2, S + L])
        rstd = sb("rstd", [P, S + L])
        AW = 28672
        arena = sb("arena", [P, AW])
        MODW = AW - 6144
        mod_w = arena[:, MODW:MODW + 4096].rearrange("p (b k n) -> p b k n", b=2, k=4)
        mod_acc = arena[:, MODW + 4096:AW].rearrange("p (b n) -> p b n", b=4)
        psum = ctx.enter_context(nc.psum_tensor("psum", [P, BANKS, S], F32))
        comb_dram = nc.dram_tensor("comb_dram", [2, 32, S], F32).ap()
        acs_dram = nc.dram_tensor("acs_dram", [32, S], F32).ap()

        tensor_done, scalar_done, vector_done, gpsimd_done = (
            sems("tensor_done"), sems("scalar_done"), sems("vector_done"), sems("gpsimd_done"))
        vraw_landed, const_landed, xraw_landed, craw_landed = sems("vraw"), sems("const"), sems("xraw"), sems("craw")
        pool_w_landed, dtb_landed, A_log_landed = sems("pool_w"), sems("dtb"), sems("A_log")
        rw_landed, rb_landed, small_landed = sems("rw"), sems("rb"), sems("small")
        rope_landed, tabs_landed = sems("rope"), sems("tabs")
        comb_out_landed, acs_out_landed, result_landed = sems("comb_out"), sems("acs_out"), sems("result")
        weights_landed = [sems(f"weights_{i}") for i in range(RING)]
        comb_row_landed = [sems(f"comb_row_{i}") for i in range(4)]
        acs_row_landed = [sems(f"acs_row_{i}") for i in range(2)]
        bias_landed = [sems(f"bias_{i}") for i in range(2)]
        mod_w_landed = [sems(f"mod_w_{i}") for i in range(2)]

        def V(name, j=0, n=1):
            r = VEC[name] + j
            return vec[:, r:r + n]

        def C(name, lo=0, n=None):
            o, w = CONST[name]
            return const[:, o + lo:o + (w if n is None else lo + n)]

        col_at = {}

        def col(name, j=0, n=1, rows=P):
            o, w = col_at[name]
            assert j + n <= w
            return cols[0:rows, o + j:o + j + n]

        _o = 0
        for _n, _w in (("zero", 1), ("one", 1), ("eps", 1), ("csilu", 24), ("mod", 96), ("mod2", 96), ("A", 8), ("A2", 8),
                       ("Dh", 16), ("nwh", 16), ("dtb", 1), ("negA", 1), ("lgf", 4), ("lgb", 4), ("lgfb", 4),
                       ("lgbb", 4), ("hb", 4), ("gate", 8), ("gate2", 8), ("epsg", 1), ("lng", 16), ("lnt", 16), ("stat", 64),
                       ("ctmp", 24), ("small", 32), ("lg", 16), ("lgt", 16), ("lgm", 16), ("lgp", 16), ("hlb", 8), ("hg", 16)):
            col_at[_n] = (_o, _w)
            _o += _w
        assert _o <= 640

        class Arena:
            def __init__(self, at=0, end=AW):
                self.at, self.end = at, end

            def take(self, *shape):
                n = 1
                for s in shape:
                    n *= s
                v = arena[:, self.at:self.at + n]
                self.at += n
                assert self.at <= self.end, (self.at, self.end)
                if len(shape) == 2:
                    v = v.rearrange("p (a b) -> p a b", b=shape[1])
                if len(shape) == 3:
                    v = v.rearrange("p (a b c) -> p a b c", b=shape[1], c=shape[2])
                return v

        def bank(name):
            return psum[:, old.get(("bank", name), 0), :]

        def block8(w, c0, width=P):
            return w[:, c0:c0 + width].rearrange("(k p) n -> p k n", p=P)

        IN_A = [12, 13, 14, 15, 0, 1, 2, 3, 4, 8, 5, 9, 6, 10, 7, 11]
        res = hT[:, :, :].rearrange("p a b -> p (a b)")

        def hT_res(t):
            return res[:, D * t:D * (t + 1)]

        def stage_on(n):
            return upto >= n

        m0 = Arena()
        vraw = m0.take(VT, P)
        xraw = m0.take(4, D)
        craw = m0.take(2, D)

        mA = Arena(end=MODW)
        aT = mA.take(8, S)
        qk = mA.take(8, S)
        vTok = mA.take(4, S)
        bias_s = mA.take(2, S)
        prob = [[mA.take(P * (t + 1)) for t in range(4)] for _ in range(2)]
        probT = mA.take(4, S)
        pool_w = mA.take(4, P)
        up = mA.take(4, S + 16)
        win_at = mA.at - 4 * (S + 16) - 4 * P - 4 * S
        win = [arena[:, win_at + (S + 16) * i:win_at + (S + 16) * (i + 1)] for i in range(2)]

        mE = Arena(end=MODW)
        hid = mE.take(8, S)
        wcomb = mE.take(4, S)
        e_t = mE.take(2, S)
        e_u = mE.take(2, S)
        rw = mE.take(8, 36)
        rb = mE.take(36)
        rt = mE.take(4, 36)
        r1 = mE.take(4, 36)
        r2 = mE.take(4, 36)
        r3 = mE.take(4, 36)
        r4 = mE.take(4, 36)
        rs_ = mE.take(12, 4)
        combT = mE.take(S)

        mM = Arena(end=MODW)
        yT = mM.take(16, S)
        g_z = mM.take(2, S)
        g_x = mM.take(2, S)
        g_bc = mM.take(2, S)
        g_pad = mM.take(S + 3)
        g_t = mM.take(S)
        g_cb = mM.take(1280)
        g_seg = mM.take(2, 1280)
        g_xdt = mM.take(4, 256)
        acs_b = mM.take(2, S)
        dtT = mM.take(3, S)
        dtTok = mM.take(4, 64)
        SOFF = [0, 512, 896, 1152]

        mB = Arena()
        br = mB.take(16, CW)
        R0 = mB.at
        zt_at = AW - 2 * (S + L)
        zt = arena[:, zt_at:AW].rearrange("p (b n) -> p b n", b=2)
        mQ = Arena(at=R0)
        q_ = mQ.take(4, S + L)
        kd = mQ.take(2, S + L)
        k_raw = mQ.take(S + L)
        v_tok = mQ.take(6, P)
        cu = mQ.take(2, 813)
        pT2 = mQ.take(5, S)
        v_raw = arena[:, mQ.at - 5 * S:mQ.at - 5 * S + S + L]
        pr2 = [mQ.take(4, 640), None]
        rope_at = mQ.at
        pr2[1] = mQ.take(4, 640)
        rope = arena[:, rope_at:rope_at + P + 2 * S]
        rot_, cos_, sin_ = rope[:, 0:P], rope[:, P:P + S], rope[:, P + S:P + 2 * S]
        mR = Arena(at=R0, end=zt_at)
        tabs = mR.take(2 * 896 + 2 * S)
        dplus, dminus = tabs[:, 0:896], tabs[:, 896:1792]
        to_end, to_start = tabs[:, 1792:1792 + S], tabs[:, 1792 + S:1792 + 2 * S]
        rq, rk, rv = mR.take(S + L), mR.take(S + L), mR.take(S + L)
        rv_tok = mR.take(6, P)
        rsc = mR.take(6, S)
        rsc_c = mR.take(2, L)
        dstrip = mR.take(896)
        rctx = mR.take(2, S)
        rtmp = mR.take(2, S)
        ro = mR.take(S + L)
        rnd = mR.take(S + L)
        rdt = arena[:, mR.at - 2 * (S + L):mR.at - 2 * (S + L) + 896]
        mS = Arena(at=R0, end=zt_at)
        sc_c = mS.take(2, S + L)
        sc_u = mS.take(2, 785)
        cf_t = mS.take(2, CW)
        mrg = mS.take(8, S + L)
        mt = mS.take(4, S + L)
        COL = dict(ret_q=0, ret_k=512, ret_v=1024, ret_z=1536, sc_b=2048, sc_c=2560, sc_x=3072, sc_z=3584, cf_a=4096,
                   cf_g=4608, cf_z=5120, att_q=5632, att_k=6144, att_v=6272, att_z=6400, gates=6912)

        def in_blocks(l):
            order = [(n, c) for c in range(4) for n in ("cf_g", "cf_a")]
            order += [("att_k", 0), ("att_v", 0)] + [("att_q", c) for c in range(4)] + [("att_z", c) for c in range(4)]
            order += [(n, 0) for n in ("ret_q", "ret_k", "ret_v")]
            for h in range(4):
                order.append(("ret_z", h))
                if h < 3:
                    order += [(n, h + 1) for n in ("ret_q", "ret_k", "ret_v")]
            order += [(n, c) for c in range(4) for n in ("sc_c", "sc_x", "sc_b", "sc_z")]
            order += [("cf_z", c) for c in range(4)]
            return order

        def key_tiles(n):
            return [t for t in (n - 1, n, n + 1) if 0 <= t < 4] if n < 4 else []

        def x_tiles(l):
            return range(6 if l == 0 else 4)

        def tile_at(n):
            return P * n if n < 4 else CO + P * (n - 4)

        def parts(c, co=S):
            return [("x", 0, S)] + ([("c", co, L)] if c else [])

        def jobname(*x):
            return ("job",) + x

        MODS = [("ada_w", l, b) for l in range(2) for b in range(12)] + \
               [("w_mod_2", l, b) for l in range(2) for b in range(6)]
        if not stage_on(3):
            MODS = MODS[:12]
        elif not stage_on(6):
            MODS = MODS[:24]
        mods_at = {("a", 2 * h): [12 + h] for h in range(4)} if stage_on(3) else {}
        mods_at.update({("g", g): v for g, v in enumerate(([20, 21], [22, 23], [24], [25, 26], [27, 28], [29, 30],
                                                           [31, 32], [33]))})
        mods_at.update({("o", 3): [34], ("o", 7): [35]})
        mods_at = {k: [i for i in v if i < (36 if stage_on(6) else 24)] for k, v in mods_at.items()}

        DVE_MODS = 4
        mod_t = arena[:, MODW - 4 * S:MODW].rearrange("p (k n) -> p k n", k=4)

        def mod_slots(i):
            if i < 24:
                return [i % 4]
            return [(24 + 2 * (i - 24)) % 4, (24 + 2 * (i - 24) + 1) % 4]

        sidx = {}
        n_ = 0
        for i in range(len(MODS)):
            sidx[i] = list(range(n_, n_ + len(mod_slots(i))))
            n_ += len(mod_slots(i))
        owner = {q: i for i, v in sidx.items() for q in v}

        a2 = {k: v for k, v in a.items()}

        block = ctx.enter_context(nc.Block())

        @block.tensor
        def _(eng):
            pe = Count(eng, "tensor_done", sems, old, new)
            slots = Ring(pe)
            held = {}
            st = {"j": 0, "l": 0, "names": []}

            def job(*name):
                name = jobname(*name)
                if pe.loop_name is None:
                    b = st["j"] % BANKS
                    st["j"] += 1
                    if b in held:
                        eng.wait_ge(pe.doer(("free",) + held[b]), pe.at(("free",) + held[b]))
                else:
                    l = st["l"]
                    b = (st["j"] + l) % BANKS
                    st["l"] += 1
                    if b in st["in"]:
                        eng.wait_ge(vector_done, pe.at(("free",) + st["in"][b]))
                    else:
                        last = old.get(("lastjobs", pe.loop_name), {})
                        if b in last:
                            eng.wait_ge(vector_done, pe.at(("free",) + last[b], lag=1))
                    st["in"][b] = name
                held[b] = name
                new[("bank", name)] = b
                return psum[:, b, :], ("full",) + name

            def take():
                slot, use, _, _ = slots.next()
                eng.wait_ge(weights_landed[slot], pe.at(("landed",) + use))
                return ring[:, slot], ("freed",) + use

            def linear(name, rhs, nk=KD, x=True, c=False, w=None, co=S):
                parts = ([("x", 0, S)] if x else []) + ([("c", co, L)] if c else [])
                ws = [take() for _ in range((nk + 7) // 8)] if w is None else w
                for pi, (tag, o, n) in enumerate(parts):
                    b, full = job(*name, tag)
                    for k in range(nk):
                        mm = nc.tensor.matmul(b[:, 0:n], ws[k // 8][0][:, k % 8, :], rhs(k)[:, o:o + n],
                                              start=(k == 0), stop=(k == nk - 1))
                    names = [full]
                    if pi == len(parts) - 1:
                        names += [w_[1] for w_ in ws]
                    mm.then_inc(tensor_done, pe.step(names))

            def mod(i):
                b, full = job("mod", i)
                eng.wait_ge(pe.doer(("mod_acc", i)), pe.at(("mod_acc", i)))
                for v, s in enumerate(mod_slots(i)):
                    for j in range(4):
                        mm = nc.tensor.matmul(b[:, 4 * v + j:4 * v + j + 1], mod_acc[:, s, j * P:(j + 1) * P],
                                              ones[:, 0:1], start=True, stop=True)
                mm.then_inc(tensor_done, pe.step(full))

            def norm_sum(name, src_n=KD, c=False, x=True):
                bx = job("ss", name, "x") if x else None
                bc = job("ss", name, "c") if c else None
                for k in range(src_n):
                    eng.wait_ge(scalar_done, pe.at(("sq", name, k)))
                    if x:
                        mm = nc.tensor.matmul(bx[0][:, :], ones[:, :], square[:, k % 2, 0:S],
                                              start=(k == 0), stop=(k == src_n - 1))
                        if k == src_n - 1 and c:
                            mm.then_inc(tensor_done, pe.step(bx[1]))
                    if c:
                        mm = nc.tensor.matmul(bc[0][:, 0:L], ones[:, :], square[:, k % 2, S:S + L],
                                              start=(k == 0), stop=(k == src_n - 1))
                    last = [("sq_used", name, k)]
                    if k == src_n - 1:
                        last.append(bc[1] if c else bx[1])
                    mm.then_inc(tensor_done, pe.step(last))

            eng.wait_ge(vraw_landed, pe.at("vraw"))
            eng.wait_ge(const_landed, pe.at("const"))
            for t in range(VT):
                b, full = job("vec", t)
                nc.tensor.transpose(b[:, 0:P], vraw[:, t, :], C("ident")).then_inc(tensor_done, pe.step(full))
            eng.wait_ge(xraw_landed, pe.at("xraw"))
            for k in range(KD):
                b, full = job("xT", k)
                for t in range(4):
                    mm = nc.tensor.transpose(b[:, t * P:(t + 1) * P], xraw[:, t, k * P:(k + 1) * P], C("ident"))
                mm.then_inc(tensor_done, pe.step(full))
            eng.wait_ge(craw_landed, pe.at("craw"))
            for k in range(KD):
                b, full = job("cT", k)
                for t in range(2):
                    mm = nc.tensor.transpose(b[:, t * P:(t + 1) * P], craw[:, t, k * P:(k + 1) * P], C("ident"))
                mm.then_inc(tensor_done, pe.step(full))
            eng.wait_ge(vector_done, pe.at("ones"))

            def moe(l):
                for k in range(KD):
                    eng.wait_ge(vector_done, pe.at(("h", f"n2_{l}", k)))
                eng.wait_ge(rw_landed, pe.at(("rw", l)))
                b, full = job("route", l)
                for t in range(4):
                    for k in range(KD):
                        mm = nc.tensor.matmul(b[:, 36 * t:36 * t + 36], hT[:, k, t * P:(t + 1) * P], rw[:, k, :],
                                              start=(k == 0), stop=(k == KD - 1))
                mm.then_inc(tensor_done, pe.step(full))
                b, full = job("combT", l)
                eng.wait_ge(vector_done, pe.at(("comb", l)))
                for t in range(4):
                    mm = nc.tensor.transpose(b[0:32, t * P:(t + 1) * P], r4[:, t, 0:32], C("ident"))
                mm.then_inc(tensor_done, pe.step(full))
                loop = f"moe{l}"
                for hb in list(held):
                    eng.wait_ge(pe.doer(("free",) + held[hb]), pe.at(("free",) + held[hb]))
                with pe.loop(loop, 4):
                    st["l"], st["in"] = 0, {}
                    slots.enter()
                    for e in range(8):
                        linear((loop, "a", e), lambda k: hT[:, k, :])
                        linear((loop, "b", e), lambda k: hT[:, k, :])
                    for j in range(8):
                        w = take()
                        b, full = job(loop, "y", j)
                        for e in range(8):
                            eng.wait_ge(vector_done, pe.at((loop, "hid", e)))
                            mm = nc.tensor.matmul(b, w[0][:, e, :], hid[:, e, :], start=(e == 0), stop=(e == 7))
                        mm.then_inc(tensor_done, pe.step([full, w[1]] + ([(loop, "hid_used")] if j == 7 else [])))
                assert st["l"] % BANKS == 0
                slots.leave(loop, 4)
                new[("lastjobs", loop)] = dict(st["in"])

            norm_sum("n1_0")
            for i in range(4):
                mod(i)
            for k in range(KD):
                eng.wait_ge(vector_done, pe.at(("h", "n1_0", k)))
            for c in range(16):
                linear(("inA", c), lambda k: hT[:, k, :])
                if c in (4, 6, 8, 10, 12, 14):
                    mod(4 + (c - 4) // 2)
            for c in range(4):
                eng.wait_ge(scalar_done, pe.at(("vA", c)))
                b, full = job("vtA", c)
                for t in range(4):
                    mm = nc.tensor.transpose(b[:, t * P:(t + 1) * P], aT[:, 4 + c, t * P:(t + 1) * P], C("ident"))
                mm.then_inc(tensor_done, pe.step(full))

            def scoresA(h):
                po, c = 64 * (h % 2), h // 2
                eng.wait_ge(scalar_done, pe.at(("qkA", c)))
                eng.wait_ge(scalar_done, pe.at(("qkA", 4 + c)))
                for t in range(4):
                    b, full = job("scA", h, t)
                    n = P * (t + 1)
                    nc.tensor.matmul(b[:, 0:n], qk[po:po + 64, c, t * P:(t + 1) * P],
                                            qk[po:po + 64, 4 + c, 0:n], start=True, stop=True).then_inc(tensor_done, pe.step(full))

            for g in range(4):
                eng.wait_ge(vector_done, pe.at(("pooled", g)))
                eng.wait_ge(pool_w_landed, pe.at("pool_w"))
                b, full = job("poolA", g)
                nc.tensor.matmul(b, pool_w[:, g, :], up[:, g, 0:S], start=True, stop=True).then_inc(tensor_done, pe.step(full))
            scoresA(0)
            for h in range(8):
                if h + 1 < 8:
                    scoresA(h + 1)
                for t in range(4):
                    eng.wait_ge(vector_done, pe.at(("probA", h, t)))
                    b, full = job("ptA", h, t)
                    for q in range(t + 1):
                        mm = nc.tensor.transpose(b[:, q * P:(q + 1) * P], prob[h % 2][t][:, q * P:(q + 1) * P],
                                                 C("ident"))
                    mm.then_inc(tensor_done, pe.step(full))
                for t in range(4):
                    eng.wait_ge(scalar_done, pe.at(("vtokA", t)))
                    eng.wait_ge(scalar_done, pe.at(("ptcA", h, t)))
                b, full = job("oA", h)
                po = 64 * (h % 2)
                for t in range(4):
                    mm = nc.tensor.matmul(b[po:po + 64, t * P:S], vTok[:, t, 64 * h:64 * h + 64],
                                          probT[:, t, t * P:S], start=(t == 0), stop=(t == 3),
                                          skip_group_check=True)
                mm.then_inc(tensor_done, pe.step(full))
                for i in ([10, 11] if h == 0 else []) + mods_at.get(("a", h), []):
                    mod(i)
            for k in range(4):
                eng.wait_ge(vector_done, pe.at(("aoutA", k)))
            for h in range(8):
                eng.wait_ge(scalar_done, pe.at(("oA_c", h)))
            for c in range(8):
                linear(("outA", c), lambda k: aT[:, k, :])
            if stage_on(2):
                norm_sum("n2_0")
                moe(0)
            if stage_on(3):
                for i in range(16, 20):
                    mod(i)
                norm_sum("n1_1")
                for k in range(KD):
                    eng.wait_ge(vector_done, pe.at(("h", "n1_1", k)))
                w = take()
                b, full = job("dt")
                for k in range(KD):
                    mm = nc.tensor.matmul(b[0:32, :], w[0][:, k, 0:32], hT[:, k, 0:S], start=(k == 0), stop=(k == 7))
                mm.then_inc(tensor_done, pe.step([full, w[1]]))
                eng.wait_ge(vector_done, pe.at("acs"))
                b, full = job("dtTok")
                for q in range(2):
                    for t in range(4):
                        mm = nc.tensor.transpose(b[:, 64 * t + 32 * q:64 * t + 32 * q + 32],
                                                 dtT[0:32, q, t * P:(t + 1) * P], C("ident")[0:32, 0:32])
                mm.then_inc(tensor_done, pe.step(full))

                for g in range(8):
                    for n in ("x0", "x1", "B", "C", "z0", "z1"):
                        linear(("ssm", g, n), lambda k: hT[:, k, :])
                    for cc in range(2):
                        eng.wait_ge(vector_done, pe.at(("ssm_x", g, cc)))
                        b, full = job("xtok", g, cc)
                        for t in range(4):
                            mm = nc.tensor.transpose(b[:, t * P:(t + 1) * P], g_x[:, cc, t * P:(t + 1) * P], C("ident"))
                        mm.then_inc(tensor_done, pe.step(full))
                    eng.wait_ge(vector_done, pe.at(("ssm_bc", g, 0)))
                    eng.wait_ge(vector_done, pe.at(("ssm_bc", g, 1)))
                    for t in range(4):
                        b, full = job("cb", g, t)
                        nc.tensor.matmul(b[:, 0:S - t * P], g_bc[:, 0, t * P:(t + 1) * P], g_bc[:, 1, t * P:S],
                                                start=True, stop=True).then_inc(tensor_done, pe.step(full))
                    for i in mods_at[("g", g)]:
                        mod(i)
                    for cc in range(2):
                        b, full = job("y", g, cc)
                        for r in range(2):
                            h = 4 * g + 2 * cc + r
                            eng.wait_ge(vector_done, pe.at(("xdt", g, cc)))
                            eng.wait_ge(vector_done, pe.at(("seg", h)))
                            for t in range(4):
                                mm = nc.tensor.matmul(b[64 * r:64 * r + 64, t * P:S],
                                                      g_xdt[:, t, 64 * (2 * cc + r):64 * (2 * cc + r) + 64],
                                                      g_seg[:, h % 2, SOFF[t]:SOFF[t] + S - t * P],
                                                      start=(t == 0), stop=(t == 3), skip_group_check=True)
                            mm.then_inc(tensor_done, pe.step([("seg_used", h)] + ([full] if r == 1 else [])))
                    norm_sum(("g", g), src_n=2)
                for c in range(8):
                    for k in range(16):
                        eng.wait_ge(vector_done, pe.at(("yn", k)))
                    linear(("outM", c), lambda k: yT[:, k, :], nk=16)
                    for i in mods_at.get(("o", c), []):
                        mod(i)
            if stage_on(4):
                norm_sum("n2_1")
                moe(1)
            if stage_on(5):
                norm_sum("fin1")
            if stage_on(6):
                eng.wait_ge(small_landed, pe.at("small"))
                for l in range(2 if upto > 6 else 1):
                    cx = l == 0
                    h_ = lambda k: hT[:, k, :]
                    norm_sum(("b2", l), c=True)
                    for k in range(KD):
                        eng.wait_ge(vector_done, pe.at(("hc", ("b2", l), k)))
                        eng.wait_ge(vector_done, pe.at(("h", ("b2", l), k)))
                    for c in range(4):
                        linear(("cf_g", l, c), h_, c=cx)
                        linear(("cf_a", l, c), h_, c=cx)
                    linear(("att_k", l), h_, c=True)
                    linear(("att_v", l), h_, c=True)
                    eng.wait_ge(rope_landed, pe.at(("rope", l)))
                    eng.wait_ge(scalar_done, pe.at(("k_raw", l)))
                    b, full = job("rot_k", l)
                    nc.tensor.matmul(b, rot_, k_raw[:, 0:S], start=True, stop=True).then_inc(tensor_done, pe.step(full))
                    eng.wait_ge(scalar_done, pe.at(("v_raw", l)))
                    for tag, t0, t1 in (("x", 0, 4), ("c", 4, 6)):
                        b, full = job("v_tok", l, tag)
                        for t in range(t0, t1):
                            mm = nc.tensor.transpose(b[:, (t - t0) * P:(t - t0 + 1) * P], v_raw[:, t * P:(t + 1) * P],
                                                     C("ident"))
                        mm.then_inc(tensor_done, pe.step(full))
                    for c in range(4):
                        linear(("att_q", l, c), h_, c=cx)
                    for c in range(4):
                        eng.wait_ge(scalar_done, pe.at(("q_raw", l, c)))
                        b, full = job("rot_q", l, c)
                        nc.tensor.matmul(b, rot_, q_[:, c, 0:S], start=True, stop=True).then_inc(tensor_done, pe.step(full))
                    eng.wait_ge(scalar_done, pe.at(("kd", l)))
                    eng.wait_ge(vector_done, pe.at(("roped", l)))

                    rounds = [(n, j) for n in x_tiles(l) for j in range(2)]

                    def att_scores(n, j):
                        for hh in range(4):
                            h = 4 * j + hh
                            po, c = 64 * (h % 2), h // 2
                            ql = q_[po:po + 64, c, n * P:(n + 1) * P]
                            kt = key_tiles(n)
                            if kt:
                                b, full = job("sl", l, h, n)
                                nc.tensor.matmul(b[:, 0:P * len(kt)], ql,
                                                        kd[po:po + 64, j, P * kt[0]:P * (kt[-1] + 1)],
                                                        start=True, stop=True).then_inc(tensor_done, pe.step(full))
                            b, full = job("sx", l, h, n)
                            nc.tensor.matmul(b[:, 0:L], ql, kd[po:po + 64, j, S:S + L], start=True, stop=True).then_inc(tensor_done, pe.step(full))

                    att_scores(*rounds[0])
                    for r, (n, j) in enumerate(rounds):
                        if r + 1 < len(rounds):
                            att_scores(*rounds[r + 1])
                        kt = key_tiles(n)
                        nl = len(kt)
                        for hh in range(4):
                            h = 4 * j + hh
                            eng.wait_ge(vector_done, pe.at(("pr2", l, n, h)))
                            pr = pr2[r % 2][:, hh, :]
                            for tag, t0, t1 in (("l", 0, nl), ("x", nl, nl + 2)):
                                if t1 == t0:
                                    continue
                                b, full = job("pt2", l, h, n, tag)
                                for t in range(t0, t1):
                                    mm = nc.tensor.transpose(b[:, (t - t0) * P:(t - t0 + 1) * P], pr[:, t * P:(t + 1) * P],
                                                             C("ident"))
                                mm.then_inc(tensor_done, pe.step(full))
                        for hh in range(4):
                            eng.wait_ge(scalar_done, pe.at(("ptc2", l, n, 4 * j + hh)))
                        b, full = job("av", l, n, j)
                        tiles = [(i, t) for i, t in enumerate(kt)] + [(3, 4), (4, 5)]
                        for i, (kb, t) in enumerate(tiles):
                            mm = nc.tensor.matmul(b[0:64, :], v_tok[:, t, 64 * j:64 * j + 64], pT2[:, kb, :],
                                                  start=(i == 0), stop=(i == len(tiles) - 1))
                        mm.then_inc(tensor_done, pe.step(full))
                    for c in range(4):
                        linear(("att_z", l, c), h_, c=cx)

                    def ret_proj(h):
                        linear(("ret_q", l, h), h_, c=cx)
                        linear(("ret_k", l, h), h_, c=True)
                        linear(("ret_v", l, h), h_, c=True)

                    def ret_tok(h):
                        eng.wait_ge(scalar_done, pe.at(("rv", l, h)))
                        for tag, t0, t1 in (("x", 0, 4), ("c", 4, 6)):
                            b, full = job("rv_tok", l, h, tag)
                            for t in range(t0, t1):
                                mm = nc.tensor.transpose(b[:, (t - t0) * P:(t - t0 + 1) * P], rv[:, t * P:(t + 1) * P],
                                                         C("ident"))
                            mm.then_inc(tensor_done, pe.step(full))

                    ret_proj(0)
                    ret_tok(0)
                    for h in range(4):
                        eng.wait_ge(scalar_done, pe.at(("rq", l, h)))
                        eng.wait_ge(scalar_done, pe.at(("rk", l, h)))
                        for t in range(6):
                            b, full = job("rs", l, h, t)
                            nc.tensor.matmul(b, rk[:, t * P:(t + 1) * P], rq[:, 0:S], start=True, stop=True).then_inc(tensor_done, pe.step(full))
                        if cx:
                            for t in range(2):
                                b, full = job("rs_c", l, h, t)
                                nc.tensor.matmul(b[:, 0:L], rk[:, (4 + t) * P:(5 + t) * P], rq[:, S:S + L],
                                                        start=True, stop=True).then_inc(tensor_done, pe.step(full))
                        linear(("ret_z", l, h), h_, c=cx)
                        eng.wait_ge(scalar_done, pe.at(("rv_tok", l, h)))
                        b, full = job("ro", l, h, "x")
                        for t in range(6):
                            eng.wait_ge(vector_done, pe.at(("rsc", l, h, t)))
                            mm = nc.tensor.matmul(b, rv_tok[:, t, :], rsc[:, t, :], start=(t == 0), stop=(t == 5))
                        mm.then_inc(tensor_done, pe.step(full))
                        if cx:
                            b, full = job("ro", l, h, "c")
                            eng.wait_ge(vector_done, pe.at(("rsc_c", l, h)))
                            for t in range(2):
                                mm = nc.tensor.matmul(b[:, 0:L], rv_tok[:, 4 + t, :], rsc_c[:, t, :], start=(t == 0),
                                                      stop=(t == 1))
                            mm.then_inc(tensor_done, pe.step(full))
                        if h < 3:
                            ret_proj(h + 1)
                        for tag, o, n in parts(cx):
                            b, full = job("rm", l, h, tag)
                            eng.wait_ge(scalar_done, pe.at(("ro_c", l, h, tag)))
                            nc.tensor.matmul(b[:, 0:n], ones[:, :], ro[:, o:o + n], start=True, stop=True).then_inc(tensor_done, pe.step(full))
                        if h < 3:
                            ret_tok(h + 1)
                        norm_sum(("ret", l, h), src_n=1, c=cx)
                    for c in range(4):
                        for n in ("sc_c", "sc_x", "sc_b", "sc_z"):
                            linear((n, l, c), h_, c=cx)
                    for tag, o, n in parts(cx, CO):
                        b, full = job("lm", l, tag)
                        for c in range(4):
                            eng.wait_ge(vector_done, pe.at(("cf_conv", l, c)))
                            mm = nc.tensor.matmul(b[:, 0:n], ones[:, :], br[:, 8 + c, o:o + n], start=(c == 0),
                                                  stop=(c == 3))
                        mm.then_inc(tensor_done, pe.step(full))
                    norm_sum(("ln", l), src_n=4, c=cx)
                    for c in range(4):
                        linear(("cf_z", l, c), h_, c=cx)
                    for i in range(4):
                        for c in range(4):
                            eng.wait_ge(vector_done, pe.at(("branch", l, 4 * i + c)))
                    for c in range(8):
                        for i in range(4):
                            linear(("gate", l, c, i), h_, c=cx)
                            linear(("by", l, c, i), lambda k: br[:, 4 * i + k, :], nk=4, c=cx, co=CO)
                    for c in range(8):
                        eng.wait_ge(vector_done, pe.at(("mrg", l, c)))
                    for c in range(8):
                        linear(("out2", l, c), lambda k: mrg[:, k, :], c=cx)
                if upto > 7:
                    norm_sum("fin2")
            for k in range(KD):
                eng.wait_ge(vector_done, pe.at("x_final"))
            for t in range(4):
                for hh in range(2):
                    b, full = job("res", t, hh)
                    for k in range(4):
                        mm = nc.tensor.transpose(b[:, k * P:(k + 1) * P], xT[:, 4 * hh + k, t * P:(t + 1) * P], C("ident"))
                    mm.then_inc(tensor_done, pe.step(full))

        @block.sync
        def _(eng):
            sp = Count(eng, "sync_none", sems, old, new)
            slots = Ring(sp)
            outstanding = {}

            def put(src, dst=None):
                slot, use, before, lag = slots.next()
                if before is not None:
                    eng.wait_ge(tensor_done, sp.at(("freed",) + before, lag=lag))
                to = ring[:, slot] if dst is None else dst(ring[:, slot])
                eng.dma_start(to, src).then_inc(weights_landed[slot], sp.landing(f"weights_{slot}", ("landed",) + use))

            eng.dma_start(vraw, a["vecs"].rearrange("(t p) n -> p t n", p=P)).then_inc(vraw_landed, sp.landing("vraw", "vraw"))
            eng.dma_start(const[:, :], a["consts"][:, 0:CONST1_W]).then_inc(const_landed, sp.landing("const", "const"))
            eng.dma_start(xraw, a["x"].rearrange("b (t p) n -> p (b t) n", p=P)).then_inc(xraw_landed, sp.landing("xraw", "xraw"))
            eng.dma_start(craw, a["ctx_2"].rearrange("b (t p) n -> p (b t) n", p=P)).then_inc(craw_landed, sp.landing("craw", "craw"))
            w = a["mix_w_in"][0]
            for c in IN_A:
                put(block8(w, P * c))
            for c in range(8):
                put(block8(a["mix_w_out"][0], P * c))

            def moe(l):
                loop = f"moe{l}"
                for b in range(RING):
                    eng.wait_ge(tensor_done, sp.at(("freed",) + (slots._flat(slots.n - 1 - b))))
                eng.wait_ge(comb_out_landed, sp.at(("comb_out", l)))
                with sp.loop(loop, 4) as g:
                    slots.enter()
                    for e in range(8):
                        w1 = a["moe_w1"][l].rearrange("(g e) k f -> g e k f", e=8)[bass.ds(g, 1), e]
                        put(w1.rearrange("o (k p) f -> p (o k) f", p=P))
                        w3 = a["moe_w3"][l].rearrange("(g e) k f -> g e k f", e=8)[bass.ds(g, 1), e]
                        put(w3.rearrange("o (k p) f -> p (o k) f", p=P))
                        cr = comb_dram[l].rearrange("(g e) s -> g e s", e=8)[bass.ds(g, 1), e]
                        if e >= 4:
                            eng.wait_ge(vector_done, sp.at((loop, "hid", e - 4)))
                        else:
                            eng.wait_ge(vector_done, sp.at((loop, "hid", e + 4), lag=1))
                        eng.dma_start(wcomb[:, e % 4, :], cr.broadcast_to([P, S])).then_inc(comb_row_landed[e % 4], sp.landing(f"comb_row_{e % 4}", (loop, "comb_row", e)))
                    for j in range(8):
                        w2 = a["moe_w2"][l].rearrange("(g e) f n -> g e f n", e=8)[bass.ds(g, 1), :, :, j * P:(j + 1) * P]
                        put(w2.rearrange("o e f n -> f (o e) n"))
                slots.leave(loop, 4)

            if stage_on(2):
                moe(0)
            if stage_on(3):
                w = a["ssm_w_in"][0]
                put(block8(w, 6144, 32), dst=lambda s: s[:, :, 0:32])
                for g in range(8):
                    for n, c0 in (("x0", 2048 + 256 * g), ("x1", 2048 + 256 * g + P), ("B", 4096 + P * g),
                                  ("C", 5120 + P * g), ("z0", 256 * g), ("z1", 256 * g + P)):
                        put(block8(w, c0))
                    for r in range(4):
                        h = 4 * g + r
                        if h == 0:
                            eng.wait_ge(acs_out_landed, sp.at("acs_out"))
                        if h >= 2:
                            eng.wait_ge(vector_done, sp.at(("acs_used", h - 2)))
                        eng.dma_start(acs_b[:, h % 2, :], acs_dram[h:h + 1, :].broadcast_to([P, S])).then_inc(acs_row_landed[h % 2], sp.landing(f"acs_row_{h % 2}", ("acs_row", h)))
                for c in range(8):
                    for k2 in range(2):
                        put(a["ssm_w_out"][0][1024 * k2:1024 * (k2 + 1), c * P:(c + 1) * P]
                            .rearrange("(k p) n -> p k n", p=P))
            if stage_on(4):
                moe(1)
            if stage_on(6):
                for l in range(2 if upto > 6 else 1):
                    w = a["w_in_2"][l]
                    for n, c in in_blocks(l):
                        put(block8(w, COL[n] + P * c))
                    for c in range(8):
                        for i in range(4):
                            put(block8(w, COL["gates"] + D * i + P * c))
                            put(a["w_branch_2"][l][i][:, c * P:(c + 1) * P].rearrange("(k p) n -> p k n", p=P),
                                dst=lambda s: s[:, 0:4, :])
                    for c in range(8):
                        put(block8(a["w_out_2"][l], c * P))
            for t in range(4):
                eng.wait_ge(scalar_done, sp.at(("res_c", t)))
                eng.dma_start(out[0, t * P:(t + 1) * P, :], hT_res(t)).then_inc(result_landed, sp.landing("result", ("result", t)))
            eng.wait_ge(result_landed, sp.at(("result", 3)))

        @block.scalar
        def _(eng):
            ac = Count(eng, "scalar_done", sems, old, new)

            def act(out_, in_, f, bias=0.0, scale=1.0, **kw):
                if bias == 0.0 and f != ACT.Copy:
                    bias = col("zero", rows=out_.shape[0]) if out_.start_partition() == 0 else bias0(out_)
                return nc.scalar.activation(out_, in_, f, bias=bias, scale=scale, **kw)

            def bias0(o):
                p = o.start_partition()
                c0 = col_at["zero"][0]
                return cols[p:p + o.shape[0], c0:c0 + 1]

            def copy(out_, in_):
                return nc.scalar.activation(out_, in_, ACT.Copy)

            def evac(job_, out_, n=S, rows=None, name=None):
                j = jobname(*job_)
                eng.wait_ge(tensor_done, ac.at(("full",) + j))
                b = bank(j)
                src = b[:, 0:n] if rows is None else b[rows[0]:rows[1], 0:n]
                copy(out_, src).then_inc(scalar_done, ac.step([("free",) + j] + ([name] if name else [])))

            def tanh_half(job_, out_, n=S, name=None):
                j = jobname(*job_)
                eng.wait_ge(tensor_done, ac.at(("full",) + j))
                act(out_, bank(j)[:, 0:n], ACT.Tanh, scale=0.5).then_inc(scalar_done, ac.step(name))

            def squares(name, src, wait, n=KD, ctxs=None):
                for k in range(n):
                    wait(k)
                    prev = sq_state["hist"]
                    if len(prev) >= 2:
                        eng.wait_ge(tensor_done, ac.at(("sq_used",) + prev[-2]))
                    if n == 1 and prev:
                        eng.wait_ge(tensor_done, ac.at(("sq_used",) + prev[-1]))
                    prev.append((name, k))
                    if ctxs is not None:
                        act(square[:, k % 2, S:S + L], ctxs(k), ACT.Square).then_inc(scalar_done, ac.step())
                    act(square[:, k % 2, 0:S], src(k), ACT.Square).then_inc(scalar_done, ac.step(("sq", name, k)))

            sq_state = {"hist": []}

            def inv_root(name, div, eps, x=True, c=False):
                eng.wait_ge(vector_done, ac.at(("rstd_used", ac_prev["r"]))) if ac_prev["r"] else None
                ac_prev["r"] = name
                parts = ([("x", 0, S)] if x else []) + ([("c", S, L)] if c else [])
                for tag, o, n in parts:
                    j = jobname("ss", name, tag)
                    eng.wait_ge(tensor_done, ac.at(("full",) + j))
                    act(rstd[:, o:o + n], bank(j)[:, 0:n], ACT.Ln, bias=eps, scale=1.0 / div).then_inc(scalar_done, ac.step(("free",) + j))
                eng.wait_ge(scalar_done, ac.own())
                for tag, o, n in parts:
                    act(rstd[:, o:o + n], rstd[:, o:o + n], ACT.Exp, scale=-0.5).then_inc(scalar_done, ac.step(("rstd", name, tag)))

            ac_prev = {"r": None}
            pad_prev = [None]

            eng.dma_start(pool_w, a["pool_w"][0].rearrange("g c d -> c g d")).then_inc(pool_w_landed, ac.landing("pool_w", "pool_w"))
            eng.dma_start(col("dtb", rows=32), a["ssm_dt_bias"].rearrange("o h -> h o")).then_inc(dtb_landed, ac.landing("dtb", "dtb"))
            eng.dma_start(col("negA", rows=32), a["ssm_A_log"].rearrange("o h -> h o")).then_inc(A_log_landed, ac.landing("A_log", "A_log"))

            def bias_load(h):
                if h >= 2:
                    eng.wait_ge(vector_done, ac.at(("biasA_used", h - 2)))
                else:
                    eng.wait_ge(vector_done, ac.at("bias_mask"))
                for lo, n in ((0, S - 64), (64, S)):
                    eng.dma_start(bias_s[lo:lo + 64, h % 2, 0:n], a["rel_tiles"][h, lo:lo + 64, 0:n]).then_inc(bias_landed[h % 2], ac.landing(f"bias_{h % 2}", ("biasA", h)))

            def router_load(l):
                eng.dma_start(rw, a["w_router"][l].rearrange("(k p) n -> p k n", p=P)).then_inc(rw_landed, ac.landing("rw", ("rw", l)))
                eng.dma_start(rb, a["small"][0:1, 36 * l:36 * l + 36].broadcast_to([P, 36])).then_inc(rb_landed, ac.landing("rb", ("rb", l)))

            eng.wait_ge(vector_done, ac.at("cols0"))
            for t in range(VT):
                evac(("vec", t), vec[:, t * P:(t + 1) * P], n=P, name=("vec", t))
            eng.wait_ge(scalar_done, ac.own())
            for v, nm in enumerate(("c", "c_2", "c_ctx_2")):
                act(col("ctmp", 8 * v, 8), V(nm, 0, 8), ACT.Tanh, scale=0.5).then_inc(scalar_done, ac.step(("tanh_c", v)))
            for k in range(KD):
                evac(("xT", k), xT[:, k, :], name=("xT", k))
            for k in range(KD):
                evac(("cT", k), cT[:, k, :], n=L, name=("cT", k))
            eng.wait_ge(scalar_done, ac.own())

            squares("n1_0", lambda k: xT[:, k, :], lambda k: None)
            inv_root("n1_0", D, col("eps"))

            for c in IN_A:
                c4 = c % 4
                if c < 4:
                    eng.wait_ge(vector_done, ac.at("up_zero"))
                    evac(("inA", IN_A.index(c), "x"), up[:, c4, 16:16 + S], name=("uA", c4))
                elif c < 12:
                    evac(("inA", IN_A.index(c), "x"), qk[:, c - 4, :], name=("qkA", c - 4))
                else:
                    evac(("inA", IN_A.index(c), "x"), aT[:, 4 + c4, :], name=("vA", c4))
            for c in range(4):
                j = jobname("vtA", c)
                eng.wait_ge(tensor_done, ac.at(("full",) + j))
                copy(vTok[:, :, c * P:(c + 1) * P], bank(j).rearrange("p (t n) -> p t n", t=4)).then_inc(scalar_done, ac.step([("free",) + j] + [("vtokA", c)]))
            bias_load(0)
            bias_load(1)

            def soft(h):
                for t in range(4):
                    eng.wait_ge(vector_done, ac.at(("smA", h, t)))
                    n = P * (t + 1)
                    pr = prob[h % 2][t][:, 0:n]
                    act(pr, pr, ACT.Exp, bias=col("stat", 8 * (h % 2) + t),
                        accum_out=col("stat", 16 + 8 * (h % 2) + t)).then_inc(scalar_done, ac.step(("expA", h, t)))
                if h + 2 < 8:
                    bias_load(h + 2)
            soft(0)
            for h in range(8):
                if h + 1 < 8:
                    soft(h + 1)
                for t in range(4):
                    j = jobname("ptA", h, t)
                    eng.wait_ge(tensor_done, ac.at(("full",) + j))
                    if h >= 1:
                        eng.wait_ge(tensor_done, ac.at(("full",) + jobname("oA", h - 1)))
                    copy(probT[:, 0:t + 1, t * P:(t + 1) * P],
                         bank(j)[:, 0:P * (t + 1)].rearrange("p (q n) -> p q n", n=P)).then_inc(scalar_done, ac.step([("free",) + j, ("ptcA", h, t)]))
                po = 64 * (h % 2)
                evac(("oA", h), aT[po:po + 64, 4 + h // 2, :], rows=(po, po + 64), name=("oA_c", h))
            if stage_on(2):
                router_load(0)
                squares("n2_0", lambda k: xT[:, k, :], lambda k: eng.wait_ge(vector_done, ac.at(("xA", k))))
                inv_root("n2_0", D, col("eps"))

            def moe(l):
                eng.wait_ge(vector_done, ac.at(("grp", l)))
                act(r1[:, :, 0:4], r1[:, :, 0:4], ACT.Exp).then_inc(scalar_done, ac.step(("eg", l)))
                eng.wait_ge(vector_done, ac.at(("top2", l)))
                act(rs_[:, 4, :], rs_[:, 4, :], ACT.Exp).then_inc(scalar_done, ac.step(("er", l)))
                j = jobname("combT", l)
                eng.wait_ge(tensor_done, ac.at(("full",) + j))
                copy(combT[0:32, :], bank(j)[0:32, :]).then_inc(scalar_done, ac.step([("free",) + j, ("combT_c", l)]))
                eng.wait_ge(scalar_done, ac.own())
                eng.dma_start(comb_dram[l], combT[0:32, :]).then_inc(comb_out_landed, ac.landing("comb_out", ("comb_out", l)))
                loop = f"moe{l}"
                with ac.loop(loop, 4):
                    for e in range(8):
                        if e >= 2:
                            eng.wait_ge(vector_done, ac.at((loop, "s", e - 2)))
                        else:
                            eng.wait_ge(vector_done, ac.at((loop, "s", e + 6), lag=1))
                        tanh_half((loop, "a", e, "x"), e_t[:, e % 2, :], name=(loop, "t", e))

            if stage_on(2):
                moe(0)
            if stage_on(3):
                squares("n1_1", lambda k: xT[:, k, :], lambda k: eng.wait_ge(vector_done, ac.at(("x", "moe0", k))))
                inv_root("n1_1", D, col("eps"))
                eng.wait_ge(A_log_landed, ac.at("A_log"))
                act(col("negA", rows=32), col("negA", rows=32), ACT.Exp).then_inc(scalar_done, ac.step("expA_log"))
                eng.wait_ge(vector_done, ac.at("dt_v"))
                act(dtT[0:32, 1, :], dtT[0:32, 0, :], ACT.Abs).then_inc(scalar_done, ac.step())
                eng.wait_ge(scalar_done, ac.own())
                act(dtT[0:32, 1, :], dtT[0:32, 1, :], ACT.Exp, scale=-1.0).then_inc(scalar_done, ac.step())
                eng.wait_ge(scalar_done, ac.own())
                act(dtT[0:32, 1, :], dtT[0:32, 1, :], ACT.Ln, bias=col("one", rows=32)).then_inc(scalar_done, ac.step("dt_ln"))
                eng.wait_ge(vector_done, ac.at("acs"))
                eng.dma_start(acs_dram, dtT[0:32, 1, :]).then_inc(acs_out_landed, ac.landing("acs_out", "acs_out"))
                for g in range(8):
                    for qi, n in enumerate(("x0", "x1", "B", "C")):
                        eng.wait_ge(vector_done, ac.at(("pad_used",) + (pad_prev[0],))) if pad_prev[0] else None
                        pad_prev[0] = (g, qi)
                        evac(("ssm", g, n, "x"), g_pad[:, 3:3 + S], name=("pad", g, qi))
                        eng.wait_ge(vector_done, ac.at(("conv", g, qi)))
                        dst = [g_x[:, 0, :], g_x[:, 1, :], g_bc[:, 0, :], g_bc[:, 1, :]][qi]
                        act(g_t, dst, ACT.Tanh, scale=0.5).then_inc(scalar_done, ac.step(("conv_t", g, qi)))
                    for zz in range(2):
                        if g >= 1:
                            eng.wait_ge(vector_done, ac.at(("yz", g - 1, zz)))
                        j = jobname("ssm", g, f"z{zz}", "x")
                        eng.wait_ge(tensor_done, ac.at(("full",) + j))
                        act(g_z[:, zz, :], bank(j), ACT.Tanh, scale=0.5).then_inc(scalar_done, ac.step(("zt", g, zz)))
                    for t in range(4):
                        j = jobname("cb", g, t)
                        eng.wait_ge(tensor_done, ac.at(("full",) + j))
                        if g >= 1:
                            eng.wait_ge(vector_done, ac.at(("seg", 4 * g - 1)))
                        act(g_cb[:, SOFF[t]:SOFF[t] + S - t * P], bank(j)[:, 0:S - t * P], ACT.Identity, scale=0.25).then_inc(scalar_done, ac.step([("free",) + j, ("cb_c", g)]))
                    for r in range(4):
                        h = 4 * g + r
                        eng.wait_ge(vector_done, ac.at(("arg", h)))
                        act(g_seg[:, h % 2, :], g_seg[:, h % 2, :], ACT.Exp).then_inc(scalar_done, ac.step(("seg_e", h)))
                    squares(("g", g), lambda k: yT[:, 2 * g + k, :], lambda k: eng.wait_ge(vector_done, ac.at(("yz", g, k))), n=2)
                    inv_root(("g", g), 4 * 256, col("eps"))
            if stage_on(4):
                eng.wait_ge(vector_done, ac.at(("yn", 15)))
                router_load(1)
                squares("n2_1", lambda k: xT[:, k, :], lambda k: eng.wait_ge(vector_done, ac.at(("xM", k))))
                inv_root("n2_1", D, col("eps"))
                moe(1)
            if stage_on(5):
                squares("fin1", lambda k: xT[:, k, :], lambda k: eng.wait_ge(vector_done, ac.at(("x", "moe1", k))))
                inv_root("fin1", D, col("eps"))
            if stage_on(6):
                eng.dma_start(col("small", 0, 32), a["small"][0:1, 72:104].broadcast_to([P, 32])).then_inc(small_landed, ac.landing("small", "small"))
                eng.wait_ge(small_landed, ac.at("small"))
                act(col("lgt", 0, 16), col("small", 0, 16), ACT.Abs).then_inc(scalar_done, ac.step())
                eng.wait_ge(scalar_done, ac.own())
                act(col("lgt", 0, 16), col("lgt", 0, 16), ACT.Exp, scale=-1.0).then_inc(scalar_done, ac.step())
                eng.wait_ge(scalar_done, ac.own())
                act(col("lgt", 0, 16), col("lgt", 0, 16), ACT.Ln, bias=col("one")).then_inc(scalar_done, ac.step("lgt"))
                zn = {"n": 0}

                def z_tanh(name, l, c, cx):
                    n = zn["n"]
                    zn["n"] += 1
                    if n >= 2:
                        eng.wait_ge(vector_done, ac.at(("zt_used", n - 2)))
                    for tag, o, w in parts(cx):
                        j = jobname(name, l, c, tag)
                        eng.wait_ge(tensor_done, ac.at(("full",) + j))
                        act(zt[:, n % 2, o:o + w], bank(j)[:, 0:w], ACT.Tanh, scale=0.5).then_inc(scalar_done, ac.step(("zt", n, tag)))

                for l in range(2 if upto > 6 else 1):
                    cx = l == 0
                    squares(("b2", l), lambda k: xT[:, k, :], lambda k: eng.wait_ge(vector_done, ac.at(("x_in", l))), ctxs=lambda k: cT[:, k, :])
                    inv_root(("b2", l), D, col("eps"), c=True)
                    o0 = CONST["rot"][0]
                    eng.wait_ge(vector_done, ac.at(("x_in", l)))
                    eng.dma_start(rope, a["consts"][:, o0:o0 + P + 2 * S]).then_inc(rope_landed, ac.landing("rope", ("rope", l)))
                    for c in range(4):
                        eng.wait_ge(vector_done, ac.at(("cu_free", l, c)))
                        for tag, o, w in parts(cx, CO):
                            j = jobname("cf_g", l, c, tag)
                            eng.wait_ge(tensor_done, ac.at(("full",) + j))
                            act(cu[:, c % 2, 15 + o:15 + o + w], bank(j)[:, 0:w], ACT.Tanh, scale=0.5).then_inc(scalar_done, ac.step([("free",) + j, ("cf_t", l, c, tag)]))
                    for tag, o, w in parts(True):
                        evac(("att_k", l, tag), k_raw[:, o:o + w], n=w, name=("k_raw", l))
                    for tag, o, w in parts(True):
                        evac(("att_v", l, tag), v_raw[:, o:o + w], n=w, name=("v_raw", l))
                    for tag, t0, t1 in (("x", 0, 4), ("c", 4, 6)):
                        evac(("v_tok", l, tag), v_tok[:, t0:t1, :].rearrange("p a b -> p (a b)"), n=P * (t1 - t0),
                             name=("v_tok", l, tag))
                    for c in range(4):
                        for tag, o, w in parts(cx):
                            evac(("att_q", l, c, tag), q_[:, c, o:o + w], n=w, name=("q_raw", l, c))
                    eng.wait_ge(vector_done, ac.at(("k_roped", l)))
                    for j in range(2):
                        for half in range(2):
                            copy(kd[64 * half:64 * half + 64, j, :], k_raw[64 * j:64 * j + 64, :]).then_inc(scalar_done, ac.step(("kd", l)))

                    def att_exp(r, n, j):
                        q = r % 2
                        for hh in range(4):
                            eng.wait_ge(vector_done, ac.at(("nm2", l, n, j)))
                            w = P * len(key_tiles(n)) + L
                            pr = pr2[q][:, hh, 0:w]
                            act(pr, pr, ACT.Exp, bias=col("stat", 32 * q + 4 + hh),
                                accum_out=col("stat", 32 * q + 8 + hh)).then_inc(scalar_done, ac.step(("exp2", l, n, 4 * j + hh)))
                        act(col("stat", 32 * q + 12, 4), col("stat", 32 * q + 12, 4), ACT.Exp).then_inc(scalar_done, ac.step(("es2", l, n, j)))
                    rounds = [(n, j) for n in x_tiles(l) for j in range(2)]
                    att_exp(0, *rounds[0])
                    for r, (n, j) in enumerate(rounds):
                        if r + 1 < len(rounds):
                            att_exp(r + 1, *rounds[r + 1])
                        nl = len(key_tiles(n))
                        if r >= 1:
                            eng.wait_ge(tensor_done, ac.at(("full",) + jobname("av", l, *rounds[r - 1])))
                        else:
                            eng.wait_ge(scalar_done, ac.at(("v_tok", l, "c")))
                        for hh in range(4):
                            h = 4 * j + hh
                            for tag, kb, m in (("l", 0, nl), ("x", 3, 2)):
                                if m == 0:
                                    continue
                                jn = jobname("pt2", l, h, n, tag)
                                eng.wait_ge(tensor_done, ac.at(("full",) + jn))
                                copy(pT2[:, kb:kb + m, P * hh:P * (hh + 1)],
                                     bank(jn)[:, 0:P * m].rearrange("p (a b) -> p a b", b=P)).then_inc(scalar_done, ac.step([("free",) + jn, ("ptc2", l, n, h)]))
                        jn = jobname("av", l, n, j)
                        eng.wait_ge(tensor_done, ac.at(("full",) + jn))
                        bv = bank(jn)[0:64, :].rearrange("p (a b n) -> p a b n", a=2, b=2)
                        for half in range(2):
                            copy(br[64 * half:64 * half + 64, 12 + 2 * j:14 + 2 * j, tile_at(n):tile_at(n) + P],
                                 bv[:, :, half, :]).then_inc(scalar_done, ac.step([("free",) + jn, ("att_o", l)]))
                    eng.dma_start(tabs, a["consts"][:, CONST["dplus"][0]:CONST_W]).then_inc(tabs_landed, ac.landing("tabs", ("tabs", l)))
                    for c in range(4):
                        z_tanh("att_z", l, c, cx)

                    def ret_in(h):
                        if h == 0:
                            eng.wait_ge(vector_done, ac.at(("att_done", l)))
                        else:
                            eng.wait_ge(tensor_done, ac.at(("full",) + jobname("ro", l, h - 1, "c" if cx else "x")))
                        for n, dst, cc in (("q", rq, cx), ("k", rk, True), ("v", rv, True)):
                            for tag, o, w in parts(cc):
                                evac((f"ret_{n}", l, h, tag), dst[:, o:o + w], n=w, name=(f"r{n}", l, h))

                    def ret_tok_c(h):
                        for tag, t0, t1 in (("x", 0, 4), ("c", 4, 6)):
                            evac(("rv_tok", l, h, tag), rv_tok[:, t0:t1, :].rearrange("p a b -> p (a b)"),
                                 n=P * (t1 - t0), name=("rv_tok", l, h))

                    def ret_decay(h):
                        lf, lb = 8 * l + h, 8 * l + 4 + h
                        if h == 0:
                            eng.wait_ge(tabs_landed, ac.at(("tabs", l)))
                            eng.wait_ge(vector_done, ac.at(("att_done", l)))
                        else:
                            eng.wait_ge(vector_done, ac.at(("rctx_used", l, h - 1)))
                        for b_ in range(2):
                            act(rctx[:, b_, :], to_end, ACT.Exp, scale=col("lg", lf),
                                bias=col("lgm", lf) if b_ else col("zero")).then_inc(scalar_done, ac.step())
                            act(rtmp[:, b_, :], to_start, ACT.Exp, scale=col("lg", lb),
                                bias=col("lgp", lb) if b_ else col("zero")).then_inc(scalar_done, ac.step(("rtmp", l, h)))
                        eng.wait_ge(vector_done, ac.at(("darg", l, h)))
                        act(dstrip, dstrip, ACT.Exp).then_inc(scalar_done, ac.step(("dstrip", l, h)))
                    ret_decay(0)
                    ret_in(0)
                    ret_tok_c(0)
                    for h in range(4):
                        z_tanh("ret_z", l, h, cx)
                        for tag, o, w in parts(cx):
                            if h >= 1:
                                eng.wait_ge(vector_done, ac.at(("rnd", l, h - 1, tag)))
                            evac(("ro", l, h, tag), ro[:, o:o + w], n=w, name=("ro_c", l, h, tag))
                        if h < 3:
                            ret_in(h + 1)
                        squares(("ret", l, h), lambda k: rnd[:, 0:S], lambda k: eng.wait_ge(vector_done, ac.at(("rnd", l, h, "c" if cx else "x"))),
                                n=1, ctxs=(lambda k: rnd[:, S:S + L]) if cx else None)
                        if h < 3:
                            ret_tok_c(h + 1)
                        inv_root(("ret", l, h), P, col("eps"), c=cx)
                        if h < 3:
                            ret_decay(h + 1)
                    for c in range(4):
                        if c == 0:
                            eng.wait_ge(vector_done, ac.at(("ret_done", l)))
                        else:
                            eng.wait_ge(vector_done, ac.at(("sc_c_used", l, c - 1)))
                        for tag, o, w in parts(cx):
                            evac(("sc_c", l, c, tag), sc_c[:, c % 2, o:o + w], n=w, name=("sc_cc", l, c, tag))
                        z_tanh("sc_z", l, c, cx)
                    squares(("ln", l), lambda k: br[:, 8 + k, 0:S], lambda k: eng.wait_ge(vector_done, ac.at(("cf_nd", l, k))), n=4,
                            ctxs=(lambda k: br[:, 8 + k, CO:CO + L]) if cx else None)
                    inv_root(("ln", l), 4 * P, col("eps"), c=cx)
                    for c in range(4):
                        eng.wait_ge(vector_done, ac.at(("cf_v", l, c)))
                        if c >= 2:
                            eng.wait_ge(vector_done, ac.at(("cf_y", l, c - 2)))
                        w = CW if cx else S
                        act(cf_t[:, c % 2, 0:w], br[:, 8 + c, 0:w], ACT.Tanh, scale=-0.5, bias=col("hlb", 4 * l + c)).then_inc(scalar_done, ac.step(("cf_tt", l, c)))
                    for c in range(4):
                        z_tanh("cf_z", l, c, cx)
                    for c in range(8):
                        for i in range(4):
                            m = 4 * c + i
                            if m >= 4:
                                eng.wait_ge(vector_done, ac.at(("mt_used", l, m - 4)))
                            else:
                                eng.wait_ge(vector_done, ac.at(("cf_done", l)))
                            for tag, o, w in parts(cx):
                                j = jobname("gate", l, c, i, tag)
                                eng.wait_ge(tensor_done, ac.at(("full",) + j))
                                act(mt[:, m % 4, o:o + w], bank(j)[:, 0:w], ACT.Tanh, scale=0.5).then_inc(scalar_done, ac.step([("free",) + j, ("mt", l, m, tag)]))
                if upto > 7:
                    squares("fin2", lambda k: xT[:, k, :], lambda k: eng.wait_ge(vector_done, ac.at(("x_in", 2))))
                    inv_root("fin2", D, col("eps"))
            for t in range(4):
                for hh in range(2):
                    evac(("res", t, hh), hT_res(t)[:, hh * S:(hh + 1) * S], name=("res_c", t))

        @block.vector
        def _(eng):
            ve = Count(eng, "vector_done", sems, old, new)
            v = nc.vector

            def ts(out_, in0, s1, s2=None, op0=ALU.mult, op1=None):
                if op1 is None:
                    return v.tensor_scalar(out_, in0, s1, None, op0)
                return v.tensor_scalar(out_, in0, s1, s2, op0, op1)

            def tt(out_, in0, in1, op):
                return v.tensor_tensor(out_, in0, in1, op)

            def stt(out_, in0, s, in1, op0=ALU.mult, op1=ALU.mult):
                return v.scalar_tensor_tensor(out_, in0, s, in1, op0, op1)

            def red(out_, in_, op, negate=False):
                return v.tensor_reduce(out_, in_, AX, op, negate=negate)

            def full(*name):
                j = jobname(*name)
                eng.wait_ge(tensor_done, ve.at(("full",) + j))
                return bank(j), ("free",) + j

            def mod(i):
                b, free = full("mod", i)
                if i < 24:
                    tt(col("mod", 4 * i, 4), b[:, 0:4], V("ada_b", 4 * i, 4), ALU.add).then_inc(vector_done, ve.step([free, ("mod", i)]))
                else:
                    q = i - 24
                    l, bb = q // 6, q % 6
                    tt(col("mod2", 48 * l + 4 * bb, 4), b[:, 0:4], V("b_mod_2", 4 * q, 4), ALU.add).then_inc(vector_done, ve.step())
                    tt(col("mod2", 48 * l + 24 + 4 * bb, 4), b[:, 4:8], V("b_mod_2", 4 * q, 4), ALU.add).then_inc(vector_done, ve.step([free, ("mod", i)]))

            def modulated(name, w, scale, shift, src, ctx_part=None):
                eng.wait_ge(vector_done, ve.own())
                stt(col("A", 0, 8), scale, 1.0, w, ALU.add, ALU.mult).then_inc(vector_done, ve.step())
                if ctx_part:
                    stt(col("A2", 0, 8), ctx_part[0], 1.0, w, ALU.add, ALU.mult).then_inc(vector_done, ve.step())
                eng.wait_ge(vector_done, ve.own())
                eng.wait_ge(scalar_done, ve.at(("rstd", name, "x")))
                for k in range(KD):
                    stt(hT[:, k, 0:S], src(k), col("A", k), rstd[:, 0:S]).then_inc(vector_done, ve.step(("rstd_used", name) if not ctx_part else None))
                if ctx_part:
                    eng.wait_ge(scalar_done, ve.at(("rstd", name, "c")))
                    for k in range(KD):
                        stt(hT[:, k, S:S + L], cT[:, k, :], col("A2", k), rstd[:, S:S + L]).then_inc(vector_done, ve.step(("rstd_used", name)))
                eng.wait_ge(vector_done, ve.own())
                if ctx_part:
                    for k in range(KD):
                        ts(hT[:, k, S:S + L], hT[:, k, S:S + L], ctx_part[1](k), op0=ALU.add).then_inc(vector_done, ve.step(("hc", name, k)))
                for k in range(KD):
                    ts(hT[:, k, 0:S], hT[:, k, 0:S], shift(k), op0=ALU.add).then_inc(vector_done, ve.step(("h", name, k)))

            v.memset(ones[:, :], 1.0).then_inc(vector_done, ve.step("ones"))
            v.memset(bias_s[0:64, :, S - 64:S], -1e30).then_inc(vector_done, ve.step("bias_mask"))
            v.memset(col("zero"), 0.0).then_inc(vector_done, ve.step())
            v.memset(col("one"), 1.0).then_inc(vector_done, ve.step())
            v.memset(col("eps"), EPS).then_inc(vector_done, ve.step("cols0"))
            for i, nm in enumerate(("c", "c_2", "c_ctx_2")):
                eng.wait_ge(scalar_done, ve.at(("tanh_c", i)))
                ts(col("ctmp", 8 * i, 8), col("ctmp", 8 * i, 8), 0.5, 0.5, ALU.mult, ALU.add).then_inc(vector_done, ve.step())
                eng.wait_ge(vector_done, ve.own())
                tt(col("csilu", 8 * i, 8), col("ctmp", 8 * i, 8), V(nm, 0, 8), ALU.mult).then_inc(vector_done, ve.step("csilu"))
            eng.wait_ge(scalar_done, ve.at(("vec", VT - 1)))
            ts(col("Dh", 0, 16), V("ssm_D", 0, 16), 0.5).then_inc(vector_done, ve.step())
            ts(col("nwh", 0, 16), V("ssm_norm_w", 0, 16), 0.5).then_inc(vector_done, ve.step())
            eng.wait_ge(tensor_done, ve.at(("full",) + jobname("cT", KD - 1)))
            v.memset(up[:, :, 0:16], 0.0).then_inc(vector_done, ve.step("up_zero"))
            for i in range(DVE_MODS):
                for half in range(2):
                    eng.wait_ge(mod_w_landed[half], ve.at(("mod_w", 2 * i + half)))
                    for k in range(4):
                        c_ = col("csilu", 4 * half + k)
                        eng.wait_ge(vector_done, ve.own())
                        if k or half:
                            stt(mod_acc[:, i, :], mod_w[:, half, k, :], c_, mod_acc[:, i, :], ALU.mult, ALU.add).then_inc(vector_done, ve.step([("mod_half", 2 * i + half)] + ([("mod_acc", i)] if half else [])))
                        else:
                            ts(mod_acc[:, i, :], mod_w[:, half, k, :], c_).then_inc(vector_done, ve.step(("mod_half", 2 * i)))
            for i in range(DVE_MODS):
                mod(i)
            M = lambda l, part, k, n=1: col("mod", 48 * l + 8 * part + k, n)
            modulated("n1_0", V("norm1_w", 0, 8), M(0, 1, 0, 8), lambda k: M(0, 0, k), lambda k: xT[:, k, :])

            nm = 4
            WIN = (2, 4, 8, 16)
            for g in range(4):
                eng.wait_ge(scalar_done, ve.at(("uA", g)))
                src = up[:, g, :]
                cur, width = src, 1
                eng.wait_ge(vector_done, ve.own())
                bufs = win
                bi = 0
                while width < WIN[g]:
                    dst = bufs[bi]
                    lo = 2 * width - 1
                    tt(dst[:, lo:S + 16], cur[:, lo:S + 16], cur[:, lo - width:S + 16 - width], ALU.add).then_inc(vector_done, ve.step())
                    eng.wait_ge(vector_done, ve.own())
                    cur, width, bi = dst, 2 * width, 1 - bi
                ic = C("inv_count", 16 * g, 16)
                other = bufs[bi]
                tt(other[:, 16:32], cur[:, 16:32], ic, ALU.mult).then_inc(vector_done, ve.step())
                eng.wait_ge(vector_done, ve.own())
                tt(other[:, 0:16], other[:, 16:32], src[:, 16:32], ALU.subtract).then_inc(vector_done, ve.step())
                stt(other[:, 32:16 + S], cur[:, 32:16 + S], 1.0 / WIN[g], src[:, 32:16 + S], ALU.mult, ALU.subtract).then_inc(vector_done, ve.step())
                eng.wait_ge(vector_done, ve.own())
                v.tensor_copy(up[:, g, 0:16], other[:, 0:16]).then_inc(vector_done, ve.step())
                v.tensor_copy(up[:, g, 16:S], other[:, 32:16 + S]).then_inc(vector_done, ve.step(("pooled", g)))
            for i in range(4, 10):
                mod(i)
            def pool_out():
                for g in range(4):
                    b, free = full("poolA", g)
                    ts(aT[:, g, :], b, V("pool_scale", g)).then_inc(vector_done, ve.step([free, ("aoutA", g)]))

            def smA(h):
                eng.wait_ge(bias_landed[h % 2], ve.at(("biasA", h)))
                for t in range(4):
                    b, free = full("scA", h, t)
                    n = P * (t + 1)
                    if h >= 2:
                        eng.wait_ge(tensor_done, ve.at(("full",) + jobname("ptA", h - 2, t)))
                    stt(prob[h % 2][t][:, 0:n], b[:, 0:n], 0.125, bias_s[:, h % 2, 3 * P - t * P:S], ALU.mult, ALU.add).then_inc(vector_done, ve.step([free, ("biasA_used", h)]))
                eng.wait_ge(vector_done, ve.own())
                for t in range(4):
                    red(col("stat", 8 * (h % 2) + t), prob[h % 2][t][:, 0:P * (t + 1)], ALU.max, negate=True).then_inc(vector_done, ve.step(("smA", h, t)))

            def nrA(h):
                for t in range(4):
                    eng.wait_ge(scalar_done, ve.at(("expA", h, t)))
                    v.reciprocal(col("stat", 32 + t), col("stat", 16 + 8 * (h % 2) + t)).then_inc(vector_done, ve.step())
                eng.wait_ge(vector_done, ve.own())
                for t in range(4):
                    pr = prob[h % 2][t][:, 0:P * (t + 1)]
                    ts(pr, pr, col("stat", 32 + t)).then_inc(vector_done, ve.step(("probA", h, t)))
            pool_out()
            smA(0)
            for h in range(8):
                nrA(h)
                if h + 1 < 8:
                    smA(h + 1)
                for i in ([10, 11] if h == 0 else []) + mods_at.get(("a", h), []):
                    mod(i)
            eng.wait_ge(vector_done, ve.own())

            def residual(jobs, gate, name):
                for k in range(8):
                    b, free = full(*jobs(k))
                    stt(xT[:, k, :], b, gate(k), xT[:, k, :], ALU.mult, ALU.add).then_inc(vector_done, ve.step([free, (name, k)]))

            residual(lambda k: ("outA", k, "x"), lambda k: M(0, 2, k), "xA")

            def route(l):
                b, free = full("route", l)
                eng.wait_ge(rb_landed, ve.at(("rb", l)))
                lg = rt[:, :, :]
                tt(lg, b[:, 0:144].rearrange("p (t n) -> p t n", t=4), rb.unsqueeze(1).broadcast_to([P, 4, 36]), ALU.add).then_inc(vector_done, ve.step(free))
                eng.wait_ge(vector_done, ve.own())
                G, E = rt[:, :, 0:4], rt[:, :, 4:36]
                m = rs_[:, 0, :]
                red(m, G, ALU.max).then_inc(vector_done, ve.step())
                eng.wait_ge(vector_done, ve.own())
                bc = lambda s, n: s.unsqueeze(2).broadcast_to([P, 4, n])
                tt(r1[:, :, 0:4], G, bc(m, 4), ALU.subtract).then_inc(vector_done, ve.step())
                eng.wait_ge(vector_done, ve.own())
                ts(r1[:, :, 4:8], r1[:, :, 0:4], 0.0, op0=ALU.is_equal).then_inc(vector_done, ve.step())
                eng.wait_ge(vector_done, ve.own())
                tt(r1[:, :, 4:8], r1[:, :, 4:8], C("rank", 0, 4).unsqueeze(1).broadcast_to([P, 4, 4]), ALU.mult).then_inc(vector_done, ve.step(("grp", l)))
                eng.wait_ge(vector_done, ve.own())
                red(rs_[:, 1, :], r1[:, :, 4:8], ALU.max).then_inc(vector_done, ve.step())
                eng.wait_ge(vector_done, ve.own())
                tt(r1[:, :, 8:12], r1[:, :, 4:8], bc(rs_[:, 1, :], 4), ALU.is_equal).then_inc(vector_done, ve.step())
                eng.wait_ge(vector_done, ve.own())
                goh = r1[:, :, 8:12]
                for t in range(4):
                    tt(r2[:, t, 0:32].rearrange("p (g e) -> p g e", g=4),
                       E[:, t, :].rearrange("p (g e) -> p g e", g=4),
                       goh[:, t, :].unsqueeze(2).broadcast_to([P, 4, 8]), ALU.mult).then_inc(vector_done, ve.step())
                eng.wait_ge(vector_done, ve.own())
                for t in range(4):
                    red(r3[:, t, 0:8], r2[:, t, 0:32].rearrange("p (g e) -> p e g", g=4), ALU.add).then_inc(vector_done, ve.step())
                eng.wait_ge(vector_done, ve.own())
                sel = r3[:, :, 0:8]

                def first_max(vals, mx, tmp, hot, name=None):
                    red(mx, vals, ALU.max).then_inc(vector_done, ve.step())
                    eng.wait_ge(vector_done, ve.own())
                    tt(tmp, vals, bc(mx, 8), ALU.is_equal).then_inc(vector_done, ve.step())
                    eng.wait_ge(vector_done, ve.own())
                    tt(tmp, tmp, C("rank", 0, 8).unsqueeze(1).broadcast_to([P, 4, 8]), ALU.mult).then_inc(vector_done, ve.step())
                    eng.wait_ge(vector_done, ve.own())
                    red(rs_[:, 11, :], tmp, ALU.max).then_inc(vector_done, ve.step())
                    eng.wait_ge(vector_done, ve.own())
                    tt(hot, tmp, bc(rs_[:, 11, :], 8), ALU.is_equal).then_inc(vector_done, ve.step(name))
                    eng.wait_ge(vector_done, ve.own())
                first_max(sel, rs_[:, 2, :], r3[:, :, 8:16], r3[:, :, 16:24])
                stt(r3[:, :, 24:32], r3[:, :, 16:24], -3e38, sel, ALU.mult, ALU.add).then_inc(vector_done, ve.step())
                eng.wait_ge(vector_done, ve.own())
                first_max(r3[:, :, 24:32], rs_[:, 3, :], r3[:, :, 8:16], r2[:, :, 0:8])
                tt(rs_[:, 4, :], rs_[:, 3, :], rs_[:, 2, :], ALU.subtract).then_inc(vector_done, ve.step(("top2", l)))
                eng.wait_ge(scalar_done, ve.at(("eg", l)))
                red(rs_[:, 5, :], r1[:, :, 0:4], ALU.add).then_inc(vector_done, ve.step())
                eng.wait_ge(scalar_done, ve.at(("er", l)))
                ts(rs_[:, 6, :], rs_[:, 4, :], 1.0, op0=ALU.add).then_inc(vector_done, ve.step())
                eng.wait_ge(vector_done, ve.own())
                tt(rs_[:, 7, :], rs_[:, 5, :], rs_[:, 6, :], ALU.mult).then_inc(vector_done, ve.step())
                eng.wait_ge(vector_done, ve.own())
                v.reciprocal(rs_[:, 8, :], rs_[:, 7, :]).then_inc(vector_done, ve.step())
                eng.wait_ge(vector_done, ve.own())
                tt(rs_[:, 9, :], rs_[:, 8, :], rs_[:, 4, :], ALU.mult).then_inc(vector_done, ve.step())
                tt(r2[:, :, 8:16], r3[:, :, 16:24], bc(rs_[:, 8, :], 8), ALU.mult).then_inc(vector_done, ve.step())
                eng.wait_ge(vector_done, ve.own())
                tt(r2[:, :, 16:24], r2[:, :, 0:8], bc(rs_[:, 9, :], 8), ALU.mult).then_inc(vector_done, ve.step())
                eng.wait_ge(vector_done, ve.own())
                tt(r2[:, :, 24:32], r2[:, :, 8:16], r2[:, :, 16:24], ALU.add).then_inc(vector_done, ve.step())
                eng.wait_ge(vector_done, ve.own())
                for t in range(4):
                    tt(r4[:, t, 0:32].rearrange("p (g e) -> p g e", g=4),
                       goh[:, t, :].unsqueeze(2).broadcast_to([P, 4, 8]),
                       r2[:, t, 24:32].unsqueeze(1).broadcast_to([P, 4, 8]), ALU.mult).then_inc(vector_done, ve.step(("comb", l)))

            def moe(l):
                route(l)
                loop = f"moe{l}"
                with ve.loop(loop, 4):
                    for e in range(8):
                        eng.wait_ge(scalar_done, ve.at((loop, "t", e)))
                        ba, fa = full(loop, "a", e, "x")
                        stt(e_u[:, e % 2, :], e_t[:, e % 2, :], 1.0, ba, ALU.add, ALU.mult).then_inc(vector_done, ve.step([fa, (loop, "s", e)]))
                        bb, fb = full(loop, "b", e, "x")
                        eng.wait_ge(vector_done, ve.own())
                        stt(e_u[:, e % 2, :], e_u[:, e % 2, :], 0.5, bb, ALU.mult, ALU.mult).then_inc(vector_done, ve.step(fb))
                        eng.wait_ge(comb_row_landed[e % 4], ve.at((loop, "comb_row", e)))
                        if e == 0:
                            eng.wait_ge(tensor_done, ve.at((loop, "hid_used"), lag=1))
                        eng.wait_ge(vector_done, ve.own())
                        tt(hid[:, e, :], e_u[:, e % 2, :], wcomb[:, e % 4, :], ALU.mult).then_inc(vector_done, ve.step((loop, "hid", e)))
                    for j in range(8):
                        b, free = full(loop, "y", j)
                        stt(xT[:, j, :], b, M(l, 5, j), xT[:, j, :], ALU.mult, ALU.add).then_inc(vector_done, ve.step([free, ("x", loop, j)]))

            if stage_on(2):
                modulated("n2_0", V("norm2_w", 0, 8), M(0, 4, 0, 8), lambda k: M(0, 3, k), lambda k: xT[:, k, :])
                moe(0)
            if stage_on(3):
                for i in range(16, 20):
                    mod(i)
                modulated("n1_1", V("norm1_w", 8, 8), M(1, 1, 0, 8), lambda k: M(1, 0, k), lambda k: xT[:, k, :])
                v.memset(g_pad[:, 0:3], 0.0).then_inc(vector_done, ve.step("pad_zero"))
                b, free = full("dt")
                eng.wait_ge(dtb_landed, ve.at("dtb"))
                ts(dtT[0:32, 0, :], b[0:32, :], col("dtb", rows=32), op0=ALU.add).then_inc(vector_done, ve.step([free, "dt_v"]))
                v.memset(dtT[0:32, 2, :], 1.0).then_inc(vector_done, ve.step())
                eng.wait_ge(scalar_done, ve.at("dt_ln"))
                stt(dtT[0:32, 0, :], dtT[0:32, 0, :], 0.0, dtT[0:32, 1, :], ALU.max, ALU.add).then_inc(vector_done, ve.step())
                eng.wait_ge(scalar_done, ve.at("expA_log"))
                eng.wait_ge(vector_done, ve.own())
                ts(dtT[0:32, 1, :], dtT[0:32, 0, :], col("negA", rows=32), -1.0, ALU.mult, ALU.mult).then_inc(vector_done, ve.step())
                eng.wait_ge(vector_done, ve.own())
                v.tensor_tensor_scan(g_t[0:32, :], dtT[0:32, 2, :], dtT[0:32, 1, :], 0.0, ALU.mult, ALU.add).then_inc(vector_done, ve.step())
                eng.wait_ge(vector_done, ve.own())
                v.tensor_copy(dtT[0:32, 1, :], g_t[0:32, :]).then_inc(vector_done, ve.step("acs"))
                b, free = full("dtTok")
                bv = b[:, 0:256].rearrange("p (t n) -> p t n", t=4)
                ts(dtTok[:, :, 0:32], bv[:, :, 0:32], 0.5).then_inc(vector_done, ve.step())
                v.tensor_copy(dtTok[:, :, 32:64], bv[:, :, 32:64]).then_inc(vector_done, ve.step([free, "dtTok"]))
                for g in range(8):
                    for qi, n in enumerate(("x0", "x1", "B", "C")):
                        chunk = [2 * g, 2 * g + 1, 16 + g, 24 + g][qi]
                        dst = [g_x[:, 0, :], g_x[:, 1, :], g_bc[:, 0, :], g_bc[:, 1, :]][qi]
                        if g >= 1:
                            if qi < 2:
                                eng.wait_ge(tensor_done, ve.at(("full",) + jobname("xtok", g - 1, qi)))
                            else:
                                eng.wait_ge(tensor_done, ve.at(("full",) + jobname("cb", g - 1, 3)))
                        eng.wait_ge(scalar_done, ve.at(("pad", g, qi)))
                        ts(dst, g_pad[:, 3:3 + S], V("ssm_conv_w", 96 + chunk), V("ssm_conv_b", chunk), ALU.mult, ALU.add).then_inc(vector_done, ve.step())
                        for tap in (2, 1, 0):
                            eng.wait_ge(vector_done, ve.own())
                            stt(dst, g_pad[:, tap:tap + S], V("ssm_conv_w", 32 * tap + chunk), dst, ALU.mult, ALU.add).then_inc(vector_done, ve.step([("conv", g, qi), ("pad_used", (g, qi))]))
                        eng.wait_ge(scalar_done, ve.at(("conv_t", g, qi)))
                        eng.wait_ge(vector_done, ve.own())
                        stt(dst, g_t, 1.0, dst, ALU.add, ALU.mult).then_inc(vector_done, ve.step(("ssm_x", g, qi) if qi < 2 else ("ssm_bc", g, qi - 2)))
                    for zz in range(2):
                        eng.wait_ge(scalar_done, ve.at(("zt", g, zz)))
                        b, free = full("ssm", g, f"z{zz}", "x")
                        stt(g_z[:, zz, :], g_z[:, zz, :], 1.0, b, ALU.add, ALU.mult).then_inc(vector_done, ve.step(free))
                    for cc in range(2):
                        b, free = full("xtok", g, cc)
                        if g >= 1:
                            eng.wait_ge(tensor_done, ve.at(("seg_used", 4 * g - 1)))
                        for t in range(4):
                            ds = dtTok[:, t, 4 * g + 2 * cc:4 * g + 2 * cc + 2].unsqueeze(2).broadcast_to([P, 2, 64])
                            tt(g_xdt[:, t, P * cc:P * (cc + 1)].rearrange("p (h d) -> p h d", h=2),
                               b[:, t * P:(t + 1) * P].rearrange("p (h d) -> p h d", h=2), ds, ALU.mult).then_inc(vector_done, ve.step([free, ("xdt", g, cc)]))

                    def arg(h):
                        eng.wait_ge(acs_row_landed[h % 2], ve.at(("acs_row", h)))
                        if h >= 2:
                            eng.wait_ge(tensor_done, ve.at(("seg_used", h - 2)))
                        for t in range(4):
                            stt(g_seg[:, h % 2, SOFF[t]:SOFF[t] + S - t * P], acs_b[:, h % 2, t * P:S],
                                dtTok[:, t, 32 + h:33 + h], C("mask_next", 0, S - t * P), ALU.subtract, ALU.min).then_inc(vector_done, ve.step([("arg", h), ("acs_used", h)]))

                    def seg(h):
                        eng.wait_ge(scalar_done, ve.at(("seg_e", h)))
                        eng.wait_ge(scalar_done, ve.at(("cb_c", g)))
                        tt(g_seg[:, h % 2, :], g_seg[:, h % 2, :], g_cb, ALU.mult).then_inc(vector_done, ve.step(("seg", h)))
                    arg(4 * g)
                    for r in range(4):
                        if r < 3:
                            arg(4 * g + r + 1)
                        seg(4 * g + r)
                    for i in mods_at[("g", g)]:
                        mod(i)
                    for cc in range(2):
                        b, free = full("y", g, cc)
                        k = 2 * g + cc
                        stt(yT[:, k, :], g_x[:, cc, :], col("Dh", k), b, ALU.mult, ALU.add).then_inc(vector_done, ve.step(free))
                        eng.wait_ge(vector_done, ve.own())
                        tt(yT[:, k, :], yT[:, k, :], g_z[:, cc, :], ALU.mult).then_inc(vector_done, ve.step(("yz", g, cc)))
                    eng.wait_ge(scalar_done, ve.at(("rstd", ("g", g), "x")))
                    for cc in range(2):
                        k = 2 * g + cc
                        stt(yT[:, k, :], yT[:, k, :], col("nwh", k), rstd[:, 0:S]).then_inc(vector_done, ve.step([("yn", k), ("rstd_used", ("g", g))]))
                for c in range(8):
                    b, free = full("outM", c, "x")
                    stt(xT[:, c, :], b, M(1, 2, c), xT[:, c, :], ALU.mult, ALU.add).then_inc(vector_done, ve.step([free, ("xM", c)]))
                    for i in mods_at.get(("o", c), []):
                        mod(i)
            if stage_on(4):
                modulated("n2_1", V("norm2_w", 8, 8), M(1, 4, 0, 8), lambda k: M(1, 3, k), lambda k: xT[:, k, :])
                moe(1)
            if stage_on(5):
                eng.wait_ge(scalar_done, ve.at(("rstd", "fin1", "x")))
                for k in range(KD):
                    stt(xT[:, k, :], xT[:, k, :], V("final_norm_w", k), rstd[:, 0:S]).then_inc(vector_done, ve.step(("rstd_used", "fin1")))
            if stage_on(6):
                eng.wait_ge(vector_done, ve.own())
                v.memset(col("stat", 0, 64), 0.0).then_inc(vector_done, ve.step(("x_in", 0)))
                eng.wait_ge(scalar_done, ve.at("lgt"))
                stt(col("lg", 0, 16), col("small", 0, 16), 0.0, col("lgt", 0, 16), ALU.min, ALU.subtract).then_inc(vector_done, ve.step())
                eng.wait_ge(vector_done, ve.own())
                ts(col("lgm", 0, 16), col("lg", 0, 16), -float(P)).then_inc(vector_done, ve.step())
                ts(col("lgp", 0, 16), col("lg", 0, 16), float(P)).then_inc(vector_done, ve.step())
                ts(col("hlb", 0, 8), V("cf_ln_b_2", 0, 8), 0.5).then_inc(vector_done, ve.step())
                zn = {"n": 0}

                def z_mul(name, l, c, cx, chunk, factor):
                    n = zn["n"]
                    zn["n"] += 1
                    for tag, o, w in parts(cx):
                        eng.wait_ge(scalar_done, ve.at(("zt", n, tag)))
                        b, free = full(name, l, c, tag)
                        stt(zt[:, n % 2, o:o + w], zt[:, n % 2, o:o + w], 1.0, b[:, 0:w], ALU.add, ALU.mult).then_inc(vector_done, ve.step(free))
                    return n

                def z_apply(n, l, cx, chunk, factor):
                    eng.wait_ge(vector_done, ve.own())
                    for tag, o, w in parts(cx):
                        bo = CO if tag == "c" else 0
                        stt(br[:, chunk, bo:bo + w], br[:, chunk, bo:bo + w], factor, zt[:, n % 2, o:o + w], ALU.mult, ALU.mult).then_inc(vector_done, ve.step([("zt_used", n), ("branch", l, chunk)]))

                for l in range(2 if upto > 6 else 1):
                    cx = l == 0
                    w_ = CW if cx else S
                    M2 = lambda part, k, n=1, vv=0: col("mod2", 48 * l + 24 * vv + 8 * part + k, n)
                    modulated(("b2", l), V("norm_w_2", 8 * l, 8), M2(1, 0, 8), lambda k: M2(0, k), lambda k: xT[:, k, :],
                              ctx_part=(M2(1, 0, 8, 1), lambda k: M2(0, k, 1, 1)))
                    for i in range(2):
                        v.memset(cu[:, i, :], 0.0).then_inc(vector_done, ve.step([("cu_free", l, i)]))
                    if cx:
                        for c in range(16):
                            v.memset(br[:, c, S:CO], 0.0).then_inc(vector_done, ve.step())
                    cw = lambda k, c: V(f"cf_conv_w_2{'ab'[l]}", 4 * k + c)
                    for c in range(4):
                        for tag, o, w in parts(cx, CO):
                            eng.wait_ge(scalar_done, ve.at(("cf_t", l, c, tag)))
                            b, free = full("cf_a", l, c, tag)
                            u = cu[:, c % 2, 15 + o:15 + o + w]
                            stt(u, u, 1.0, b[:, 0:w], ALU.add, ALU.mult).then_inc(vector_done, ve.step(free))
                        eng.wait_ge(vector_done, ve.own())
                        acc = br[:, 8 + c, 0:w_]
                        ts(acc, cu[:, c % 2, 0:w_], cw(0, c)).then_inc(vector_done, ve.step())
                        for k in range(1, 31):
                            eng.wait_ge(vector_done, ve.own())
                            stt(acc, cu[:, c % 2, k:k + w_], cw(k, c), acc, ALU.mult, ALU.add).then_inc(vector_done, ve.step(("cu_free", l, c + 2) if k == 30 else None))
                        eng.wait_ge(vector_done, ve.own())
                        ts(acc, acc, 0.5, V("cf_conv_b_2", 4 * l + c), ALU.mult, ALU.add).then_inc(vector_done, ve.step(("cf_conv", l, c)))

                    eng.wait_ge(rope_landed, ve.at(("rope", l)))

                    def rotate(t, job_, name):
                        b, free = full(*job_)
                        tt(t, t, cos_, ALU.mult).then_inc(vector_done, ve.step())
                        r_ = square[:, 0, 0:S]
                        tt(r_, b, sin_, ALU.mult).then_inc(vector_done, ve.step(free))
                        eng.wait_ge(vector_done, ve.own())
                        tt(t, t, r_, ALU.add).then_inc(vector_done, ve.step(name))
                    eng.wait_ge(tensor_done, ve.at(("sq_used", ("b2", l), KD - 1)))
                    rotate(k_raw[:, 0:S], ("rot_k", l), ("k_roped", l))
                    eng.wait_ge(vector_done, ve.own())
                    for c in range(4):
                        rotate(q_[:, c, 0:S], ("rot_q", l, c), ("roped", l))
                        eng.wait_ge(vector_done, ve.own())

                    rounds = [(n, j) for n in x_tiles(l) for j in range(2)]

                    def att_max(r, n, j):
                        q = r % 2
                        kt = key_tiles(n)
                        wl = P * len(kt)
                        for hh in range(4):
                            h = 4 * j + hh
                            if r >= 2:
                                pn, pj = rounds[r - 2]
                                eng.wait_ge(tensor_done, ve.at(("full",) + jobname("pt2", l, 4 * pj + hh, pn, "x")))
                            if wl:
                                off = P * (kt[0] - (n - 1))
                                b, free = full("sl", l, h, n)
                                stt(pr2[q][:, hh, 0:wl], b[:, 0:wl], 0.125, C("window", off, wl), ALU.mult, ALU.add).then_inc(vector_done, ve.step(free))
                            b, free = full("sx", l, h, n)
                            ts(pr2[q][:, hh, wl:wl + L], b[:, 0:L], 0.125).then_inc(vector_done, ve.step(free))
                        eng.wait_ge(vector_done, ve.own())
                        red(col("stat", 32 * q, 4), pr2[q][:, :, 0:wl + L], ALU.max).then_inc(vector_done, ve.step())
                        eng.wait_ge(vector_done, ve.own())
                        sink = col("small", 16 + 8 * l + 4 * j, 4)
                        tt(col("stat", 32 * q, 4), col("stat", 32 * q, 4), sink, ALU.max).then_inc(vector_done, ve.step())
                        eng.wait_ge(vector_done, ve.own())
                        ts(col("stat", 32 * q + 4, 4), col("stat", 32 * q, 4), -1.0).then_inc(vector_done, ve.step())
                        tt(col("stat", 32 * q + 12, 4), sink, col("stat", 32 * q, 4), ALU.subtract).then_inc(vector_done, ve.step(("nm2", l, n, j)))

                    def att_norm(r, n, j):
                        q = r % 2
                        w = P * len(key_tiles(n)) + L
                        eng.wait_ge(scalar_done, ve.at(("es2", l, n, j)))
                        tt(col("stat", 32 * q + 16, 4), col("stat", 32 * q + 8, 4), col("stat", 32 * q + 12, 4), ALU.add).then_inc(vector_done, ve.step())
                        eng.wait_ge(vector_done, ve.own())
                        v.reciprocal(col("stat", 32 * q + 20, 4), col("stat", 32 * q + 16, 4)).then_inc(vector_done, ve.step())
                        eng.wait_ge(vector_done, ve.own())
                        for hh in range(4):
                            pr = pr2[q][:, hh, 0:w]
                            ts(pr, pr, col("stat", 32 * q + 20 + hh)).then_inc(vector_done, ve.step(("pr2", l, n, 4 * j + hh)))
                    att_max(0, *rounds[0])
                    for r, (n, j) in enumerate(rounds):
                        att_norm(r, n, j)
                        if r + 1 < len(rounds):
                            att_max(r + 1, *rounds[r + 1])
                    eng.wait_ge(scalar_done, ve.at(("att_o", l)))
                    for c in range(4):
                        z_apply(z_mul("att_z", l, c, cx, 12 + c, 0.5), l, cx, 12 + c, 0.5)
                    eng.wait_ge(vector_done, ve.own())
                    v.memset(col("stat", 0, 1), 0.0).then_inc(vector_done, ve.step(("att_done", l)))

                    def decay(h):
                        lf, lb = 8 * l + h, 8 * l + 4 + h
                        eng.wait_ge(tabs_landed, ve.at(("tabs", l)))
                        eng.wait_ge(vector_done, ve.own())
                        ts(rdt, dminus, col("lg", lb)).then_inc(vector_done, ve.step())
                        eng.wait_ge(vector_done, ve.own())
                        stt(dstrip, dplus, col("lg", lf), rdt, ALU.mult, ALU.add).then_inc(vector_done, ve.step(("darg", l, h)))
                        eng.wait_ge(scalar_done, ve.at(("rtmp", l, h)))
                        tt(rctx[:, :, :], rctx[:, :, :], rtmp[:, :, :], ALU.add).then_inc(vector_done, ve.step())
                        eng.wait_ge(scalar_done, ve.at(("dstrip", l, h)))
                        eng.wait_ge(vector_done, ve.own())
                    for h in range(4):
                        decay(h)
                        ks = P ** -0.5
                        for t in range(6):
                            b, free = full("rs", l, h, t)
                            dec = dstrip[:, 384 - P * t:384 - P * t + S] if t < 4 else rctx[:, t - 4, :]
                            stt(rsc[:, t, :], b, ks, dec, ALU.mult, ALU.mult).then_inc(vector_done, ve.step([free, ("rsc", l, h, t)]))
                        if cx:
                            for t in range(2):
                                b, free = full("rs_c", l, h, t)
                                stt(rsc_c[:, t, :], b[:, 0:L], ks, dstrip[:, 384 - P * t:384 - P * t + L], ALU.mult, ALU.mult).then_inc(vector_done, ve.step([free, ("rsc_c", l, h)]))
                        eng.wait_ge(vector_done, ve.own())
                        v.memset(col("stat", 1, 1), 0.0).then_inc(vector_done, ve.step(("rctx_used", l, h)))
                        zi = z_mul("ret_z", l, h, cx, h, -0.5)
                        for tag, o, w in parts(cx):
                            b, free = full("rm", l, h, tag)
                            stt(rnd[:, o:o + w], b[:, 0:w], 1.0 / P, ro[:, o:o + w], ALU.mult, ALU.subtract).then_inc(vector_done, ve.step([free, ("rnd", l, h, tag)]))
                        eng.wait_ge(scalar_done, ve.at(("rstd", ("ret", l, h), "c" if cx else "x")))
                        for tag, o, w in parts(cx):
                            bo = CO if tag == "c" else 0
                            stt(br[:, h, bo:bo + w], rnd[:, o:o + w], V("ret_gn_w_2", 4 * l + h), rstd[:, o:o + w]).then_inc(vector_done, ve.step([("rstd_used", ("ret", l, h))]))
                        z_apply(zi, l, cx, h, -0.5)
                    eng.wait_ge(vector_done, ve.own())
                    v.memset(sc_u[:, :, :], 0.0).then_inc(vector_done, ve.step(("ret_done", l)))
                    eng.wait_ge(vector_done, ve.own())
                    for c in range(4):
                        for tag, o, w in parts(cx):
                            bo = CO if tag == "c" else 0
                            eng.wait_ge(scalar_done, ve.at(("sc_cc", l, c, tag)))
                            b, free = full("sc_x", l, c, tag)
                            tt(sc_u[:, c % 2, 1 + bo:1 + bo + w], b[:, 0:w], sc_c[:, c % 2, o:o + w], ALU.mult).then_inc(vector_done, ve.step([free, ("sc_c_used", l, c)]))
                        wv = lambda k: V("sc_conv_w_2", 12 * l + 4 * k + c)
                        y = br[:, 4 + c, 0:w_]
                        eng.wait_ge(vector_done, ve.own())
                        ts(y, sc_u[:, c % 2, 0:w_], wv(0)).then_inc(vector_done, ve.step())
                        for k in (1, 2):
                            eng.wait_ge(vector_done, ve.own())
                            stt(y, sc_u[:, c % 2, k:k + w_], wv(k), y, ALU.mult, ALU.add).then_inc(vector_done, ve.step())
                        eng.wait_ge(vector_done, ve.own())
                        for tag, o, w in parts(cx):
                            bo = CO if tag == "c" else 0
                            b, free = full("sc_b", l, c, tag)
                            tt(br[:, 4 + c, bo:bo + w], br[:, 4 + c, bo:bo + w], b[:, 0:w], ALU.mult).then_inc(vector_done, ve.step(free))
                        z_apply(z_mul("sc_z", l, c, cx, 4 + c, 0.5), l, cx, 4 + c, 0.5)
                    eng.wait_ge(vector_done, ve.own())
                    for tag, o, w in parts(cx, CO):
                        b, free = full("lm", l, tag)
                        for c in range(4):
                            t_ = br[:, 8 + c, o:o + w]
                            stt(t_, b[:, 0:w], 1.0 / (4 * P), t_, ALU.mult, ALU.subtract).then_inc(vector_done, ve.step([("cf_nd", l, c)] + ([free] if c == 3 else [])))
                    eng.wait_ge(scalar_done, ve.at(("rstd", ("ln", l), "c" if cx else "x")))
                    for c in range(4):
                        for tag, o, w in parts(cx):
                            bo = CO if tag == "c" else 0
                            t_ = br[:, 8 + c, bo:bo + w]
                            stt(t_, t_, V("cf_ln_w_2", 4 * l + c), rstd[:, o:o + w]).then_inc(vector_done, ve.step([("cf_v", l, c), ("rstd_used", ("ln", l))]))
                    for c in range(4):
                        t_ = br[:, 8 + c, 0:w_]
                        eng.wait_ge(scalar_done, ve.at(("cf_tt", l, c)))
                        ts(t_, t_, -1.0, V("cf_ln_b_2", 4 * l + c), ALU.mult, ALU.add).then_inc(vector_done, ve.step())
                        eng.wait_ge(vector_done, ve.own())
                        stt(t_, cf_t[:, c % 2, 0:w_], 1.0, t_, ALU.add, ALU.mult).then_inc(vector_done, ve.step(("cf_y", l, c)))
                    for c in range(4):
                        z_apply(z_mul("cf_z", l, c, cx, 8 + c, 0.25), l, cx, 8 + c, 0.25)
                    eng.wait_ge(vector_done, ve.own())
                    v.memset(col("stat", 0, 1), 0.0).then_inc(vector_done, ve.step(("cf_done", l)))
                    for c in range(8):
                        for i in range(4):
                            m = 4 * c + i
                            for tag, o, w in parts(cx):
                                eng.wait_ge(scalar_done, ve.at(("mt", l, m, tag)))
                                b, free = full("by", l, c, i, tag)
                                dst = mrg[:, c, o:o + w] if i == 0 else mt[:, m % 4, o:o + w]
                                stt(dst, mt[:, m % 4, o:o + w], 1.0, b[:, 0:w], ALU.add, ALU.mult).then_inc(vector_done, ve.step([free, ("mt_used", l, m)]))
                            if i:
                                eng.wait_ge(vector_done, ve.own())
                                w = S + L if cx else S
                                tt(mrg[:, c, 0:w], mrg[:, c, 0:w], mt[:, m % 4, 0:w], ALU.add).then_inc(vector_done, ve.step([("mt_used", l, m)] + ([("mrg", l, c)] if i == 3 else [])))
                    for vv in range(2):
                        ts(col("hg", 8 * vv, 8), M2(2, 0, 8, vv), 0.5).then_inc(vector_done, ve.step())
                    eng.wait_ge(vector_done, ve.own())
                    for c in range(8):
                        for tag, o, w in parts(cx):
                            b, free = full("out2", l, c, tag)
                            t_ = (xT if tag == "x" else cT)[:, c, :]
                            stt(t_, b[:, 0:w], col("hg", c if tag == "x" else 8 + c), t_, ALU.mult, ALU.add).then_inc(vector_done, ve.step(free))
                    eng.wait_ge(vector_done, ve.own())
                    v.memset(col("stat", 0, 1), 0.0).then_inc(vector_done, ve.step(("x_in", l + 1)))
                if upto > 7:
                    eng.wait_ge(scalar_done, ve.at(("rstd", "fin2", "x")))
                    for k in range(KD):
                        stt(xT[:, k, :], xT[:, k, :], V("final_norm_w_2", k), rstd[:, 0:S]).then_inc(vector_done, ve.step(("rstd_used", "fin2")))
            eng.wait_ge(vector_done, ve.own())
            v.memset(col("stat", 0, 1), 0.0).then_inc(vector_done, ve.step("x_final"))

        @block.gpsimd
        def _(eng):
            po = Count(eng, "gpsimd_done", sems, old, new)
            g = nc.gpsimd

            def mod_load(q):
                i, half = q // 2, q % 2
                kind, l, b = MODS[i]
                if q >= 2:
                    eng.wait_ge(po.doer(("mod_half", q - 2)), po.at(("mod_half", q - 2)))
                eng.dma_start(mod_w[:, half], a[kind][l][512 * half:512 * half + 512, 512 * b:512 * b + 512]
                       .rearrange("(k p) n -> p k n", p=P)).then_inc(mod_w_landed[half], po.landing(f"mod_w_{half}", ("mod_w", q)))

            mod_load(0)
            mod_load(1)
            eng.wait_ge(vector_done, po.at("csilu"))
            for i in range(len(MODS)):
                for half in range(2):
                    if i >= DVE_MODS:
                        eng.wait_ge(mod_w_landed[half], po.at(("mod_w", 2 * i + half)))
                        w = mod_w[:, half]
                        for vi, s in enumerate(mod_slots(i)):
                            if half == 0:
                                q = sidx[i][vi]
                                eng.wait_ge(tensor_done, po.at(("full",) + jobname("mod", owner[q - 4])))
                            prod = w if vi == len(mod_slots(i)) - 1 else mod_t
                            c_ = col("csilu", (0 if i < 24 else 8 * (1 + vi)) + 4 * half, 4)
                            if (i, half) != (DVE_MODS, 0):
                                eng.wait_ge(gpsimd_done, po.own())
                            g.tensor_tensor(prod, w, c_.unsqueeze(2).broadcast_to([P, 4, S]), ALU.mult).then_inc(gpsimd_done, po.step())
                            eng.wait_ge(gpsimd_done, po.own())
                            g.tensor_tensor(prod[:, 0:2], prod[:, 0:2], prod[:, 2:4], ALU.add).then_inc(gpsimd_done, po.step())
                            eng.wait_ge(gpsimd_done, po.own())
                            if half:
                                g.tensor_tensor(prod[:, 0], prod[:, 0], prod[:, 1], ALU.add).then_inc(gpsimd_done, po.step())
                                eng.wait_ge(gpsimd_done, po.own())
                                g.tensor_tensor(mod_acc[:, s, :], mod_acc[:, s, :], prod[:, 0], ALU.add).then_inc(gpsimd_done, po.step([("mod_half", 2 * i + 1), ("mod_acc", i)]))
                            else:
                                g.tensor_tensor(mod_acc[:, s, :], prod[:, 0], prod[:, 1], ALU.add).then_inc(gpsimd_done, po.step(("mod_half", 2 * i)))
                    if 2 * (i + 1) + half < 2 * len(MODS):
                        mod_load(2 * (i + 1) + half)


def host_constants():
    import numpy as np
    p = np.arange(P)[:, None]
    t = {}
    t["ident"] = np.eye(P)
    m = np.arange(S)[None, :]
    t["mask_next"] = np.where(m >= p, 0.0, -1e30)
    k = np.arange(P)[None, :]
    t["window"] = np.concatenate([np.where(k >= p, 0, -1e30), np.zeros((P, P)), np.where(k <= p, 0, -1e30)], 1)
    t["rank"] = np.broadcast_to(np.arange(8, 0, -1), (P, 8))
    t["inv_count"] = np.concatenate([np.broadcast_to(np.float32(1) / np.minimum(np.arange(1, 17), w), (P, 16))
                                     for w in (2, 4, 8, 16)], 1)
    rot = np.zeros((P, P))
    for h in range(2):
        for j in range(32):
            rot[64 * h + 32 + j, 64 * h + j] = -1.0
            rot[64 * h + j, 64 * h + 32 + j] = 1.0
    t["rot"] = rot
    inv = np.float32(10000.0) ** (-np.arange(16, dtype=np.float32) / np.float32(16))
    pos = np.arange(S)
    ang = np.concatenate([(pos // 64).astype(np.float32)[:, None] * inv, (pos % 64).astype(np.float32)[:, None] * inv], 1)
    t["cos"] = np.tile(np.cos(ang).T, (4, 1))
    t["sin"] = np.tile(np.sin(ang).T, (4, 1))
    d = np.arange(896)[None, :] - 384 - p
    t["dplus"], t["dminus"] = np.maximum(d, 0), np.maximum(-d, 0)
    i = np.arange(S)[None, :]
    t["to_end"] = i + L - p
    t["to_start"] = S - i + p
    return np.ascontiguousarray(np.concatenate([np.broadcast_to(t[n], (P, w)) for n, w in CONST_COLS], 1), np.float32)


UPTO = 99


def layout(inputs):
    import numpy as np
    big = ["x", "ctx_2", "ada_w", "mix_w_in", "pool_w", "mix_w_out", "ssm_w_in", "ssm_w_out", "moe_w1", "moe_w3",
           "moe_w2", "w_mod_2", "w_in_2", "w_branch_2", "w_out_2", "ssm_dt_bias", "ssm_A_log"]
    arrays = {n: np.ascontiguousarray(inputs[n]) for n in big}
    rows = []
    for n, k in VEC_ROWS:
        if n.startswith("pad"):
            v = np.zeros((k, P), np.float32)
        elif n == "ssm_D":
            v = np.repeat(np.asarray(inputs[n])[0], 64).reshape(k, P)
        elif n in ("cf_conv_w_2a", "cf_conv_w_2b"):
            v = np.asarray(inputs["cf_conv_w_2"])[int(n[-1] == "b")].reshape(k, P)
        else:
            v = np.asarray(inputs[n]).reshape(k, P)
        rows.append(v)
    arrays["vecs"] = np.concatenate(rows, 0)
    arrays["w_router"] = np.concatenate([np.asarray(inputs["moe_w_group"]),
                                         np.asarray(inputs["moe_w_expert"]).reshape(2, D, 32)], 2)
    arrays["small"] = np.concatenate([np.concatenate([np.asarray(inputs["moe_b_group"]),
                                                      np.asarray(inputs["moe_b_expert"]).reshape(2, 32)], 1).reshape(-1),
                                      np.asarray(inputs["ret_decay_2"]).reshape(-1),
                                      np.asarray(inputs["att_sink_2"]).reshape(-1)])[None, :]
    rel = np.asarray(inputs["rel_bias"])[0][:, ::-1]
    rel = np.concatenate([np.repeat(rel[:, :1], 255, 1), rel[:, :385]], 1)
    arrays["rel_tiles"] = np.stack([rel[:, P - 1 - q:P - 1 - q + S] for q in range(P)], 1)
    arrays["consts"] = host_constants()
    return {n: np.ascontiguousarray(v) for n, v in arrays.items()}


def kernel(**inputs):
    from concourse import bacc
    from concourse.bass_utils import run_bass_kernel_spmd

    arrays = layout(inputs)
    marks = {}
    for _ in range(2):
        nc = bacc.Bacc("TRN2", target_bir_lowering=False, num_devices=1, dynamic_dma_scratch_size=8192)
        aps = {n: nc.dram_tensor(f"in_{n}", v.shape, mybir.dt.from_np(v.dtype), kind="ExternalInput").ap()
               for n, v in arrays.items()}
        result = nc.dram_tensor("result_dram", (1, S, D), F32, kind="ExternalOutput").ap()
        found = {}
        program(nc, aps, result, UPTO, marks, found)
        marks = found
    r = run_bass_kernel_spmd(nc, [{f"in_{n}": v for n, v in arrays.items()}], core_ids=[0])
    return r.results[0]["result_dram"]
```

```python
from contextlib import ExitStack, contextmanager

import concourse.bass as bass
from concourse import mybir

F32 = mybir.dt.float32
ALU = mybir.AluOpType
ACT = mybir.ActivationFunctionType
AX = mybir.AxisListType.X

P = 128
S = 512
L = 256
D = 1024
KD = D // P
EPS = 1e-6
RING = 8
BANKS = 8
EXPERTS = 32
BLOCKS = 40
assert BLOCKS >= EXPERTS + (2 * S - EXPERTS) // P
AHEAD = 4
TURN = 8
NO_PAIR = 8192
CW = 783
CO = S + 15

VEC_ROWS = [
    ("c", 8), ("norm1_w", 16), ("norm2_w", 16), ("final_norm_w", 8), ("pool_scale", 4), ("c_2", 8),
    ("c_ctx_2", 8), ("norm_w_2", 16), ("final_norm_w_2", 8), ("ssm_norm_w", 16), ("ssm_D", 16), ("pad0", 4),
    ("ada_b", 96), ("cf_conv_b_2", 8), ("cf_ln_w_2", 8), ("cf_ln_b_2", 8), ("ret_gn_w_2", 8),
    ("ssm_conv_w", 128),
    ("ssm_conv_b", 32), ("b_mod_2", 48), ("sc_conv_w_2", 24), ("pad1", 24),
    ("cf_conv_w_2a", 124), ("pad2", 4), ("cf_conv_w_2b", 124), ("pad3", 4),
]
VEC = {}
_row = 0
for _name, _n in VEC_ROWS:
    VEC[_name] = _row
    _row += _n
VT = _row // P

CONST_COLS = [("ident", P), ("mask_next", S), ("window", 3 * P), ("rank", 8), ("inv_count", 64),
              ("rot", P), ("cos", S), ("sin", S),
              ("dplus", 896), ("dminus", 896), ("to_end", S), ("to_start", S),
              ("prefix", 32), ("thresholds", 4), ("block_no", 40), ("pair_less", 8), ("block_start", 41), ("lane", P)]
CONST = {}
_col = 0
for _name, _n in CONST_COLS:
    CONST[_name] = (_col, _n)
    _col += _n
CONST_W = _col
ROUTE_W = 253
CONST1_W = CONST["rot"][0]


class Count:

    def __init__(self, eng, key, sems, old, new):
        self.eng, self.key, self.sems, self.old, self.new = eng, key, sems, old, new
        self.n, self.local = {}, {}
        self.loop_name, self.i, self.last = None, None, None

    def landing(self, key, name):
        return self._bump(key, 16, name)

    def step(self, name=None):
        return self._bump(self.key, 1, name)

    def _bump(self, key, amount, name):
        book = self.n if self.loop_name is None else self.local
        book[key] = book.get(key, 0) + amount
        at = (key, self.loop_name, book[key])
        for x in name if isinstance(name, list) else [name]:
            if x is not None:
                self.new[x] = at
        if key == self.key:
            self.last = at
        return amount

    def _value(self, at, lag=0):
        key, loop, value = at
        if loop is None:
            return value
        base, per, count = self.old.get(("loop", loop, key), (0, 1, 1))
        if loop == self.loop_name:
            return self.i * per + (base + value - lag * per)
        return base + (count - 1) * per + value

    def at(self, name, lag=0):
        return self._value(self.old[name], lag) if self.old else 1

    def own(self):
        return self._value(self.last)

    def doer(self, name):
        return self.sems(self.old[name][0] if self.old else self.key)

    @contextmanager
    def loop(self, name, count):
        base = dict(self.n)
        self.local, self.last = {}, None
        with self.eng.Fori(0, count) as i:
            self.loop_name, self.i = name, i
            yield i
        for key, per in self.local.items():
            self.new[("loop", name, key)] = (base.get(key, 0), per, count)
            self.n[key] = base.get(key, 0) + per * count
        self.loop_name, self.i, self.local = None, None, {}
        self.last = (self.key, None, self.n.get(self.key, 0)) if self.n.get(self.key) else None


class Ring:

    def __init__(self, lane):
        self.lane, self.n, self.l, self.parts = lane, 0, 0, []

    def next(self):
        if self.lane.loop_name is None:
            n = self.n
            self.n += 1
            return n % RING, ("use", n), self._flat(n - RING), 0
        loop, l = self.lane.loop_name, self.l
        self.l += 1
        per = self.lane.old.get(("ring", loop), RING)
        back, lag = (l - RING, 0) if l >= RING else (l - RING + per, 1)
        return (self.n + l) % RING, ("use", loop, l), ("use", loop, back), lag

    def _flat(self, n):
        for start, per, count, loop in self.parts:
            if start <= n < start + per * count:
                return ("use", loop, (n - start) % per)
        return ("use", n) if n >= 0 else None

    def enter(self):
        self.l = 0

    def leave(self, loop, count):
        self.lane.new[("ring", loop)] = self.l
        assert self.l % RING == 0
        self.parts.append((self.n, self.l, count, loop))
        self.n += self.l * count


def program(nc, a, out, upto, old, new):
    ctx = ExitStack()
    with ctx:
        def sb(name, shape, dt=F32):
            return ctx.enter_context(nc.sbuf_tensor(name, shape, dt))

        semaphores = {}

        def sems(key):
            if key not in semaphores:
                semaphores[key] = ctx.enter_context(nc.semaphore(key))
            return semaphores[key]

        xT = sb("xT", [P, KD, S])
        cT = sb("cT", [P, KD, L])
        hT = sb("hT", [P, KD, S + L])
        ring = sb("ring", [P, RING, KD, P])
        vec = sb("vec", [P, VT * P])
        const = sb("const", [P, CONST1_W])
        ones = sb("ones", [P, P])
        cols = sb("cols", [P, 640])
        square = sb("square", [P, 2, S + L])
        rstd = sb("rstd", [P, S + L])
        AW = 28672
        arena = sb("arena", [P, AW])
        MODW = AW - 6144
        mod_w = arena[:, MODW:MODW + 4096].rearrange("p (b k n) -> p b k n", b=2, k=4)
        mod_acc = arena[:, MODW + 4096:AW].rearrange("p (b n) -> p b n", b=4)
        psum = ctx.enter_context(nc.psum_tensor("psum", [P, BANKS, S], F32))
        h_dram = [nc.dram_tensor(f"h_dram_{l}", [S, D], F32).ap() for l in range(2)]
        y_dram = [nc.dram_tensor(f"y_dram_{l}", [2 * S, D], F32).ap() for l in range(2)]
        U32 = mybir.dt.uint32
        pair_u = sb("pair_u", [P, 2, BLOCKS + AHEAD], U32)
        expert_u = sb("expert_u", [1, BLOCKS], U32)
        now_u = sb("now_u", [P, 2, AHEAD], U32)
        acs_dram = nc.dram_tensor("acs_dram", [32, S], F32).ap()

        tensor_done, scalar_done, vector_done, gpsimd_done = (
            sems("tensor_done"), sems("scalar_done"), sems("vector_done"), sems("gpsimd_done"))
        vraw_landed, const_landed, xraw_landed, craw_landed = sems("vraw"), sems("const"), sems("xraw"), sems("craw")
        ident_landed = sems("ident_in")
        pool_w_landed, dtb_landed, A_log_landed = sems("pool_w"), sems("dtb"), sems("A_log")
        rw_landed, rb_landed, small_landed = sems("rw"), sems("rb"), sems("small")
        rope_landed, tabs_landed = sems("rope"), sems("tabs")
        acs_out_landed, result_landed = sems("acs_out"), sems("result")
        route_c_landed, h_rows_stored = sems("route_c"), sems("h_rows_stored")
        pool_go = sems("pool_go")
        rows_landed = [sems(f"rows_{i}") for i in range(AHEAD)]
        y_stored = [sems(f"y_stored_{i}") for i in range(AHEAD)]
        y_back_landed = [sems(f"y_back_{i}") for i in range(4)]
        weights_landed = [sems(f"weights_{i}") for i in range(RING)]
        acs_row_landed = [sems(f"acs_row_{i}") for i in range(2)]
        bias_landed = [sems(f"bias_{i}") for i in range(2)]
        mod_w_landed = [sems(f"mod_w_{i}") for i in range(2)]

        def V(name, j=0, n=1):
            r = VEC[name] + j
            return vec[:, r:r + n]

        def C(name, lo=0, n=None):
            o, w = CONST[name]
            return const[:, o + lo:o + (w if n is None else lo + n)]

        col_at = {}

        def col(name, j=0, n=1, rows=P):
            o, w = col_at[name]
            assert j + n <= w
            return cols[0:rows, o + j:o + j + n]

        _o = 0
        for _n, _w in (("zero", 1), ("one", 1), ("eps", 1), ("csilu", 24), ("mod", 96), ("mod2", 96), ("A", 8), ("A2", 8),
                       ("Dh", 16), ("nwh", 16), ("dtb", 1), ("negA", 1), ("lgf", 4), ("lgb", 4), ("lgfb", 4),
                       ("lgbb", 4), ("hb", 4), ("gate", 8), ("gate2", 8), ("epsg", 1), ("lng", 16), ("lnt", 16), ("stat", 64),
                       ("ctmp", 24), ("small", 32), ("lg", 16), ("lgt", 16), ("lgm", 16), ("lgp", 16), ("hlb", 8), ("hg", 16)):
            col_at[_n] = (_o, _w)
            _o += _w
        assert _o <= 640

        class Arena:
            def __init__(self, at=0, end=AW):
                self.at, self.end = at, end

            def take(self, *shape):
                n = 1
                for s in shape:
                    n *= s
                v = arena[:, self.at:self.at + n]
                self.at += n
                assert self.at <= self.end, (self.at, self.end)
                if len(shape) == 2:
                    v = v.rearrange("p (a b) -> p a b", b=shape[1])
                if len(shape) == 3:
                    v = v.rearrange("p (a b c) -> p a b c", b=shape[1], c=shape[2])
                return v

        def bank(name):
            return psum[:, old.get(("bank", name), 0), :]

        def block8(w, c0, width=P):
            return w[:, c0:c0 + width].rearrange("(k p) n -> p k n", p=P)

        IN_A = [12, 13, 14, 15, 0, 1, 2, 3, 4, 8, 5, 9, 6, 10, 7, 11]
        res = hT[:, :, :].rearrange("p a b -> p (a b)")

        def hT_res(t):
            return res[:, D * t:D * (t + 1)]

        def stage_on(n):
            return upto >= n

        m0 = Arena()
        vraw = m0.take(VT, P)
        xraw = m0.take(4, D)
        craw = m0.take(2, D)

        mA = Arena(end=MODW)
        aT = mA.take(8, S)
        qk = mA.take(8, S)
        vTok = mA.take(4, S)
        bias_s = mA.take(2, S)
        prob = [[mA.take(P * (t + 1)) for t in range(4)] for _ in range(2)]
        probT = mA.take(4, S)
        pool_w = mA.take(4, P)
        up = mA.take(4, S + 16)
        win_at = mA.at - 4 * (S + 16) - 4 * P - 4 * S
        win = [arena[:, win_at + (S + 16) * i:win_at + (S + 16) * (i + 1)] for i in range(2)]

        mE = Arena(end=MODW - 4 * S)
        rows = mE.take(AHEAD, D)
        y_rows = mE.take(AHEAD, D)
        rowsT = mE.take(2, 8, P)
        e_t = mE.take(2, P)
        e_u = mE.take(2, P)
        hid = mE.take(2, P)
        h_tok = mE.take(4, D)
        y_tok = [h_tok, rows]
        route_c = mE.take(ROUTE_W)
        scan_one = mE.take(S)
        pos = mE.take(S)
        slot_of = mE.take(S)
        place = mE.take(3, 8)
        passed = mE.take(8, BLOCKS + 1)
        in_block = mE.take(8, BLOCKS)
        in_lane = mE.take(8, P)
        pick = mE.take(2, 4 * 32)
        block_t = mE.take(3, BLOCKS + AHEAD)
        e_col = mE.take(8)
        rw = mE.take(8, 36)
        rb = mE.take(1)
        logitT = scan_one
        rt = mE.take(4, 36)
        r1 = mE.take(4, 36)
        r2 = mE.take(4, 36)
        r3 = mE.take(4, 36)
        r4 = mE.take(4, 36)
        rs_ = mE.take(12, 4)

        mM = Arena(end=MODW)
        yT = mM.take(16, S)
        g_z = mM.take(2, S)
        g_x = mM.take(2, S)
        g_bc = mM.take(2, S)
        g_pad = mM.take(S + 3)
        g_t = mM.take(S)
        g_cb = mM.take(1280)
        g_seg = mM.take(2, 1280)
        g_xdt = mM.take(4, 256)
        acs_b = mM.take(2, S)
        dtT = mM.take(3, S)
        dtTok = mM.take(4, 64)
        SOFF = [0, 512, 896, 1152]

        mB = Arena()
        br = mB.take(16, CW)
        R0 = mB.at
        zt_at = AW - 2 * (S + L)
        zt = arena[:, zt_at:AW].rearrange("p (b n) -> p b n", b=2)
        mQ = Arena(at=R0)
        q_ = mQ.take(4, S + L)
        kd = mQ.take(2, S + L)
        k_raw = mQ.take(S + L)
        v_tok = mQ.take(6, P)
        cu = mQ.take(2, 813)
        pT2 = mQ.take(5, S)
        v_raw = arena[:, mQ.at - 5 * S:mQ.at - 5 * S + S + L]
        pr2 = [mQ.take(4, 640), None]
        rope_at = mQ.at
        pr2[1] = mQ.take(4, 640)
        rope = arena[:, rope_at:rope_at + P + 2 * S]
        rot_, cos_, sin_ = rope[:, 0:P], rope[:, P:P + S], rope[:, P + S:P + 2 * S]
        mR = Arena(at=R0, end=zt_at)
        tabs = mR.take(2 * 896 + 2 * S)
        dplus, dminus = tabs[:, 0:896], tabs[:, 896:1792]
        to_end, to_start = tabs[:, 1792:1792 + S], tabs[:, 1792 + S:1792 + 2 * S]
        rq, rk, rv = mR.take(S + L), mR.take(S + L), mR.take(S + L)
        rv_tok = mR.take(6, P)
        rsc = mR.take(6, S)
        rsc_c = mR.take(2, L)
        dstrip = mR.take(896)
        rctx = mR.take(2, S)
        rtmp = mR.take(2, S)
        ro = mR.take(S + L)
        rnd = mR.take(S + L)
        rdt = arena[:, mR.at - 2 * (S + L):mR.at - 2 * (S + L) + 896]
        mS = Arena(at=R0, end=zt_at)
        sc_c = mS.take(2, S + L)
        sc_u = mS.take(2, 785)
        cf_t = mS.take(2, CW)
        mrg = mS.take(8, S + L)
        mt = mS.take(4, S + L)
        COL = dict(ret_q=0, ret_k=512, ret_v=1024, ret_z=1536, sc_b=2048, sc_c=2560, sc_x=3072, sc_z=3584, cf_a=4096,
                   cf_g=4608, cf_z=5120, att_q=5632, att_k=6144, att_v=6272, att_z=6400, gates=6912)

        ATT_AFTER = [[("att_k", 0), ("att_v", 0)], [("att_q", 0)], [("att_q", 1)], [("att_q", 2), ("att_q", 3)]]

        def in_blocks(l):
            order = []
            for c in range(4):
                order += [("cf_g", c), ("cf_a", c)] + ATT_AFTER[c]
            order += [("att_z", c) for c in range(4)]
            order += [(n, 0) for n in ("ret_q", "ret_k", "ret_v")]
            for h in range(4):
                order.append(("ret_z", h))
                if h < 3:
                    order += [(n, h + 1) for n in ("ret_q", "ret_k", "ret_v")]
            order += [(n, c) for c in range(4) for n in ("sc_c", "sc_x", "sc_b", "sc_z")]
            order += [("cf_z", c) for c in range(4)]
            return order

        def key_tiles(n):
            return [t for t in (n - 1, n, n + 1) if 0 <= t < 4] if n < 4 else []

        def x_tiles(l):
            return range(6 if l == 0 else 4)

        def tile_at(n):
            return P * n if n < 4 else CO + P * (n - 4)

        def parts(c, co=S):
            return [("x", 0, S)] + ([("c", co, L)] if c else [])

        def jobname(*x):
            return ("job",) + x

        MODS = [("ada_w", l, b) for l in range(2) for b in range(12)] + \
               [("w_mod_2", l, b) for l in range(2) for b in range(6)]
        if not stage_on(3):
            MODS = MODS[:12]
        elif not stage_on(6):
            MODS = MODS[:24]
        mods_at = {("a", 2 * h + 1): [10 + h] for h in range(4)}
        mods_at.update({("oA", 3): [14], ("oA", 7): [15]})
        mods_at.update({("g", g): v for g, v in enumerate(([20, 21], [22, 23], [24], [25, 26], [27, 28], [29, 30],
                                                           [31, 32], [33]))})
        mods_at.update({("o", 3): [34], ("o", 7): [35]})
        mods_at = {k: [i for i in v if i < len(MODS)] for k, v in mods_at.items()}

        DVE_MODS = 4
        mod_t = arena[:, MODW - 4 * S:MODW].rearrange("p (k n) -> p k n", k=4)

        mod_odd = mod_t

        def mod_slots(i):
            if i < 24:
                return [i % 4]
            return [(24 + 2 * (i - 24)) % 4, (24 + 2 * (i - 24) + 1) % 4]

        sidx = {}
        n_ = 0
        for i in range(len(MODS)):
            sidx[i] = list(range(n_, n_ + len(mod_slots(i))))
            n_ += len(mod_slots(i))
        owner = {q: i for i, v in sidx.items() for q in v}

        _r0 = CONST["prefix"][0]

        def R(name, rows_=P):
            o, w = CONST[name]
            return route_c[0:rows_, o - _r0:o - _r0 + w]

        def rows_at(l, i, b):
            return i * (16 * TURN // AHEAD) + 16 * (l * (BLOCKS // AHEAD + 1) + b // AHEAD + 1)

        def y_free_at(l, i, b):
            return rows_at(l, i, b)

        block = ctx.enter_context(nc.Block())

        @block.tensor
        def _(eng):
            pe = Count(eng, "tensor_done", sems, old, new)
            slots = Ring(pe)
            held = {}
            st = {"j": 0, "l": 0, "names": []}

            def job(*name):
                name = jobname(*name)
                if pe.loop_name is None:
                    b = st["j"] % BANKS
                    st["j"] += 1
                    if b in held:
                        eng.wait_ge(pe.doer(("free",) + held[b]), pe.at(("free",) + held[b]))
                else:
                    l = st["l"]
                    b = (st["j"] + l) % BANKS
                    st["l"] += 1
                    if b in st["in"]:
                        eng.wait_ge(pe.doer(("free",) + st["in"][b]), pe.at(("free",) + st["in"][b]))
                    else:
                        last = old.get(("lastjobs", pe.loop_name), {})
                        if b in last:
                            eng.wait_ge(pe.doer(("free",) + last[b]), pe.at(("free",) + last[b], lag=1))
                    st["in"][b] = name
                held[b] = name
                new[("bank", name)] = b
                return psum[:, b, :], ("full",) + name

            def take():
                slot, use, _, _ = slots.next()
                eng.wait_ge(weights_landed[slot], pe.at(("landed",) + use))
                return ring[:, slot], ("freed",) + use

            def linear(name, rhs, nk=KD, x=True, c=False, w=None, co=S, ready=None):
                parts = ([("x", 0, S)] if x else []) + ([("c", co, L)] if c else [])
                ws = [take() for _ in range((nk + 7) // 8)] if w is None else w
                for pi, (tag, o, n) in enumerate(parts):
                    b, full = job(*name, tag)
                    for k in range(nk):
                        if ready is not None:
                            eng.wait_ge(vector_done, pe.at(("h" if tag == "x" else "hc", ready, k)))
                        mm = nc.tensor.matmul(b[:, 0:n], ws[k // 8][0][:, k % 8, :], rhs(k)[:, o:o + n],
                                              start=(k == 0), stop=(k == nk - 1))
                    names = [full]
                    if pi == len(parts) - 1:
                        names += [w_[1] for w_ in ws]
                    mm.then_inc(tensor_done, pe.step(names))

            def mod(i):
                b, full = job("mod", i)
                eng.wait_ge(pe.doer(("mod_acc", i)), pe.at(("mod_acc", i)))
                for v, s in enumerate(mod_slots(i)):
                    sums = [mod_acc, mod_odd] if i < DVE_MODS else [mod_acc]
                    for j in range(4):
                        for n, acc in enumerate(sums):
                            mm = nc.tensor.matmul(b[:, 4 * v + j:4 * v + j + 1], acc[:, s, j * P:(j + 1) * P],
                                                  ones[:, 0:1], start=(n == 0), stop=(n == len(sums) - 1))
                mm.then_inc(tensor_done, pe.step(full))

            def norm_sum(name, src_n=KD, c=False, x=True):
                bx = job("ss", name, "x") if x else None
                bc = job("ss", name, "c") if c else None
                for k in range(src_n):
                    eng.wait_ge(scalar_done, pe.at(("sq", name, k)))
                    if x:
                        mm = nc.tensor.matmul(bx[0][:, :], ones[:, :], square[:, k % 2, 0:S],
                                              start=(k == 0), stop=(k == src_n - 1))
                        if k == src_n - 1 and c:
                            mm.then_inc(tensor_done, pe.step(bx[1]))
                    if c:
                        mm = nc.tensor.matmul(bc[0][:, 0:L], ones[:, :], square[:, k % 2, S:S + L],
                                              start=(k == 0), stop=(k == src_n - 1))
                    last = [("sq_used", name, k)]
                    if k == src_n - 1:
                        last.append(bc[1] if c else bx[1])
                    mm.then_inc(tensor_done, pe.step(last))

            eng.wait_ge(vraw_landed, pe.at("vraw"))
            eng.wait_ge(ident_landed, pe.at("ident"))
            for t in range(VT):
                b, full = job("vec", t)
                nc.tensor.transpose(b[:, 0:P], vraw[:, t, :], C("ident")).then_inc(tensor_done, pe.step(full))
            eng.wait_ge(xraw_landed, pe.at("xraw"))
            for k in range(KD):
                b, full = job("xT", k)
                for t in range(4):
                    mm = nc.tensor.transpose(b[:, t * P:(t + 1) * P], xraw[:, t, k * P:(k + 1) * P], C("ident"))
                mm.then_inc(tensor_done, pe.step(full))
            eng.wait_ge(craw_landed, pe.at("craw"))
            for k in range(KD):
                b, full = job("cT", k)
                for t in range(2):
                    mm = nc.tensor.transpose(b[:, t * P:(t + 1) * P], craw[:, t, k * P:(k + 1) * P], C("ident"))
                mm.then_inc(tensor_done, pe.step(full))
            eng.wait_ge(vector_done, pe.at("ones"))

            def moe(l):
                eng.wait_ge(rw_landed, pe.at(("rw", l)))
                b, full = job("route", l)
                for k in range(KD):
                    eng.wait_ge(vector_done, pe.at(("h", f"n2_{l}", k)))
                    mm = nc.tensor.matmul(b[0:36, :], rw[:, k, :], hT[:, k, 0:S], start=(k == 0), stop=(k == KD - 1))
                mm.then_inc(tensor_done, pe.step(full))
                def token_rows(t):
                    for half in range(2):
                        b, full = job("h_tok", l, t, half)
                        for j in range(4):
                            mm = nc.tensor.transpose(b[:, j * P:(j + 1) * P], hT[:, 4 * half + j, t * P:(t + 1) * P], C("ident"))
                        mm.then_inc(tensor_done, pe.step(full))
                token_rows(0)
                b, full = job("logits", l)
                eng.wait_ge(vector_done, pe.at(("logitT", l)))
                for t in range(4):
                    mm = nc.tensor.transpose(b[:, 36 * t:36 * t + 36], logitT[0:36, t * P:(t + 1) * P], C("ident")[0:36, 0:36])
                mm.then_inc(tensor_done, pe.step(full))
                for t in range(1, 4):
                    token_rows(t)
                b, full = job("picksT", l)
                eng.wait_ge(vector_done, pe.at(("picks", l)))
                for t in range(4):
                    mm = nc.tensor.transpose(b[0:32, t * P:(t + 1) * P], r4[:, t, 0:32], C("ident"))
                mm.then_inc(tensor_done, pe.step(full))
                b, full = job("ends", l)
                eng.wait_ge(vector_done, pe.at(("need", l)))
                nc.tensor.matmul(b[0:32, 0:1], R("prefix", 32), e_col[0:32, 1:2], start=True, stop=True).then_inc(tensor_done, pe.step(full))
                b, full = job("slots", l)
                eng.wait_ge(vector_done, pe.at(("slot_of", l)))
                for t in range(4):
                    mm = nc.tensor.transpose(b[:, 32 * t:32 * t + 32], slot_of[0:32, t * P:(t + 1) * P], C("ident")[0:32, 0:32])
                mm.then_inc(tensor_done, pe.step(full))
                b, full = job("experts", l)
                eng.wait_ge(vector_done, pe.at(("ended", l)))
                nc.tensor.matmul(b[0:1, 0:BLOCKS], ones[0:32, 0:1], block_t[0:32, 0, 0:BLOCKS], start=True, stop=True).then_inc(tensor_done, pe.step(full))
                b, full = job("pairs", l)
                eng.wait_ge(vector_done, pe.at(("in_lane", l)))
                eng.wait_ge(vector_done, pe.at(("in_block", l)))
                for q in range(8):
                    mm = nc.tensor.matmul(b[:, 0:BLOCKS], in_lane[:, q, :], in_block[:, q, :], start=(q == 0), stop=(q == 7))
                mm.then_inc(tensor_done, pe.step(full))
                loop = f"moe{l}"
                for hb in list(held):
                    eng.wait_ge(pe.doer(("free",) + held[hb]), pe.at(("free",) + held[hb]))

                def rows_T(l, i, b):
                    eng.wait_ge(rows_landed[b % AHEAD], rows_at(l, i, b))
                    for half in range(2):
                        bk, full = job(loop, "rowsT", b, half)
                        for j in range(4):
                            mm = nc.tensor.transpose(bk[:, j * P:(j + 1) * P],
                                                     rows[:, b % AHEAD, :].rearrange("p (f c) -> p c f", c=8)[:, 4 * half + j, :], C("ident"))
                        mm.then_inc(tensor_done, pe.step([full, (loop, "rows_used", b)]))

                with pe.loop(loop, BLOCKS // TURN) as i:
                    st["l"], st["in"] = 0, {}
                    slots.enter()
                    w2 = {}

                    def products(b):
                        bk, full = job(loop, "ab", b)
                        ws = [take(), take(), take()]
                        w2[b] = (ws[2][0].rearrange("p k n -> p (k n)"), ws[2][1])
                        eng.wait_ge(scalar_done, pe.at((loop, "rowsT", b)))
                        for m in range(2):
                            for k in range(KD):
                                mm = nc.tensor.matmul(bk[:, m * P:(m + 1) * P], ws[m][0][:, k, :], rowsT[:, b % 2, k, :],
                                                      start=(k == 0), stop=(k == KD - 1))
                            mm.then_inc(tensor_done, pe.step([ws[m][1]] + ([full] if m == 1 else [])))

                    rows_T(l, i, 0)
                    products(0)
                    rows_T(l, i, 1)
                    for b in range(TURN):
                        if b + 1 < TURN:
                            products(b + 1)
                        if b + 2 < TURN:
                            rows_T(l, i, b + 2)
                        eng.wait_ge(vector_done, pe.at((loop, "hid", b)))
                        for half in range(2):
                            bk, full = job(loop, "y", b, half)
                            nc.tensor.matmul(bk, hid[:, b % 2, :], w2[b][0][:, half * S:(half + 1) * S],
                                             start=True, stop=True).then_inc(tensor_done, pe.step([full] + ([w2[b][1]] if half else [])))
                assert st["l"] % BANKS == 0
                slots.leave(loop, BLOCKS // TURN)
                new[("lastjobs", loop)] = dict(st["in"])
                for i in range(16, 20) if l == 0 and stage_on(3) else ():
                    mod(i)
                for t in range(4):
                    eng.wait_ge(vector_done, pe.at(("y_tok", l, t)))
                for k in range(KD):
                    b, full = job("moe_y", l, k)
                    for t in range(4):
                        mm = nc.tensor.transpose(b[:, t * P:(t + 1) * P], y_tok[0][:, t, k * P:(k + 1) * P], C("ident"))
                    mm.then_inc(tensor_done, pe.step(full))

            norm_sum("n1_0")
            for i in range(4):
                mod(i)
            for c in range(16):
                linear(("inA", c), lambda k: hT[:, k, :], ready="n1_0" if c == 0 else None)
                if c in (4, 6, 8, 10, 12, 14):
                    mod(4 + (c - 4) // 2)
            for c in range(4):
                eng.wait_ge(scalar_done, pe.at(("vA", c)))
                b, full = job("vtA", c)
                for t in range(4):
                    mm = nc.tensor.transpose(b[:, t * P:(t + 1) * P], aT[:, 4 + c, t * P:(t + 1) * P], C("ident"))
                mm.then_inc(tensor_done, pe.step(full))

            def scoresA(h):
                po, c = 64 * (h % 2), h // 2
                eng.wait_ge(scalar_done, pe.at(("qkA", c)))
                eng.wait_ge(scalar_done, pe.at(("qkA", 4 + c)))
                for t in range(4):
                    b, full = job("scA", h, t)
                    n = P * (t + 1)
                    nc.tensor.matmul(b[:, 0:n], qk[po:po + 64, c, t * P:(t + 1) * P],
                                            qk[po:po + 64, 4 + c, 0:n], start=True, stop=True).then_inc(tensor_done, pe.step(full))

            for g in range(4):
                eng.wait_ge(vector_done, pe.at(("pooled", g)))
                eng.wait_ge(pool_w_landed, pe.at("pool_w"))
                b, full = job("poolA", g)
                nc.tensor.matmul(b, pool_w[:, g, :], up[:, g, 0:S], start=True, stop=True).then_inc(tensor_done, pe.step(full))
            scoresA(0)
            for h in range(8):
                if h + 1 < 8:
                    scoresA(h + 1)
                for t in range(4):
                    eng.wait_ge(vector_done, pe.at(("probA", h, t)))
                    b, full = job("ptA", h, t)
                    for q in range(t + 1):
                        mm = nc.tensor.transpose(b[:, q * P:(q + 1) * P], prob[h % 2][t][:, q * P:(q + 1) * P],
                                                 C("ident"))
                    mm.then_inc(tensor_done, pe.step(full))
                for t in range(4):
                    eng.wait_ge(scalar_done, pe.at(("vtokA", t)))
                    eng.wait_ge(scalar_done, pe.at(("ptcA", h, t)))
                b, full = job("oA", h)
                po = 64 * (h % 2)
                for t in range(4):
                    mm = nc.tensor.matmul(b[po:po + 64, t * P:S], vTok[:, t, 64 * h:64 * h + 64],
                                          probT[:, t, t * P:S], start=(t == 0), stop=(t == 3),
                                          skip_group_check=True)
                mm.then_inc(tensor_done, pe.step(full))
                for i in mods_at.get(("a", h), []):
                    mod(i)
            for k in range(4):
                eng.wait_ge(vector_done, pe.at(("aoutA", k)))
            for h in range(8):
                eng.wait_ge(scalar_done, pe.at(("oA_c", h)))
            for c in range(8):
                linear(("outA", c), lambda k: aT[:, k, :])
                for i in mods_at.get(("oA", c), []):
                    mod(i)
            if stage_on(2):
                norm_sum("n2_0")
                moe(0)
            if stage_on(3):
                norm_sum("n1_1")
                w = take()
                b, full = job("dt")
                for k in range(KD):
                    eng.wait_ge(vector_done, pe.at(("h", "n1_1", k)))
                    mm = nc.tensor.matmul(b[0:32, :], w[0][:, k, 0:32], hT[:, k, 0:S], start=(k == 0), stop=(k == 7))
                mm.then_inc(tensor_done, pe.step([full, w[1]]))
                for n in ("x0", "x1"):
                    linear(("ssm", 0, n), lambda k: hT[:, k, :])
                eng.wait_ge(vector_done, pe.at("acs"))
                b, full = job("dtTok")
                for q in range(2):
                    for t in range(4):
                        mm = nc.tensor.transpose(b[:, 64 * t + 32 * q:64 * t + 32 * q + 32],
                                                 dtT[0:32, q, t * P:(t + 1) * P], C("ident")[0:32, 0:32])
                mm.then_inc(tensor_done, pe.step(full))

                for g in range(8):
                    for n in ("B", "C", "z0", "z1"):
                        linear(("ssm", g, n), lambda k: hT[:, k, :])
                    for cc in range(2):
                        eng.wait_ge(vector_done, pe.at(("ssm_x", g, cc)))
                        b, full = job("xtok", g, cc)
                        for t in range(4):
                            mm = nc.tensor.transpose(b[:, t * P:(t + 1) * P], g_x[:, cc, t * P:(t + 1) * P], C("ident"))
                        mm.then_inc(tensor_done, pe.step(full))
                    eng.wait_ge(vector_done, pe.at(("ssm_bc", g, 0)))
                    eng.wait_ge(vector_done, pe.at(("ssm_bc", g, 1)))
                    for t in range(4):
                        b, full = job("cb", g, t)
                        nc.tensor.matmul(b[:, 0:S - t * P], g_bc[:, 0, t * P:(t + 1) * P], g_bc[:, 1, t * P:S],
                                                start=True, stop=True).then_inc(tensor_done, pe.step(full))
                    for cc in range(2):
                        if g < 7:
                            linear(("ssm", g + 1, f"x{cc}"), lambda k: hT[:, k, :])
                        b, full = job("y", g, cc)
                        for r in range(2):
                            h = 4 * g + 2 * cc + r
                            eng.wait_ge(vector_done, pe.at(("xdt", g, cc)))
                            eng.wait_ge(vector_done, pe.at(("seg", h)))
                            for t in range(4):
                                mm = nc.tensor.matmul(b[64 * r:64 * r + 64, t * P:S],
                                                      g_xdt[:, t, 64 * (2 * cc + r):64 * (2 * cc + r) + 64],
                                                      g_seg[:, h % 2, SOFF[t]:SOFF[t] + S - t * P],
                                                      start=(t == 0), stop=(t == 3), skip_group_check=True)
                            mm.then_inc(tensor_done, pe.step([("seg_used", h)] + ([full] if r == 1 else [])))
                            if r == 0:
                                for i in mods_at[("g", g)][cc:cc + 1]:
                                    mod(i)
                    norm_sum(("g", g), src_n=2)
                for c in range(8):
                    for k in range(16):
                        eng.wait_ge(vector_done, pe.at(("yn", k)))
                    linear(("outM", c), lambda k: yT[:, k, :], nk=16)
                    for i in mods_at.get(("o", c), []):
                        mod(i)
            if stage_on(4):
                norm_sum("n2_1")
                moe(1)
            if stage_on(5):
                norm_sum("fin1")
            if stage_on(6):
                eng.wait_ge(small_landed, pe.at("small"))
                for l in range(2 if upto > 6 else 1):
                    cx = l == 0
                    h_ = lambda k: hT[:, k, :]
                    norm_sum(("b2", l), c=True)

                    def rot_v_tok():
                        eng.wait_ge(rope_landed, pe.at(("rope", l)))
                        eng.wait_ge(scalar_done, pe.at(("k_raw", l)))
                        b, full = job("rot_k", l)
                        nc.tensor.matmul(b, rot_, k_raw[:, 0:S], start=True, stop=True).then_inc(tensor_done, pe.step(full))
                        eng.wait_ge(scalar_done, pe.at(("v_raw", l)))
                        for tag, t0, t1 in (("x", 0, 4), ("c", 4, 6)):
                            b, full = job("v_tok", l, tag)
                            for t in range(t0, t1):
                                mm = nc.tensor.transpose(b[:, (t - t0) * P:(t - t0 + 1) * P], v_raw[:, t * P:(t + 1) * P],
                                                         C("ident"))
                            mm.then_inc(tensor_done, pe.step(full))

                    def rot_q(c):
                        eng.wait_ge(scalar_done, pe.at(("q_raw", l, c)))
                        b, full = job("rot_q", l, c)
                        nc.tensor.matmul(b, rot_, q_[:, c, 0:S], start=True, stop=True).then_inc(tensor_done, pe.step(full))

                    for c in range(4):
                        if c == 2:
                            rot_v_tok()
                            rot_q(0)
                        if c == 3:
                            rot_q(1)
                        linear(("cf_g", l, c), h_, c=cx, ready=("b2", l) if c == 0 else None)
                        linear(("cf_a", l, c), h_, c=cx)
                        if c == 0:
                            for k in range(KD):
                                eng.wait_ge(vector_done, pe.at(("hc", ("b2", l), k)))
                        for n, q in ATT_AFTER[c]:
                            linear((n, l, q), h_, c=cx or n != "att_q")
                    rot_q(2)
                    rot_q(3)
                    eng.wait_ge(scalar_done, pe.at(("kd", l)))
                    eng.wait_ge(vector_done, pe.at(("roped", l)))

                    rounds = [(n, j) for n in x_tiles(l) for j in range(2)]

                    def att_scores(n, j):
                        for hh in range(4):
                            h = 4 * j + hh
                            po, c = 64 * (h % 2), h // 2
                            ql = q_[po:po + 64, c, n * P:(n + 1) * P]
                            kt = key_tiles(n)
                            if kt:
                                b, full = job("sl", l, h, n)
                                nc.tensor.matmul(b[:, 0:P * len(kt)], ql,
                                                        kd[po:po + 64, j, P * kt[0]:P * (kt[-1] + 1)],
                                                        start=True, stop=True).then_inc(tensor_done, pe.step(full))
                            b, full = job("sx", l, h, n)
                            nc.tensor.matmul(b[:, 0:L], ql, kd[po:po + 64, j, S:S + L], start=True, stop=True).then_inc(tensor_done, pe.step(full))

                    att_scores(*rounds[0])
                    for r, (n, j) in enumerate(rounds):
                        if r + 1 < len(rounds):
                            att_scores(*rounds[r + 1])
                        kt = key_tiles(n)
                        nl = len(kt)
                        for hh in range(4):
                            h = 4 * j + hh
                            eng.wait_ge(vector_done, pe.at(("pr2", l, n, h)))
                            pr = pr2[r % 2][:, hh, :]
                            for tag, t0, t1 in (("l", 0, nl), ("x", nl, nl + 2)):
                                if t1 == t0:
                                    continue
                                b, full = job("pt2", l, h, n, tag)
                                for t in range(t0, t1):
                                    mm = nc.tensor.transpose(b[:, (t - t0) * P:(t - t0 + 1) * P], pr[:, t * P:(t + 1) * P],
                                                             C("ident"))
                                mm.then_inc(tensor_done, pe.step(full))
                        for hh in range(4):
                            eng.wait_ge(scalar_done, pe.at(("ptc2", l, n, 4 * j + hh)))
                        b, full = job("av", l, n, j)
                        tiles = [(i, t) for i, t in enumerate(kt)] + [(3, 4), (4, 5)]
                        for i, (kb, t) in enumerate(tiles):
                            mm = nc.tensor.matmul(b[0:64, :], v_tok[:, t, 64 * j:64 * j + 64], pT2[:, kb, :],
                                                  start=(i == 0), stop=(i == len(tiles) - 1))
                        mm.then_inc(tensor_done, pe.step(full))
                    for c in range(4):
                        linear(("att_z", l, c), h_, c=cx)

                    def ret_proj(h):
                        linear(("ret_q", l, h), h_, c=cx)
                        linear(("ret_k", l, h), h_, c=True)
                        linear(("ret_v", l, h), h_, c=True)

                    def ret_tok(h):
                        eng.wait_ge(scalar_done, pe.at(("rv", l, h)))
                        for tag, t0, t1 in (("x", 0, 4), ("c", 4, 6)):
                            b, full = job("rv_tok", l, h, tag)
                            for t in range(t0, t1):
                                mm = nc.tensor.transpose(b[:, (t - t0) * P:(t - t0 + 1) * P], rv[:, t * P:(t + 1) * P],
                                                         C("ident"))
                            mm.then_inc(tensor_done, pe.step(full))

                    ret_proj(0)
                    ret_tok(0)
                    for h in range(4):
                        eng.wait_ge(scalar_done, pe.at(("rq", l, h)))
                        eng.wait_ge(scalar_done, pe.at(("rk", l, h)))
                        for t in range(6):
                            b, full = job("rs", l, h, t)
                            nc.tensor.matmul(b, rk[:, t * P:(t + 1) * P], rq[:, 0:S], start=True, stop=True).then_inc(tensor_done, pe.step(full))
                        linear(("ret_z", l, h), h_, c=cx)
                        if cx:
                            for t in range(2):
                                b, full = job("rs_c", l, h, t)
                                nc.tensor.matmul(b[:, 0:L], rk[:, (4 + t) * P:(5 + t) * P], rq[:, S:S + L],
                                                        start=True, stop=True).then_inc(tensor_done, pe.step(full))
                        eng.wait_ge(scalar_done, pe.at(("rv_tok", l, h)))
                        b, full = job("ro", l, h, "x")
                        for t in range(6):
                            eng.wait_ge(vector_done, pe.at(("rsc", l, h, t)))
                            mm = nc.tensor.matmul(b, rv_tok[:, t, :], rsc[:, t, :], start=(t == 0), stop=(t == 5))
                        mm.then_inc(tensor_done, pe.step(full))
                        if cx:
                            b, full = job("ro", l, h, "c")
                            eng.wait_ge(vector_done, pe.at(("rsc_c", l, h)))
                            for t in range(2):
                                mm = nc.tensor.matmul(b[:, 0:L], rv_tok[:, 4 + t, :], rsc_c[:, t, :], start=(t == 0),
                                                      stop=(t == 1))
                            mm.then_inc(tensor_done, pe.step(full))
                        if h < 3:
                            ret_proj(h + 1)
                        for tag, o, n in parts(cx):
                            b, full = job("rm", l, h, tag)
                            eng.wait_ge(scalar_done, pe.at(("ro_c", l, h, tag)))
                            nc.tensor.matmul(b[:, 0:n], ones[:, :], ro[:, o:o + n], start=True, stop=True).then_inc(tensor_done, pe.step(full))
                        if h < 3:
                            ret_tok(h + 1)
                        norm_sum(("ret", l, h), src_n=1, c=cx)
                    for c in range(4):
                        for n in ("sc_c", "sc_x", "sc_b", "sc_z"):
                            linear((n, l, c), h_, c=cx)
                    for tag, o, n in parts(cx, CO):
                        b, full = job("lm", l, tag)
                        for c in range(4):
                            eng.wait_ge(vector_done, pe.at(("cf_conv", l, c)))
                            mm = nc.tensor.matmul(b[:, 0:n], ones[:, :], br[:, 8 + c, o:o + n], start=(c == 0),
                                                  stop=(c == 3))
                        mm.then_inc(tensor_done, pe.step(full))
                    norm_sum(("ln", l), src_n=4, c=cx)
                    for c in range(4):
                        linear(("cf_z", l, c), h_, c=cx)
                    for i in range(4):
                        for c in range(4):
                            eng.wait_ge(vector_done, pe.at(("branch", l, 4 * i + c)))
                    for c in range(8):
                        for i in range(4):
                            linear(("gate", l, c, i), h_, c=cx)
                            linear(("by", l, c, i), lambda k: br[:, 4 * i + k, :], nk=4, c=cx, co=CO)
                    for c in range(8):
                        eng.wait_ge(vector_done, pe.at(("mrg", l, c)))
                    for c in range(8):
                        linear(("out2", l, c), lambda k: mrg[:, k, :], c=cx)
                if upto > 7:
                    norm_sum("fin2")
            if upto <= 7:
                eng.wait_ge(vector_done, pe.at("x_final"))
            for t in range(4):
                for hh in range(2):
                    b, full = job("res", t, hh)
                    for k in range(4):
                        if t == 0 and upto > 7:
                            eng.wait_ge(vector_done, pe.at(("x_out", 4 * hh + k)))
                        mm = nc.tensor.transpose(b[:, k * P:(k + 1) * P], xT[:, 4 * hh + k, t * P:(t + 1) * P], C("ident"))
                    mm.then_inc(tensor_done, pe.step(full))

        @block.sync
        def _(eng):
            sp = Count(eng, "sync_none", sems, old, new)
            slots = Ring(sp)
            outstanding = {}

            def put(src, dst=None):
                slot, use, before, lag = slots.next()
                if before is not None:
                    eng.wait_ge(tensor_done, sp.at(("freed",) + before, lag=lag))
                to = ring[:, slot] if dst is None else dst(ring[:, slot])
                eng.dma_start(to, src).then_inc(weights_landed[slot], sp.landing(f"weights_{slot}", ("landed",) + use))

            eng.dma_start(const[:, 0:P], a["consts"][:, 0:P]).then_inc(ident_landed, sp.landing("ident_in", "ident"))
            eng.dma_start(vraw, a["vecs"].rearrange("(t p) n -> p t n", p=P)).then_inc(vraw_landed, sp.landing("vraw", "vraw"))
            eng.dma_start(xraw, a["x"].rearrange("b (t p) n -> p (b t) n", p=P)).then_inc(xraw_landed, sp.landing("xraw", "xraw"))
            eng.dma_start(craw, a["ctx_2"].rearrange("b (t p) n -> p (b t) n", p=P)).then_inc(craw_landed, sp.landing("craw", "craw"))
            w = a["mix_w_in"][0]
            for c in IN_A[0:4]:
                put(block8(w, P * c))
            eng.dma_start(const[:, P:], a["consts"][:, P:CONST1_W]).then_inc(const_landed, sp.landing("const", "const"))
            for c in IN_A[4:]:
                put(block8(w, P * c))
            for c in range(8):
                put(block8(a["mix_w_out"][0], P * c))

            def moe(l):
                loop = f"moe{l}"
                for b in range(RING):
                    eng.wait_ge(tensor_done, sp.at(("freed",) + (slots._flat(slots.n - 1 - b))))
                eng.wait_ge(vector_done, sp.at(("expert_u", l)))
                w1 = a["moe_w1"][l].rearrange("e (p c) f -> p e (c f)", c=8)
                w3 = a["moe_w3"][l].rearrange("e (p c) f -> p e (c f)", c=8)
                w2 = a["moe_w2"][l].rearrange("e f n -> f e n")
                flat = lambda s: s.rearrange("p k n -> p (k n)").unsqueeze(1)
                with sp.loop(loop, BLOCKS // TURN) as i:
                    slots.enter()
                    for b in range(TURN):
                        e = eng.value_load(expert_u[0:1, bass.ds(i * TURN + b, 1)], min_val=0, max_val=EXPERTS - 1)
                        put(w1[:, bass.ds(e, 1), :], dst=flat)
                        put(w3[:, bass.ds(e, 1), :], dst=flat)
                        put(w2[:, bass.ds(e, 1), :], dst=flat)
                slots.leave(loop, BLOCKS // TURN)
                for s_ in range(AHEAD):
                    eng.wait_ge(y_stored[s_], 16 * (l + 1) * (BLOCKS // AHEAD + 1))
                    eng.wait_ge(rows_landed[s_], 16 * (l + 1) * (BLOCKS // AHEAD + 1))
                for t in range(4):
                    for c in range(2):
                        r0 = S * c + P * t
                        eng.dma_start(y_tok[c][:, t, :], y_dram[l][r0:r0 + P, :]).then_inc(y_back_landed[t], 16)

            if stage_on(2):
                moe(0)
            if stage_on(3):
                w = a["ssm_w_in"][0]
                put(block8(w, 6144, 32), dst=lambda s: s[:, :, 0:32])
                for g in range(8):
                    for c0 in ((2048, 2048 + P) if g == 0 else ()) + (4096 + P * g, 5120 + P * g, 256 * g, 256 * g + P):
                        put(block8(w, c0))
                    if g < 7:
                        for c0 in (2048 + 256 * (g + 1), 2048 + 256 * (g + 1) + P):
                            put(block8(w, c0))
                    for r in range(4):
                        h = 4 * g + r
                        if h == 0:
                            eng.wait_ge(acs_out_landed, sp.at("acs_out"))
                        if h >= 2:
                            eng.wait_ge(vector_done, sp.at(("acs_used", h - 2)))
                        eng.dma_start(acs_b[:, h % 2, :], acs_dram[h:h + 1, :].broadcast_to([P, S])).then_inc(acs_row_landed[h % 2], sp.landing(f"acs_row_{h % 2}", ("acs_row", h)))
                for c in range(8):
                    for k2 in range(2):
                        put(a["ssm_w_out"][0][1024 * k2:1024 * (k2 + 1), c * P:(c + 1) * P]
                            .rearrange("(k p) n -> p k n", p=P))
            if stage_on(4):
                moe(1)
            if stage_on(6):
                for l in range(2 if upto > 6 else 1):
                    w = a["w_in_2"][l]
                    for n, c in in_blocks(l):
                        put(block8(w, COL[n] + P * c))
                    for c in range(8):
                        for i in range(4):
                            put(block8(w, COL["gates"] + D * i + P * c))
                            put(a["w_branch_2"][l][i][:, c * P:(c + 1) * P].rearrange("(k p) n -> p k n", p=P),
                                dst=lambda s: s[:, 0:4, :])
                    for c in range(8):
                        put(block8(a["w_out_2"][l], c * P))
            for t in range(4):
                eng.wait_ge(scalar_done, sp.at(("res_c", t)))
                eng.dma_start(out[0, t * P:(t + 1) * P, :], hT_res(t)).then_inc(result_landed, sp.landing("result", ("result", t)))
            eng.wait_ge(result_landed, sp.at(("result", 3)))

        @block.scalar
        def _(eng):
            ac = Count(eng, "scalar_done", sems, old, new)

            def act(out_, in_, f, bias=0.0, scale=1.0, **kw):
                if bias == 0.0 and f != ACT.Copy:
                    bias = col("zero", rows=out_.shape[0]) if out_.start_partition() == 0 else bias0(out_)
                return nc.scalar.activation(out_, in_, f, bias=bias, scale=scale, **kw)

            def bias0(o):
                p = o.start_partition()
                c0 = col_at["zero"][0]
                return cols[p:p + o.shape[0], c0:c0 + 1]

            def copy(out_, in_):
                return nc.scalar.activation(out_, in_, ACT.Copy)

            def evac(job_, out_, n=S, rows=None, name=None):
                j = jobname(*job_)
                eng.wait_ge(tensor_done, ac.at(("full",) + j))
                b = bank(j)
                src = b[:, 0:n] if rows is None else b[rows[0]:rows[1], 0:n]
                copy(out_, src).then_inc(scalar_done, ac.step([("free",) + j] + ([name] if name else [])))

            def tanh_half(job_, out_, n=S, name=None):
                j = jobname(*job_)
                eng.wait_ge(tensor_done, ac.at(("full",) + j))
                act(out_, bank(j)[:, 0:n], ACT.Tanh, scale=0.5).then_inc(scalar_done, ac.step(name))

            def squares(name, src, wait, n=KD, ctxs=None):
                for k in range(n):
                    wait(k)
                    prev = sq_state["hist"]
                    if len(prev) >= 2:
                        eng.wait_ge(tensor_done, ac.at(("sq_used",) + prev[-2]))
                    if n == 1 and prev:
                        eng.wait_ge(tensor_done, ac.at(("sq_used",) + prev[-1]))
                    prev.append((name, k))
                    if ctxs is not None:
                        act(square[:, k % 2, S:S + L], ctxs(k), ACT.Square).then_inc(scalar_done, ac.step())
                    act(square[:, k % 2, 0:S], src(k), ACT.Square).then_inc(scalar_done, ac.step(("sq", name, k)))

            sq_state = {"hist": []}

            def inv_root(name, div, eps, x=True, c=False):
                eng.wait_ge(vector_done, ac.at(("rstd_used", ac_prev["r"]))) if ac_prev["r"] else None
                ac_prev["r"] = name
                parts = ([("x", 0, S)] if x else []) + ([("c", S, L)] if c else [])
                for tag, o, n in parts:
                    j = jobname("ss", name, tag)
                    eng.wait_ge(tensor_done, ac.at(("full",) + j))
                    act(rstd[:, o:o + n], bank(j)[:, 0:n], ACT.Ln, bias=eps, scale=1.0 / div).then_inc(scalar_done, ac.step(("free",) + j))
                eng.wait_ge(scalar_done, ac.own())
                for tag, o, n in parts:
                    act(rstd[:, o:o + n], rstd[:, o:o + n], ACT.Exp, scale=-0.5).then_inc(scalar_done, ac.step(("rstd", name, tag)))

            ac_prev = {"r": None}
            pad_prev = [None]

            eng.dma_start(pool_w, a["pool_w"][0].rearrange("g c d -> c g d")).then_inc(pool_w_landed, ac.landing("pool_w", "pool_w"))
            eng.dma_start(col("dtb", rows=32), a["ssm_dt_bias"].rearrange("o h -> h o")).then_inc(dtb_landed, ac.landing("dtb", "dtb"))
            eng.dma_start(col("negA", rows=32), a["ssm_A_log"].rearrange("o h -> h o")).then_inc(A_log_landed, ac.landing("A_log", "A_log"))

            def bias_load(h):
                if h >= 2:
                    eng.wait_ge(vector_done, ac.at(("biasA_used", h - 2)))
                else:
                    eng.wait_ge(vector_done, ac.at("bias_mask"))
                for lo, n in ((0, S - 64), (64, S)):
                    eng.dma_start(bias_s[lo:lo + 64, h % 2, 0:n], a["rel_tiles"][h, lo:lo + 64, 0:n]).then_inc(bias_landed[h % 2], ac.landing(f"bias_{h % 2}", ("biasA", h)))

            def router_load(l):
                eng.dma_start(rw, a["w_router"][l].rearrange("(k p) n -> p k n", p=P)).then_inc(rw_landed, ac.landing("rw", ("rw", l)))
                eng.dma_start(route_c, a["consts"][:, CONST_W - ROUTE_W:CONST_W]).then_inc(route_c_landed, 16)
                eng.dma_start(rb[0:36, :], a["small"][0:1, 36 * l:36 * l + 36].rearrange("o n -> n o")).then_inc(rb_landed, ac.landing("rb", ("rb", l)))

            eng.wait_ge(vector_done, ac.at("cols0"))
            for t in range(VT):
                evac(("vec", t), vec[:, t * P:(t + 1) * P], n=P, name=("vec", t))
            eng.wait_ge(scalar_done, ac.own())
            for v, nm in enumerate(("c", "c_2", "c_ctx_2")):
                act(col("ctmp", 8 * v, 8), V(nm, 0, 8), ACT.Tanh, scale=0.5).then_inc(scalar_done, ac.step(("tanh_c", v)))
            for k in range(KD):
                evac(("xT", k), xT[:, k, :], name=("xT", k))
            for k in range(KD):
                evac(("cT", k), cT[:, k, :], n=L, name=("cT", k))
            eng.wait_ge(scalar_done, ac.own())

            squares("n1_0", lambda k: xT[:, k, :], lambda k: None)
            inv_root("n1_0", D, col("eps"))

            for c in IN_A:
                c4 = c % 4
                if c < 4:
                    eng.wait_ge(vector_done, ac.at("up_zero"))
                    evac(("inA", IN_A.index(c), "x"), up[:, c4, 16:16 + S], name=("uA", c4))
                elif c < 12:
                    evac(("inA", IN_A.index(c), "x"), qk[:, c - 4, :], name=("qkA", c - 4))
                else:
                    evac(("inA", IN_A.index(c), "x"), aT[:, 4 + c4, :], name=("vA", c4))
            for c in range(4):
                j = jobname("vtA", c)
                eng.wait_ge(tensor_done, ac.at(("full",) + j))
                copy(vTok[:, :, c * P:(c + 1) * P], bank(j).rearrange("p (t n) -> p t n", t=4)).then_inc(scalar_done, ac.step([("free",) + j] + [("vtokA", c)]))
            bias_load(0)
            bias_load(1)

            def soft(h):
                for t in range(4):
                    eng.wait_ge(vector_done, ac.at(("smA", h, t)))
                    n = P * (t + 1)
                    pr = prob[h % 2][t][:, 0:n]
                    act(pr, pr, ACT.Exp, bias=col("stat", 8 * (h % 2) + t),
                        accum_out=col("stat", 16 + 8 * (h % 2) + t)).then_inc(scalar_done, ac.step(("expA", h, t)))
                if h + 2 < 8:
                    bias_load(h + 2)
            soft(0)
            for h in range(8):
                for t in range(4):
                    j = jobname("ptA", h, t)
                    eng.wait_ge(tensor_done, ac.at(("full",) + j))
                    if h >= 1:
                        eng.wait_ge(tensor_done, ac.at(("full",) + jobname("oA", h - 1)))
                    copy(probT[:, 0:t + 1, t * P:(t + 1) * P],
                         bank(j)[:, 0:P * (t + 1)].rearrange("p (q n) -> p q n", n=P)).then_inc(scalar_done, ac.step([("free",) + j, ("ptcA", h, t)]))
                if h + 1 < 8:
                    soft(h + 1)
                po = 64 * (h % 2)
                evac(("oA", h), aT[po:po + 64, 4 + h // 2, :], rows=(po, po + 64), name=("oA_c", h))
            if stage_on(2):
                router_load(0)
                squares("n2_0", lambda k: xT[:, k, :], lambda k: eng.wait_ge(vector_done, ac.at(("xA", k))))
                inv_root("n2_0", D, col("eps"))

            def moe(l):
                for t in range(4):
                    for half in range(2):
                        evac(("h_tok", l, t, half), h_tok[:, t, half * S:(half + 1) * S])
                    eng.wait_ge(scalar_done, ac.own())
                    eng.dma_start(h_dram[l][t * P:(t + 1) * P, :], h_tok[:, t, :]).then_inc(h_rows_stored, 16)
                eng.wait_ge(vector_done, ac.at(("top2", l)))
                act(r1[:, :, 0:4], r1[:, :, 0:4], ACT.Exp).then_inc(scalar_done, ac.step(("eg", l)))
                act(rs_[:, 4, :], rs_[:, 4, :], ACT.Exp).then_inc(scalar_done, ac.step(("er", l)))
                loop = f"moe{l}"

                def rows_copy(b):
                    for half in range(2):
                        j = jobname(loop, "rowsT", b, half)
                        eng.wait_ge(tensor_done, ac.at(("full",) + j))
                        copy(rowsT[:, b % 2, 4 * half:4 * half + 4, :].rearrange("p k n -> p (k n)"), bank(j)).then_inc(scalar_done, ac.step([("free",) + j, (loop, "rowsT", b)]))

                with ac.loop(loop, BLOCKS // TURN):
                    rows_copy(0)
                    tanh_half((loop, "ab", 0), e_t[:, 0, :], n=P, name=(loop, "t", 0))
                    rows_copy(1)
                    for b in range(1, TURN):
                        tanh_half((loop, "ab", b), e_t[:, b % 2, :], n=P, name=(loop, "t", b))
                        if b + 1 < TURN:
                            rows_copy(b + 1)

            if stage_on(2):
                moe(0)
            if stage_on(3):
                squares("n1_1", lambda k: xT[:, k, :], lambda k: eng.wait_ge(vector_done, ac.at(("x", "moe0", k))))
                inv_root("n1_1", D, col("eps"))
                eng.wait_ge(A_log_landed, ac.at("A_log"))
                act(col("negA", rows=32), col("negA", rows=32), ACT.Exp).then_inc(scalar_done, ac.step("expA_log"))
                eng.wait_ge(vector_done, ac.at("dt_v"))
                act(dtT[0:32, 1, :], dtT[0:32, 0, :], ACT.Abs).then_inc(scalar_done, ac.step())
                eng.wait_ge(scalar_done, ac.own())
                act(dtT[0:32, 1, :], dtT[0:32, 1, :], ACT.Exp, scale=-1.0).then_inc(scalar_done, ac.step())
                eng.wait_ge(scalar_done, ac.own())
                act(dtT[0:32, 1, :], dtT[0:32, 1, :], ACT.Ln, bias=col("one", rows=32)).then_inc(scalar_done, ac.step("dt_ln"))
                eng.wait_ge(vector_done, ac.at("acs"))
                eng.dma_start(acs_dram, dtT[0:32, 1, :]).then_inc(acs_out_landed, ac.landing("acs_out", "acs_out"))
                for g in range(8):
                    for qi, n in enumerate(("x0", "x1", "B", "C")):
                        eng.wait_ge(vector_done, ac.at(("pad_used",) + (pad_prev[0],))) if pad_prev[0] else None
                        pad_prev[0] = (g, qi)
                        evac(("ssm", g, n, "x"), g_pad[:, 3:3 + S], name=("pad", g, qi))
                        eng.wait_ge(vector_done, ac.at(("conv", g, qi)))
                        dst = [g_x[:, 0, :], g_x[:, 1, :], g_bc[:, 0, :], g_bc[:, 1, :]][qi]
                        act(g_t, dst, ACT.Tanh, scale=0.5).then_inc(scalar_done, ac.step(("conv_t", g, qi)))
                    for zz in range(2):
                        if g >= 1:
                            eng.wait_ge(vector_done, ac.at(("yz", g - 1, zz)))
                        j = jobname("ssm", g, f"z{zz}", "x")
                        eng.wait_ge(tensor_done, ac.at(("full",) + j))
                        act(g_z[:, zz, :], bank(j), ACT.Tanh, scale=0.5).then_inc(scalar_done, ac.step(("zt", g, zz)))
                    for t in range(4):
                        j = jobname("cb", g, t)
                        eng.wait_ge(tensor_done, ac.at(("full",) + j))
                        if g >= 1:
                            eng.wait_ge(vector_done, ac.at(("seg", 4 * g - 1)))
                        act(g_cb[:, SOFF[t]:SOFF[t] + S - t * P], bank(j)[:, 0:S - t * P], ACT.Identity, scale=0.25).then_inc(scalar_done, ac.step([("free",) + j, ("cb_c", g)]))
                    for r in range(4):
                        h = 4 * g + r
                        eng.wait_ge(vector_done, ac.at(("arg", h)))
                        act(g_seg[:, h % 2, :], g_seg[:, h % 2, :], ACT.Exp).then_inc(scalar_done, ac.step(("seg_e", h)))
                    squares(("g", g), lambda k: yT[:, 2 * g + k, :], lambda k: eng.wait_ge(vector_done, ac.at(("yz", g, k))), n=2)
                    inv_root(("g", g), 4 * 256, col("eps"))
            if stage_on(4):
                eng.wait_ge(vector_done, ac.at(("yn", 15)))
                router_load(1)
                squares("n2_1", lambda k: xT[:, k, :], lambda k: eng.wait_ge(vector_done, ac.at(("xM", k))))
                inv_root("n2_1", D, col("eps"))
                moe(1)
            if stage_on(5):
                squares("fin1", lambda k: xT[:, k, :], lambda k: eng.wait_ge(vector_done, ac.at(("x", "moe1", k))))
                inv_root("fin1", D, col("eps"))
            if stage_on(6):
                eng.dma_start(col("small", 0, 32), a["small"][0:1, 72:104].broadcast_to([P, 32])).then_inc(small_landed, ac.landing("small", "small"))
                eng.wait_ge(small_landed, ac.at("small"))
                act(col("lgt", 0, 16), col("small", 0, 16), ACT.Abs).then_inc(scalar_done, ac.step())
                eng.wait_ge(scalar_done, ac.own())
                act(col("lgt", 0, 16), col("lgt", 0, 16), ACT.Exp, scale=-1.0).then_inc(scalar_done, ac.step())
                eng.wait_ge(scalar_done, ac.own())
                act(col("lgt", 0, 16), col("lgt", 0, 16), ACT.Ln, bias=col("one")).then_inc(scalar_done, ac.step("lgt"))
                zn = {"n": 0}

                def z_tanh(name, l, c, cx):
                    n = zn["n"]
                    zn["n"] += 1
                    if n >= 2:
                        eng.wait_ge(vector_done, ac.at(("zt_used", n - 2)))
                    for tag, o, w in parts(cx):
                        j = jobname(name, l, c, tag)
                        eng.wait_ge(tensor_done, ac.at(("full",) + j))
                        act(zt[:, n % 2, o:o + w], bank(j)[:, 0:w], ACT.Tanh, scale=0.5).then_inc(scalar_done, ac.step(("zt", n, tag)))

                for l in range(2 if upto > 6 else 1):
                    cx = l == 0
                    squares(("b2", l), lambda k: xT[:, k, :], lambda k: eng.wait_ge(vector_done, ac.at(("x_new", l, k))), ctxs=lambda k: cT[:, k, :])
                    inv_root(("b2", l), D, col("eps"), c=True)
                    o0 = CONST["rot"][0]
                    eng.wait_ge(vector_done, ac.at(("x_in", l)))
                    eng.dma_start(rope, a["consts"][:, o0:o0 + P + 2 * S]).then_inc(rope_landed, ac.landing("rope", ("rope", l)))
                    for c in range(4):
                        if c == 2:
                            for tag, t0, t1 in (("x", 0, 4), ("c", 4, 6)):
                                evac(("v_tok", l, tag), v_tok[:, t0:t1, :].rearrange("p a b -> p (a b)"), n=P * (t1 - t0),
                                     name=("v_tok", l, tag))
                        eng.wait_ge(vector_done, ac.at(("cu_free", l, c)))
                        for tag, o, w in parts(cx, CO):
                            j = jobname("cf_g", l, c, tag)
                            eng.wait_ge(tensor_done, ac.at(("full",) + j))
                            act(cu[:, c % 2, 15 + o:15 + o + w], bank(j)[:, 0:w], ACT.Tanh, scale=0.5).then_inc(scalar_done, ac.step([("free",) + j, ("cf_t", l, c, tag)]))
                        for n, q in ATT_AFTER[c]:
                            to, name = {"att_k": (k_raw, ("k_raw", l)), "att_v": (v_raw, ("v_raw", l)),
                                        "att_q": (q_[:, q, :], ("q_raw", l, q))}[n]
                            for tag, o, w in parts(cx or n != "att_q"):
                                evac((n, l, q, tag), to[:, o:o + w], n=w, name=name)
                    eng.wait_ge(vector_done, ac.at(("k_roped", l)))
                    for j in range(2):
                        for half in range(2):
                            copy(kd[64 * half:64 * half + 64, j, :], k_raw[64 * j:64 * j + 64, :]).then_inc(scalar_done, ac.step(("kd", l)))

                    def att_exp(r, n, j):
                        q = r % 2
                        for hh in range(4):
                            eng.wait_ge(vector_done, ac.at(("nm2", l, n, j)))
                            w = P * len(key_tiles(n)) + L
                            pr = pr2[q][:, hh, 0:w]
                            act(pr, pr, ACT.Exp, bias=col("stat", 32 * q + 4 + hh),
                                accum_out=col("stat", 32 * q + 8 + hh)).then_inc(scalar_done, ac.step(("exp2", l, n, 4 * j + hh)))
                        act(col("stat", 32 * q + 12, 4), col("stat", 32 * q + 12, 4), ACT.Exp).then_inc(scalar_done, ac.step(("es2", l, n, j)))
                    rounds = [(n, j) for n in x_tiles(l) for j in range(2)]
                    att_exp(0, *rounds[0])
                    for r, (n, j) in enumerate(rounds):
                        nl = len(key_tiles(n))
                        if r >= 1:
                            eng.wait_ge(tensor_done, ac.at(("full",) + jobname("av", l, *rounds[r - 1])))
                        else:
                            eng.wait_ge(scalar_done, ac.at(("v_tok", l, "c")))
                        for hh in range(4):
                            h = 4 * j + hh
                            for tag, kb, m in (("l", 0, nl), ("x", 3, 2)):
                                if m == 0:
                                    continue
                                jn = jobname("pt2", l, h, n, tag)
                                eng.wait_ge(tensor_done, ac.at(("full",) + jn))
                                copy(pT2[:, kb:kb + m, P * hh:P * (hh + 1)],
                                     bank(jn)[:, 0:P * m].rearrange("p (a b) -> p a b", b=P)).then_inc(scalar_done, ac.step([("free",) + jn, ("ptc2", l, n, h)]))
                        if r + 1 < len(rounds):
                            att_exp(r + 1, *rounds[r + 1])
                        jn = jobname("av", l, n, j)
                        eng.wait_ge(tensor_done, ac.at(("full",) + jn))
                        bv = bank(jn)[0:64, :].rearrange("p (a b n) -> p a b n", a=2, b=2)
                        for half in range(2):
                            copy(br[64 * half:64 * half + 64, 12 + 2 * j:14 + 2 * j, tile_at(n):tile_at(n) + P],
                                 bv[:, :, half, :]).then_inc(scalar_done, ac.step([("free",) + jn, ("att_o", l)]))
                    eng.dma_start(tabs, a["consts"][:, CONST["dplus"][0]:CONST_W - ROUTE_W]).then_inc(tabs_landed, ac.landing("tabs", ("tabs", l)))
                    for c in range(4):
                        z_tanh("att_z", l, c, cx)

                    def ret_in(h):
                        if h == 0:
                            eng.wait_ge(vector_done, ac.at(("att_done", l)))
                        else:
                            eng.wait_ge(tensor_done, ac.at(("full",) + jobname("ro", l, h - 1, "c" if cx else "x")))
                        for n, dst, cc in (("q", rq, cx), ("k", rk, True), ("v", rv, True)):
                            for tag, o, w in parts(cc):
                                evac((f"ret_{n}", l, h, tag), dst[:, o:o + w], n=w, name=(f"r{n}", l, h))

                    def ret_tok_c(h):
                        for tag, t0, t1 in (("x", 0, 4), ("c", 4, 6)):
                            evac(("rv_tok", l, h, tag), rv_tok[:, t0:t1, :].rearrange("p a b -> p (a b)"),
                                 n=P * (t1 - t0), name=("rv_tok", l, h))

                    def ret_decay(h):
                        lf, lb = 8 * l + h, 8 * l + 4 + h
                        if h == 0:
                            eng.wait_ge(tabs_landed, ac.at(("tabs", l)))
                            eng.wait_ge(vector_done, ac.at(("att_done", l)))
                        else:
                            eng.wait_ge(vector_done, ac.at(("rctx_used", l, h - 1)))
                        for b_ in range(2):
                            act(rctx[:, b_, :], to_end, ACT.Exp, scale=col("lg", lf),
                                bias=col("lgm", lf) if b_ else col("zero")).then_inc(scalar_done, ac.step())
                            act(rtmp[:, b_, :], to_start, ACT.Exp, scale=col("lg", lb),
                                bias=col("lgp", lb) if b_ else col("zero")).then_inc(scalar_done, ac.step(("rtmp", l, h)))
                        eng.wait_ge(vector_done, ac.at(("darg", l, h)))
                        act(dstrip, dstrip, ACT.Exp).then_inc(scalar_done, ac.step(("dstrip", l, h)))
                    ret_decay(0)
                    ret_in(0)
                    ret_tok_c(0)
                    for h in range(4):
                        z_tanh("ret_z", l, h, cx)
                        for tag, o, w in parts(cx):
                            if h >= 1:
                                eng.wait_ge(vector_done, ac.at(("rnd", l, h - 1, tag)))
                            evac(("ro", l, h, tag), ro[:, o:o + w], n=w, name=("ro_c", l, h, tag))
                        if h < 3:
                            ret_in(h + 1)
                        squares(("ret", l, h), lambda k: rnd[:, 0:S], lambda k: eng.wait_ge(vector_done, ac.at(("rnd", l, h, "c" if cx else "x"))),
                                n=1, ctxs=(lambda k: rnd[:, S:S + L]) if cx else None)
                        if h < 3:
                            ret_tok_c(h + 1)
                        inv_root(("ret", l, h), P, col("eps"), c=cx)
                        if h < 3:
                            ret_decay(h + 1)
                    for c in range(4):
                        if c == 0:
                            eng.wait_ge(vector_done, ac.at(("ret_done", l)))
                        else:
                            eng.wait_ge(vector_done, ac.at(("sc_c_used", l, c - 1)))
                        for tag, o, w in parts(cx):
                            evac(("sc_c", l, c, tag), sc_c[:, c % 2, o:o + w], n=w, name=("sc_cc", l, c, tag))
                        z_tanh("sc_z", l, c, cx)
                    squares(("ln", l), lambda k: br[:, 8 + k, 0:S], lambda k: eng.wait_ge(vector_done, ac.at(("cf_nd", l, k))), n=4,
                            ctxs=(lambda k: br[:, 8 + k, CO:CO + L]) if cx else None)
                    inv_root(("ln", l), 4 * P, col("eps"), c=cx)
                    for c in range(4):
                        eng.wait_ge(vector_done, ac.at(("cf_v", l, c)))
                        if c >= 2:
                            eng.wait_ge(vector_done, ac.at(("cf_y", l, c - 2)))
                        w = CW if cx else S
                        act(cf_t[:, c % 2, 0:w], br[:, 8 + c, 0:w], ACT.Tanh, scale=-0.5, bias=col("hlb", 4 * l + c)).then_inc(scalar_done, ac.step(("cf_tt", l, c)))
                    for c in range(4):
                        z_tanh("cf_z", l, c, cx)
                    for c in range(8):
                        for i in range(4):
                            m = 4 * c + i
                            if m >= 4:
                                eng.wait_ge(vector_done, ac.at(("mt_used", l, m - 4)))
                            else:
                                eng.wait_ge(vector_done, ac.at(("cf_done", l)))
                            for tag, o, w in parts(cx):
                                j = jobname("gate", l, c, i, tag)
                                eng.wait_ge(tensor_done, ac.at(("full",) + j))
                                act(mt[:, m % 4, o:o + w], bank(j)[:, 0:w], ACT.Tanh, scale=0.5).then_inc(scalar_done, ac.step([("free",) + j, ("mt", l, m, tag)]))
                if upto > 7:
                    squares("fin2", lambda k: xT[:, k, :], lambda k: eng.wait_ge(vector_done, ac.at(("x_new", 2, k))))
                    inv_root("fin2", D, col("eps"))
            for t in range(4):
                for hh in range(2):
                    evac(("res", t, hh), hT_res(t)[:, hh * S:(hh + 1) * S], name=("res_c", t))

        @block.vector
        def _(eng):
            ve = Count(eng, "vector_done", sems, old, new)
            v = nc.vector

            def ts(out_, in0, s1, s2=None, op0=ALU.mult, op1=None):
                if op1 is None:
                    return v.tensor_scalar(out_, in0, s1, None, op0)
                return v.tensor_scalar(out_, in0, s1, s2, op0, op1)

            def tt(out_, in0, in1, op):
                return v.tensor_tensor(out_, in0, in1, op)

            def stt(out_, in0, s, in1, op0=ALU.mult, op1=ALU.mult):
                return v.scalar_tensor_tensor(out_, in0, s, in1, op0, op1)

            def red(out_, in_, op, negate=False):
                return v.tensor_reduce(out_, in_, AX, op, negate=negate)

            def full(*name):
                j = jobname(*name)
                eng.wait_ge(tensor_done, ve.at(("full",) + j))
                return bank(j), ("free",) + j

            def mod(i):
                b, free = full("mod", i)
                if i < 24:
                    tt(col("mod", 4 * i, 4), b[:, 0:4], V("ada_b", 4 * i, 4), ALU.add).then_inc(vector_done, ve.step([free, ("mod", i)]))
                else:
                    q = i - 24
                    l, bb = q // 6, q % 6
                    tt(col("mod2", 48 * l + 4 * bb, 4), b[:, 0:4], V("b_mod_2", 4 * q, 4), ALU.add).then_inc(vector_done, ve.step())
                    tt(col("mod2", 48 * l + 24 + 4 * bb, 4), b[:, 4:8], V("b_mod_2", 4 * q, 4), ALU.add).then_inc(vector_done, ve.step([free, ("mod", i)]))

            def modulated(name, w, scale, shift, src, ctx_part=None):
                eng.wait_ge(vector_done, ve.own())
                stt(col("A", 0, 8), scale, 1.0, w, ALU.add, ALU.mult).then_inc(vector_done, ve.step())
                if ctx_part:
                    stt(col("A2", 0, 8), ctx_part[0], 1.0, w, ALU.add, ALU.mult).then_inc(vector_done, ve.step())
                eng.wait_ge(vector_done, ve.own())
                eng.wait_ge(scalar_done, ve.at(("rstd", name, "x")))
                for k in range(KD + 1):
                    if k < KD:
                        stt(hT[:, k, 0:S], src(k), col("A", k), rstd[:, 0:S]).then_inc(vector_done, ve.step([("hs", name, k)] + ([] if ctx_part else [("rstd_used", name)])))
                    if k >= 1:
                        eng.wait_ge(vector_done, ve.at(("hs", name, k - 1)))
                        ts(hT[:, k - 1, 0:S], hT[:, k - 1, 0:S], shift(k - 1), op0=ALU.add).then_inc(vector_done, ve.step(("h", name, k - 1)))
                if ctx_part:
                    eng.wait_ge(scalar_done, ve.at(("rstd", name, "c")))
                    for k in range(KD + 1):
                        if k < KD:
                            stt(hT[:, k, S:S + L], cT[:, k, :], col("A2", k), rstd[:, S:S + L]).then_inc(vector_done, ve.step([("hcs", name, k), ("rstd_used", name)]))
                        if k >= 1:
                            eng.wait_ge(vector_done, ve.at(("hcs", name, k - 1)))
                            ts(hT[:, k - 1, S:S + L], hT[:, k - 1, S:S + L], ctx_part[1](k - 1), op0=ALU.add).then_inc(vector_done, ve.step(("hc", name, k - 1)))

            v.memset(ones[:, :], 1.0).then_inc(vector_done, ve.step("ones"))
            v.memset(bias_s[0:64, :, S - 64:S], -1e30).then_inc(vector_done, ve.step("bias_mask"))
            v.memset(col("zero"), 0.0).then_inc(vector_done, ve.step())
            v.memset(col("one"), 1.0).then_inc(vector_done, ve.step())
            v.memset(col("eps"), EPS).then_inc(vector_done, ve.step("cols0"))
            for i, nm in enumerate(("c", "c_2", "c_ctx_2")):
                eng.wait_ge(scalar_done, ve.at(("tanh_c", i)))
                ts(col("ctmp", 8 * i, 8), col("ctmp", 8 * i, 8), 0.5, 0.5, ALU.mult, ALU.add).then_inc(vector_done, ve.step())
                eng.wait_ge(vector_done, ve.own())
                tt(col("csilu", 8 * i, 8), col("ctmp", 8 * i, 8), V(nm, 0, 8), ALU.mult).then_inc(vector_done, ve.step("csilu"))
            eng.wait_ge(scalar_done, ve.at(("vec", VT - 1)))
            ts(col("Dh", 0, 16), V("ssm_D", 0, 16), 0.5).then_inc(vector_done, ve.step())
            ts(col("nwh", 0, 16), V("ssm_norm_w", 0, 16), 0.5).then_inc(vector_done, ve.step())
            eng.wait_ge(tensor_done, ve.at(("full",) + jobname("cT", KD - 1)))
            v.memset(up[:, :, 0:16], 0.0).then_inc(vector_done, ve.step("up_zero"))
            for i in range(DVE_MODS):
                for half in range(2):
                    eng.wait_ge(mod_w_landed[half], ve.at(("mod_w", 2 * i + half)))
                    for k in range(4):
                        c_ = col("csilu", 4 * half + k)
                        acc = (mod_acc if k % 2 == 0 else mod_odd)[:, i, :]
                        last = [("mod_half", 2 * i + half)] + ([("mod_acc", i)] if half else [])
                        if k >= 2 or half:
                            eng.wait_ge(vector_done, ve.at(("mod_sum", i, k % 2, (4 * half + k) // 2 - 1)))
                            stt(acc, mod_w[:, half, k, :], c_, acc, ALU.mult, ALU.add).then_inc(vector_done, ve.step(last + [("mod_sum", i, k % 2, (4 * half + k) // 2)]))
                        else:
                            ts(acc, mod_w[:, half, k, :], c_).then_inc(vector_done, ve.step(last + [("mod_sum", i, k % 2, 0)]))
            for i in range(DVE_MODS):
                mod(i)
            M = lambda l, part, k, n=1: col("mod", 48 * l + 8 * part + k, n)
            modulated("n1_0", V("norm1_w", 0, 8), M(0, 1, 0, 8), lambda k: M(0, 0, k), lambda k: xT[:, k, :])

            eng.wait_ge(const_landed, ve.at("const"))
            nm = 4
            WIN = (2, 4, 8, 16)
            for g in range(4):
                eng.wait_ge(scalar_done, ve.at(("uA", g)))
                src = up[:, g, :]
                cur, width = src, 1
                eng.wait_ge(vector_done, ve.own())
                bufs = win
                bi = 0
                while width < WIN[g]:
                    dst = bufs[bi]
                    lo = 2 * width - 1
                    tt(dst[:, lo:S + 16], cur[:, lo:S + 16], cur[:, lo - width:S + 16 - width], ALU.add).then_inc(vector_done, ve.step())
                    eng.wait_ge(vector_done, ve.own())
                    cur, width, bi = dst, 2 * width, 1 - bi
                ic = C("inv_count", 16 * g, 16)
                other = bufs[bi]
                tt(other[:, 16:32], cur[:, 16:32], ic, ALU.mult).then_inc(vector_done, ve.step())
                eng.wait_ge(vector_done, ve.own())
                tt(other[:, 0:16], other[:, 16:32], src[:, 16:32], ALU.subtract).then_inc(vector_done, ve.step())
                stt(other[:, 32:16 + S], cur[:, 32:16 + S], 1.0 / WIN[g], src[:, 32:16 + S], ALU.mult, ALU.subtract).then_inc(vector_done, ve.step())
                eng.wait_ge(vector_done, ve.own())
                v.tensor_copy(up[:, g, 0:16], other[:, 0:16]).then_inc(vector_done, ve.step())
                v.tensor_copy(up[:, g, 16:S], other[:, 32:16 + S]).then_inc(vector_done, ve.step(("pooled", g)))
            for i in range(4, 10):
                mod(i)
            def pool_out():
                for g in range(4):
                    b, free = full("poolA", g)
                    ts(aT[:, g, :], b, V("pool_scale", g)).then_inc(vector_done, ve.step([free, ("aoutA", g)]))

            def smA(h):
                eng.wait_ge(bias_landed[h % 2], ve.at(("biasA", h)))
                for t in range(4):
                    b, free = full("scA", h, t)
                    n = P * (t + 1)
                    if h >= 2:
                        eng.wait_ge(tensor_done, ve.at(("full",) + jobname("ptA", h - 2, t)))
                    stt(prob[h % 2][t][:, 0:n], b[:, 0:n], 0.125, bias_s[:, h % 2, 3 * P - t * P:S], ALU.mult, ALU.add).then_inc(vector_done, ve.step([free, ("biasA_used", h)]))
                eng.wait_ge(vector_done, ve.own())
                for t in range(4):
                    red(col("stat", 8 * (h % 2) + t), prob[h % 2][t][:, 0:P * (t + 1)], ALU.max, negate=True).then_inc(vector_done, ve.step(("smA", h, t)))

            def nrA(h):
                for t in range(4):
                    eng.wait_ge(scalar_done, ve.at(("expA", h, t)))
                    v.reciprocal(col("stat", 32 + t), col("stat", 16 + 8 * (h % 2) + t)).then_inc(vector_done, ve.step())
                eng.wait_ge(vector_done, ve.own())
                for t in range(4):
                    pr = prob[h % 2][t][:, 0:P * (t + 1)]
                    ts(pr, pr, col("stat", 32 + t)).then_inc(vector_done, ve.step(("probA", h, t)))
            pool_out()
            smA(0)
            for h in range(8):
                nrA(h)
                if h + 1 < 8:
                    smA(h + 1)
                for i in mods_at.get(("a", h), []):
                    mod(i)
            eng.wait_ge(vector_done, ve.own())

            def residual(jobs, gate, name):
                for k in range(8):
                    b, free = full(*jobs(k))
                    stt(xT[:, k, :], b, gate(k), xT[:, k, :], ALU.mult, ALU.add).then_inc(vector_done, ve.step([free, (name, k)]))
                    for i in mods_at.get(("oA", k), []):
                        mod(i)

            residual(lambda k: ("outA", k, "x"), lambda k: M(0, 2, k), "xA")

            def route(l):
                b, free = full("route", l)
                eng.wait_ge(rb_landed, ve.at(("rb", l)))
                ts(logitT[0:36, :], b[0:36, :], rb[0:36, :], op0=ALU.add).then_inc(vector_done, ve.step([free, ("logitT", l)]))
                b, free = full("logits", l)
                v.tensor_copy(rt[:, :, :], b[:, 0:144].rearrange("p (t n) -> p t n", t=4)).then_inc(vector_done, ve.step(free))
                eng.wait_ge(vector_done, ve.own())
                G, E = rt[:, :, 0:4], rt[:, :, 4:36]
                m = rs_[:, 0, :]
                red(m, G, ALU.max).then_inc(vector_done, ve.step())
                eng.wait_ge(vector_done, ve.own())
                bc = lambda s, n: s.unsqueeze(2).broadcast_to([P, 4, n])
                tt(r1[:, :, 0:4], G, bc(m, 4), ALU.subtract).then_inc(vector_done, ve.step())
                eng.wait_ge(vector_done, ve.own())
                ts(r1[:, :, 4:8], r1[:, :, 0:4], 0.0, op0=ALU.is_equal).then_inc(vector_done, ve.step())
                eng.wait_ge(vector_done, ve.own())
                tt(r1[:, :, 4:8], r1[:, :, 4:8], C("rank", 0, 4).unsqueeze(1).broadcast_to([P, 4, 4]), ALU.mult).then_inc(vector_done, ve.step(("grp", l)))
                eng.wait_ge(vector_done, ve.own())
                red(rs_[:, 1, :], r1[:, :, 4:8], ALU.max).then_inc(vector_done, ve.step())
                eng.wait_ge(vector_done, ve.own())
                tt(r1[:, :, 8:12], r1[:, :, 4:8], bc(rs_[:, 1, :], 4), ALU.is_equal).then_inc(vector_done, ve.step())
                eng.wait_ge(vector_done, ve.own())
                goh = r1[:, :, 8:12]
                for t in range(4):
                    tt(r2[:, t, 0:32].rearrange("p (g e) -> p g e", g=4),
                       E[:, t, :].rearrange("p (g e) -> p g e", g=4),
                       goh[:, t, :].unsqueeze(2).broadcast_to([P, 4, 8]), ALU.mult).then_inc(vector_done, ve.step())
                eng.wait_ge(vector_done, ve.own())
                for t in range(4):
                    red(r3[:, t, 0:8], r2[:, t, 0:32].rearrange("p (g e) -> p e g", g=4), ALU.add).then_inc(vector_done, ve.step())
                eng.wait_ge(vector_done, ve.own())
                sel = r3[:, :, 0:8]

                def first_max(vals, mx, tmp, hot, name=None):
                    red(mx, vals, ALU.max).then_inc(vector_done, ve.step())
                    eng.wait_ge(vector_done, ve.own())
                    tt(tmp, vals, bc(mx, 8), ALU.is_equal).then_inc(vector_done, ve.step())
                    eng.wait_ge(vector_done, ve.own())
                    tt(tmp, tmp, C("rank", 0, 8).unsqueeze(1).broadcast_to([P, 4, 8]), ALU.mult).then_inc(vector_done, ve.step())
                    eng.wait_ge(vector_done, ve.own())
                    red(rs_[:, 11, :], tmp, ALU.max).then_inc(vector_done, ve.step())
                    eng.wait_ge(vector_done, ve.own())
                    tt(hot, tmp, bc(rs_[:, 11, :], 8), ALU.is_equal).then_inc(vector_done, ve.step(name))
                    eng.wait_ge(vector_done, ve.own())
                first_max(sel, rs_[:, 2, :], r3[:, :, 8:16], r3[:, :, 16:24])
                stt(r3[:, :, 24:32], r3[:, :, 16:24], -3e38, sel, ALU.mult, ALU.add).then_inc(vector_done, ve.step())
                eng.wait_ge(vector_done, ve.own())
                first_max(r3[:, :, 24:32], rs_[:, 3, :], r3[:, :, 8:16], r2[:, :, 0:8])
                tt(rs_[:, 4, :], rs_[:, 3, :], rs_[:, 2, :], ALU.subtract).then_inc(vector_done, ve.step(("top2", l)))
                for c, hot in enumerate((r3[:, :, 16:24], r2[:, :, 0:8])):
                    for t in range(4):
                        tt(pick[:, c, 32 * t:32 * t + 32].rearrange("p (g e) -> p g e", g=4),
                           goh[:, t, :].unsqueeze(2).broadcast_to([P, 4, 8]),
                           hot[:, t, :].unsqueeze(1).broadcast_to([P, 4, 8]), ALU.mult).then_inc(vector_done, ve.step())
                eng.wait_ge(vector_done, ve.own())
                tt(r4[:, :, 0:32], pick[:, 0, :].rearrange("p (t e) -> p t e", t=4), pick[:, 1, :].rearrange("p (t e) -> p t e", t=4),
                   ALU.add).then_inc(vector_done, ve.step(("picks", l)))
                v.memset(scan_one[0:32, :], 1.0).then_inc(vector_done, ve.step())
                v.memset(block_t[:, :, BLOCKS:], float(NO_PAIR)).then_inc(vector_done, ve.step())
                b, free = full("picksT", l)
                eng.wait_ge(vector_done, ve.own())
                v.tensor_tensor_scan(pos[0:32, :], scan_one[0:32, :], b[0:32, :], 0.0, ALU.mult, ALU.add).then_inc(vector_done, ve.step(free))
                eng.wait_ge(route_c_landed, 16 * (l + 1))
                eng.wait_ge(vector_done, ve.own())
                tt(e_col[0:32, 4:8], R("thresholds", 32), pos[0:32, S - 1:S].broadcast_to([32, 4]), ALU.is_lt).then_inc(vector_done, ve.step())
                eng.wait_ge(vector_done, ve.own())
                red(e_col[0:32, 1:2], e_col[0:32, 4:8], ALU.add).then_inc(vector_done, ve.step(("need", l)))
                b, free = full("ends", l)
                eng.wait_ge(vector_done, ve.own())
                v.tensor_copy(e_col[0:32, 2:3], b[0:32, 0:1]).then_inc(vector_done, ve.step(free))
                eng.wait_ge(vector_done, ve.own())
                tt(e_col[0:32, 3:4], e_col[0:32, 2:3], e_col[0:32, 1:2], ALU.subtract).then_inc(vector_done, ve.step())
                eng.wait_ge(vector_done, ve.own())
                ts(e_col[0:32, 3:4], e_col[0:32, 3:4], float(P), -1.0, ALU.mult, ALU.add).then_inc(vector_done, ve.step())
                eng.wait_ge(vector_done, ve.own())
                ts(slot_of[0:32, :], pos[0:32, :], e_col[0:32, 3:4], op0=ALU.add).then_inc(vector_done, ve.step(("slot_of", l)))
                ts(block_t[0:32, 0, 0:BLOCKS], R("block_no", 32), e_col[0:32, 2:3], op0=ALU.is_ge).then_inc(vector_done, ve.step(("ended", l)))
                b, free = full("slots", l)
                for c in range(2):
                    tt(pick[:, c, :], pick[:, c, :], b[:, 0:128], ALU.mult).then_inc(vector_done, ve.step(free if c else None))
                eng.wait_ge(vector_done, ve.own())
                for c in range(2):
                    red(place[:, 0, 4 * c:4 * c + 4], pick[:, c, :].rearrange("p (t e) -> p t e", t=4), ALU.add).then_inc(vector_done, ve.step())
                eng.wait_ge(vector_done, ve.own())
                tt(passed[:, :, :], place[:, 0, :].unsqueeze(2).broadcast_to([P, 8, BLOCKS + 1]),
                   R("block_start").unsqueeze(1).broadcast_to([P, 8, BLOCKS + 1]), ALU.is_ge).then_inc(vector_done, ve.step())
                eng.wait_ge(vector_done, ve.own())
                red(place[:, 1, :], passed[:, :, :], ALU.add).then_inc(vector_done, ve.step())
                tt(in_block[:, :, :], passed[:, :, 0:BLOCKS], passed[:, :, 1:BLOCKS + 1], ALU.subtract).then_inc(vector_done, ve.step())
                eng.wait_ge(vector_done, ve.own())
                ts(place[:, 2, :], place[:, 1, :], -float(P), float(P), ALU.mult, ALU.add).then_inc(vector_done, ve.step())
                tt(in_block[:, :, :], in_block[:, :, :], R("pair_less").unsqueeze(2).broadcast_to([P, 8, BLOCKS]), ALU.mult).then_inc(vector_done, ve.step(("in_block", l)))
                eng.wait_ge(vector_done, ve.own())
                tt(place[:, 2, :], place[:, 2, :], place[:, 0, :], ALU.add).then_inc(vector_done, ve.step())
                eng.wait_ge(vector_done, ve.own())
                tt(in_lane[:, :, :], place[:, 2, :].unsqueeze(2).broadcast_to([P, 8, P]),
                   R("lane").unsqueeze(1).broadcast_to([P, 8, P]), ALU.is_equal).then_inc(vector_done, ve.step(("in_lane", l)))
                b, free = full("experts", l)
                ts(expert_u[0:1, :], b[0:1, 0:BLOCKS], float(EXPERTS - 1), op0=ALU.min).then_inc(vector_done, ve.step([free, ("expert_u", l)]))
                b, free = full("pairs", l)
                ts(block_t[:, 1, 0:BLOCKS], b[:, 0:BLOCKS], float(NO_PAIR), op0=ALU.add).then_inc(vector_done, ve.step(free))
                eng.wait_ge(vector_done, ve.own())
                ts(block_t[:, 2, :], block_t[:, 1, :], float(S), -float(S), ALU.is_ge, ALU.mult).then_inc(vector_done, ve.step())
                eng.wait_ge(vector_done, ve.own())
                tt(block_t[:, 2, :], block_t[:, 2, :], block_t[:, 1, :], ALU.add).then_inc(vector_done, ve.step())
                eng.wait_ge(vector_done, ve.own())
                v.tensor_copy(pair_u[:, 0, :], block_t[:, 2, :]).then_inc(vector_done, ve.step())
                v.tensor_copy(pair_u[:, 1, :], block_t[:, 1, :]).then_inc(vector_done, ve.step(("pair_u", l)))
                eng.wait_ge(scalar_done, ve.at(("eg", l)))
                red(rs_[:, 5, :], r1[:, :, 0:4], ALU.add).then_inc(vector_done, ve.step())
                eng.wait_ge(scalar_done, ve.at(("er", l)))
                ts(rs_[:, 6, :], rs_[:, 4, :], 1.0, op0=ALU.add).then_inc(vector_done, ve.step())
                eng.wait_ge(vector_done, ve.own())
                tt(rs_[:, 7, :], rs_[:, 5, :], rs_[:, 6, :], ALU.mult).then_inc(vector_done, ve.step())
                eng.wait_ge(vector_done, ve.own())
                v.reciprocal(rs_[:, 8, :], rs_[:, 7, :]).then_inc(vector_done, ve.step())
                eng.wait_ge(vector_done, ve.own())
                tt(rs_[:, 9, :], rs_[:, 8, :], rs_[:, 4, :], ALU.mult).then_inc(vector_done, ve.step())

            def moe(l):
                route(l)
                loop = f"moe{l}"
                with ve.loop(loop, BLOCKS // TURN) as i:
                    def hidden(b):
                        eng.wait_ge(scalar_done, ve.at((loop, "t", b)))
                        bk, free = full(loop, "ab", b)
                        stt(e_u[:, b % 2, :], e_t[:, b % 2, :], 1.0, bk[:, 0:P], ALU.add, ALU.mult).then_inc(vector_done, ve.step())
                        eng.wait_ge(vector_done, ve.own())
                        stt(hid[:, b % 2, :], e_u[:, b % 2, :], 0.5, bk[:, P:2 * P], ALU.mult, ALU.mult).then_inc(vector_done, ve.step([free, (loop, "hid", b)]))

                    hidden(0)
                    for b in range(TURN):
                        if b + 1 < TURN:
                            hidden(b + 1)
                        eng.wait_ge(y_stored[b % AHEAD], y_free_at(l, i, b))
                        for half in range(2):
                            bk, free = full(loop, "y", b, half)
                            v.tensor_copy(y_rows[:, b % AHEAD, half * S:(half + 1) * S], bk).then_inc(vector_done, ve.step([free, (loop, "y_rows", b)]))
                for i in range(16, 20) if l == 0 and stage_on(3) else ():
                    mod(i)
                for t in range(4):
                    eng.wait_ge(y_back_landed[t], 32 * (l + 1))
                    ts(y_tok[0][:, t, :], y_tok[0][:, t, :], rs_[:, 8, t:t + 1]).then_inc(vector_done, ve.step())
                    eng.wait_ge(vector_done, ve.own())
                    stt(y_tok[0][:, t, :], y_tok[1][:, t, :], rs_[:, 9, t:t + 1], y_tok[0][:, t, :], ALU.mult, ALU.add).then_inc(vector_done, ve.step(("y_tok", l, t)))
                for k in range(KD):
                    b, free = full("moe_y", l, k)
                    stt(xT[:, k, :], b, M(l, 5, k), xT[:, k, :], ALU.mult, ALU.add).then_inc(vector_done, ve.step([free, ("x", loop, k)]))

            if stage_on(2):
                modulated("n2_0", V("norm2_w", 0, 8), M(0, 4, 0, 8), lambda k: M(0, 3, k), lambda k: xT[:, k, :])
                moe(0)
            if stage_on(3):
                modulated("n1_1", V("norm1_w", 8, 8), M(1, 1, 0, 8), lambda k: M(1, 0, k), lambda k: xT[:, k, :])
                v.memset(g_pad[:, 0:3], 0.0).then_inc(vector_done, ve.step("pad_zero"))
                b, free = full("dt")
                eng.wait_ge(dtb_landed, ve.at("dtb"))
                ts(dtT[0:32, 0, :], b[0:32, :], col("dtb", rows=32), op0=ALU.add).then_inc(vector_done, ve.step([free, "dt_v"]))
                v.memset(dtT[0:32, 2, :], 1.0).then_inc(vector_done, ve.step())
                eng.wait_ge(scalar_done, ve.at("dt_ln"))
                stt(dtT[0:32, 0, :], dtT[0:32, 0, :], 0.0, dtT[0:32, 1, :], ALU.max, ALU.add).then_inc(vector_done, ve.step())
                eng.wait_ge(scalar_done, ve.at("expA_log"))
                eng.wait_ge(vector_done, ve.own())
                ts(dtT[0:32, 1, :], dtT[0:32, 0, :], col("negA", rows=32), -1.0, ALU.mult, ALU.mult).then_inc(vector_done, ve.step())
                eng.wait_ge(vector_done, ve.own())
                v.tensor_tensor_scan(g_t[0:32, :], dtT[0:32, 2, :], dtT[0:32, 1, :], 0.0, ALU.mult, ALU.add).then_inc(vector_done, ve.step())
                eng.wait_ge(vector_done, ve.own())
                v.tensor_copy(dtT[0:32, 1, :], g_t[0:32, :]).then_inc(vector_done, ve.step("acs"))
                b, free = full("dtTok")
                bv = b[:, 0:256].rearrange("p (t n) -> p t n", t=4)
                ts(dtTok[:, :, 0:32], bv[:, :, 0:32], 0.5).then_inc(vector_done, ve.step())
                v.tensor_copy(dtTok[:, :, 32:64], bv[:, :, 32:64]).then_inc(vector_done, ve.step([free, "dtTok"]))
                for g in range(8):
                    for qi, n in enumerate(("x0", "x1", "B", "C")):
                        chunk = [2 * g, 2 * g + 1, 16 + g, 24 + g][qi]
                        dst = [g_x[:, 0, :], g_x[:, 1, :], g_bc[:, 0, :], g_bc[:, 1, :]][qi]
                        if g >= 1:
                            if qi < 2:
                                eng.wait_ge(tensor_done, ve.at(("full",) + jobname("xtok", g - 1, qi)))
                            else:
                                eng.wait_ge(tensor_done, ve.at(("full",) + jobname("cb", g - 1, 3)))
                        eng.wait_ge(scalar_done, ve.at(("pad", g, qi)))
                        ts(dst, g_pad[:, 3:3 + S], V("ssm_conv_w", 96 + chunk), V("ssm_conv_b", chunk), ALU.mult, ALU.add).then_inc(vector_done, ve.step())
                        for tap in (2, 1, 0):
                            eng.wait_ge(vector_done, ve.own())
                            stt(dst, g_pad[:, tap:tap + S], V("ssm_conv_w", 32 * tap + chunk), dst, ALU.mult, ALU.add).then_inc(vector_done, ve.step([("conv", g, qi), ("pad_used", (g, qi))]))
                        eng.wait_ge(scalar_done, ve.at(("conv_t", g, qi)))
                        eng.wait_ge(vector_done, ve.own())
                        stt(dst, g_t, 1.0, dst, ALU.add, ALU.mult).then_inc(vector_done, ve.step(("ssm_x", g, qi) if qi < 2 else ("ssm_bc", g, qi - 2)))
                    for zz in range(2):
                        eng.wait_ge(scalar_done, ve.at(("zt", g, zz)))
                        b, free = full("ssm", g, f"z{zz}", "x")
                        stt(g_z[:, zz, :], g_z[:, zz, :], 1.0, b, ALU.add, ALU.mult).then_inc(vector_done, ve.step(free))
                    for cc in range(2):
                        b, free = full("xtok", g, cc)
                        if g >= 1:
                            eng.wait_ge(tensor_done, ve.at(("seg_used", 4 * g - 1)))
                        for t in range(4):
                            ds = dtTok[:, t, 4 * g + 2 * cc:4 * g + 2 * cc + 2].unsqueeze(2).broadcast_to([P, 2, 64])
                            tt(g_xdt[:, t, P * cc:P * (cc + 1)].rearrange("p (h d) -> p h d", h=2),
                               b[:, t * P:(t + 1) * P].rearrange("p (h d) -> p h d", h=2), ds, ALU.mult).then_inc(vector_done, ve.step([free, ("xdt", g, cc)]))

                    def arg(h):
                        eng.wait_ge(acs_row_landed[h % 2], ve.at(("acs_row", h)))
                        if h >= 2:
                            eng.wait_ge(tensor_done, ve.at(("seg_used", h - 2)))
                        for t in range(4):
                            stt(g_seg[:, h % 2, SOFF[t]:SOFF[t] + S - t * P], acs_b[:, h % 2, t * P:S],
                                dtTok[:, t, 32 + h:33 + h], C("mask_next", 0, S - t * P), ALU.subtract, ALU.min).then_inc(vector_done, ve.step([("arg", h), ("acs_used", h)]))

                    def seg(h):
                        eng.wait_ge(scalar_done, ve.at(("seg_e", h)))
                        eng.wait_ge(scalar_done, ve.at(("cb_c", g)))
                        tt(g_seg[:, h % 2, :], g_seg[:, h % 2, :], g_cb, ALU.mult).then_inc(vector_done, ve.step(("seg", h)))
                    arg(4 * g)
                    for r in range(4):
                        if r < 3:
                            arg(4 * g + r + 1)
                        seg(4 * g + r)
                    for i in mods_at[("g", g)]:
                        mod(i)
                    for cc in range(2):
                        b, free = full("y", g, cc)
                        k = 2 * g + cc
                        stt(yT[:, k, :], g_x[:, cc, :], col("Dh", k), b, ALU.mult, ALU.add).then_inc(vector_done, ve.step(free))
                        eng.wait_ge(vector_done, ve.own())
                        tt(yT[:, k, :], yT[:, k, :], g_z[:, cc, :], ALU.mult).then_inc(vector_done, ve.step(("yz", g, cc)))
                    eng.wait_ge(scalar_done, ve.at(("rstd", ("g", g), "x")))
                    for cc in range(2):
                        k = 2 * g + cc
                        stt(yT[:, k, :], yT[:, k, :], col("nwh", k), rstd[:, 0:S]).then_inc(vector_done, ve.step([("yn", k), ("rstd_used", ("g", g))]))
                for c in range(8):
                    b, free = full("outM", c, "x")
                    stt(xT[:, c, :], b, M(1, 2, c), xT[:, c, :], ALU.mult, ALU.add).then_inc(vector_done, ve.step([free, ("xM", c)]))
                    for i in mods_at.get(("o", c), []):
                        mod(i)
            if stage_on(4):
                modulated("n2_1", V("norm2_w", 8, 8), M(1, 4, 0, 8), lambda k: M(1, 3, k), lambda k: xT[:, k, :])
                moe(1)
            if stage_on(5):
                eng.wait_ge(scalar_done, ve.at(("rstd", "fin1", "x")))
                for k in range(KD):
                    stt(xT[:, k, :], xT[:, k, :], V("final_norm_w", k), rstd[:, 0:S]).then_inc(vector_done, ve.step([("rstd_used", "fin1"), ("x_new", 0, k)]))
            if stage_on(6):
                eng.wait_ge(vector_done, ve.own())
                v.memset(col("stat", 0, 64), 0.0).then_inc(vector_done, ve.step(("x_in", 0)))
                eng.wait_ge(scalar_done, ve.at("lgt"))
                stt(col("lg", 0, 16), col("small", 0, 16), 0.0, col("lgt", 0, 16), ALU.min, ALU.subtract).then_inc(vector_done, ve.step())
                eng.wait_ge(vector_done, ve.own())
                ts(col("lgm", 0, 16), col("lg", 0, 16), -float(P)).then_inc(vector_done, ve.step())
                ts(col("lgp", 0, 16), col("lg", 0, 16), float(P)).then_inc(vector_done, ve.step())
                ts(col("hlb", 0, 8), V("cf_ln_b_2", 0, 8), 0.5).then_inc(vector_done, ve.step())
                zn = {"n": 0}

                def z_mul(name, l, c, cx, chunk, factor):
                    n = zn["n"]
                    zn["n"] += 1
                    for tag, o, w in parts(cx):
                        eng.wait_ge(scalar_done, ve.at(("zt", n, tag)))
                        b, free = full(name, l, c, tag)
                        stt(zt[:, n % 2, o:o + w], zt[:, n % 2, o:o + w], 1.0, b[:, 0:w], ALU.add, ALU.mult).then_inc(vector_done, ve.step(free))
                    return n

                def z_apply(n, l, cx, chunk, factor):
                    eng.wait_ge(vector_done, ve.own())
                    for tag, o, w in parts(cx):
                        bo = CO if tag == "c" else 0
                        stt(br[:, chunk, bo:bo + w], br[:, chunk, bo:bo + w], factor, zt[:, n % 2, o:o + w], ALU.mult, ALU.mult).then_inc(vector_done, ve.step([("zt_used", n), ("branch", l, chunk)]))

                for l in range(2 if upto > 6 else 1):
                    cx = l == 0
                    w_ = CW if cx else S
                    M2 = lambda part, k, n=1, vv=0: col("mod2", 48 * l + 24 * vv + 8 * part + k, n)
                    modulated(("b2", l), V("norm_w_2", 8 * l, 8), M2(1, 0, 8), lambda k: M2(0, k), lambda k: xT[:, k, :],
                              ctx_part=(M2(1, 0, 8, 1), lambda k: M2(0, k, 1, 1)))
                    for i in range(2):
                        v.memset(cu[:, i, :], 0.0).then_inc(vector_done, ve.step([("cu_free", l, i)]))
                    if cx:
                        for c in range(16):
                            v.memset(br[:, c, S:CO], 0.0).then_inc(vector_done, ve.step())
                    cw = lambda k, c: V(f"cf_conv_w_2{'ab'[l]}", 4 * k + c)

                    def glu(c):
                        for tag, o, w in parts(cx, CO):
                            eng.wait_ge(scalar_done, ve.at(("cf_t", l, c, tag)))
                            b, free = full("cf_a", l, c, tag)
                            u = cu[:, c % 2, 15 + o:15 + o + w]
                            stt(u, u, 1.0, b[:, 0:w], ALU.add, ALU.mult).then_inc(vector_done, ve.step(free))

                    def conv(c):
                        eng.wait_ge(vector_done, ve.own())
                        acc = br[:, 8 + c, 0:w_]
                        ts(acc, cu[:, c % 2, 0:w_], cw(0, c)).then_inc(vector_done, ve.step())
                        for k in range(1, 31):
                            eng.wait_ge(vector_done, ve.own())
                            stt(acc, cu[:, c % 2, k:k + w_], cw(k, c), acc, ALU.mult, ALU.add).then_inc(vector_done, ve.step(("cu_free", l, c + 2) if k == 30 else None))
                        eng.wait_ge(vector_done, ve.own())
                        ts(acc, acc, 0.5, V("cf_conv_b_2", 4 * l + c), ALU.mult, ALU.add).then_inc(vector_done, ve.step(("cf_conv", l, c)))

                    for c in range(2):
                        glu(c)
                        conv(c)
                    eng.wait_ge(rope_landed, ve.at(("rope", l)))

                    def rotate(t, job_, name):
                        b, free = full(*job_)
                        tt(t, t, cos_, ALU.mult).then_inc(vector_done, ve.step())
                        r_ = square[:, 0, 0:S]
                        tt(r_, b, sin_, ALU.mult).then_inc(vector_done, ve.step(free))
                        eng.wait_ge(vector_done, ve.own())
                        tt(t, t, r_, ALU.add).then_inc(vector_done, ve.step(name))
                    eng.wait_ge(tensor_done, ve.at(("sq_used", ("b2", l), KD - 1)))
                    eng.wait_ge(vector_done, ve.own())
                    rotate(k_raw[:, 0:S], ("rot_k", l), ("k_roped", l))
                    eng.wait_ge(vector_done, ve.own())
                    for c in range(4):
                        if c == 1:
                            glu(2)
                            conv(2)
                            eng.wait_ge(vector_done, ve.own())
                        if c == 2:
                            glu(3)
                        rotate(q_[:, c, 0:S], ("rot_q", l, c), ("roped", l))
                        eng.wait_ge(vector_done, ve.own())

                    rounds = [(n, j) for n in x_tiles(l) for j in range(2)]

                    def att_max(r, n, j):
                        q = r % 2
                        kt = key_tiles(n)
                        wl = P * len(kt)
                        for hh in range(4):
                            h = 4 * j + hh
                            if r >= 2:
                                pn, pj = rounds[r - 2]
                                eng.wait_ge(tensor_done, ve.at(("full",) + jobname("pt2", l, 4 * pj + hh, pn, "x")))
                            if wl:
                                off = P * (kt[0] - (n - 1))
                                b, free = full("sl", l, h, n)
                                stt(pr2[q][:, hh, 0:wl], b[:, 0:wl], 0.125, C("window", off, wl), ALU.mult, ALU.add).then_inc(vector_done, ve.step(free))
                            b, free = full("sx", l, h, n)
                            ts(pr2[q][:, hh, wl:wl + L], b[:, 0:L], 0.125).then_inc(vector_done, ve.step(free))
                        eng.wait_ge(vector_done, ve.own())
                        red(col("stat", 32 * q, 4), pr2[q][:, :, 0:wl + L], ALU.max).then_inc(vector_done, ve.step())
                        eng.wait_ge(vector_done, ve.own())
                        sink = col("small", 16 + 8 * l + 4 * j, 4)
                        tt(col("stat", 32 * q, 4), col("stat", 32 * q, 4), sink, ALU.max).then_inc(vector_done, ve.step())
                        eng.wait_ge(vector_done, ve.own())
                        ts(col("stat", 32 * q + 4, 4), col("stat", 32 * q, 4), -1.0).then_inc(vector_done, ve.step())
                        tt(col("stat", 32 * q + 12, 4), sink, col("stat", 32 * q, 4), ALU.subtract).then_inc(vector_done, ve.step(("nm2", l, n, j)))

                    def att_norm(r, n, j):
                        q = r % 2
                        w = P * len(key_tiles(n)) + L
                        eng.wait_ge(scalar_done, ve.at(("es2", l, n, j)))
                        tt(col("stat", 32 * q + 16, 4), col("stat", 32 * q + 8, 4), col("stat", 32 * q + 12, 4), ALU.add).then_inc(vector_done, ve.step())
                        eng.wait_ge(vector_done, ve.own())
                        v.reciprocal(col("stat", 32 * q + 20, 4), col("stat", 32 * q + 16, 4)).then_inc(vector_done, ve.step())
                        eng.wait_ge(vector_done, ve.own())
                        for hh in range(4):
                            pr = pr2[q][:, hh, 0:w]
                            ts(pr, pr, col("stat", 32 * q + 20 + hh)).then_inc(vector_done, ve.step(("pr2", l, n, 4 * j + hh)))
                    att_max(0, *rounds[0])
                    for r, (n, j) in enumerate(rounds):
                        att_norm(r, n, j)
                        if r + 1 < len(rounds):
                            att_max(r + 1, *rounds[r + 1])
                    conv(3)
                    eng.wait_ge(scalar_done, ve.at(("att_o", l)))
                    for c in range(4):
                        z_apply(z_mul("att_z", l, c, cx, 12 + c, 0.5), l, cx, 12 + c, 0.5)
                    eng.wait_ge(vector_done, ve.own())
                    v.memset(col("stat", 0, 1), 0.0).then_inc(vector_done, ve.step(("att_done", l)))

                    def decay(h):
                        lf, lb = 8 * l + h, 8 * l + 4 + h
                        eng.wait_ge(tabs_landed, ve.at(("tabs", l)))
                        eng.wait_ge(vector_done, ve.own())
                        ts(rdt, dminus, col("lg", lb)).then_inc(vector_done, ve.step())
                        eng.wait_ge(vector_done, ve.own())
                        stt(dstrip, dplus, col("lg", lf), rdt, ALU.mult, ALU.add).then_inc(vector_done, ve.step(("darg", l, h)))
                        eng.wait_ge(scalar_done, ve.at(("rtmp", l, h)))
                        tt(rctx[:, :, :], rctx[:, :, :], rtmp[:, :, :], ALU.add).then_inc(vector_done, ve.step())
                        eng.wait_ge(scalar_done, ve.at(("dstrip", l, h)))
                        eng.wait_ge(vector_done, ve.own())
                    for h in range(4):
                        decay(h)
                        ks = P ** -0.5
                        for t in range(6):
                            b, free = full("rs", l, h, t)
                            dec = dstrip[:, 384 - P * t:384 - P * t + S] if t < 4 else rctx[:, t - 4, :]
                            stt(rsc[:, t, :], b, ks, dec, ALU.mult, ALU.mult).then_inc(vector_done, ve.step([free, ("rsc", l, h, t)]))
                        if cx:
                            for t in range(2):
                                b, free = full("rs_c", l, h, t)
                                stt(rsc_c[:, t, :], b[:, 0:L], ks, dstrip[:, 384 - P * t:384 - P * t + L], ALU.mult, ALU.mult).then_inc(vector_done, ve.step([free, ("rsc_c", l, h)]))
                        eng.wait_ge(vector_done, ve.own())
                        v.memset(col("stat", 1, 1), 0.0).then_inc(vector_done, ve.step(("rctx_used", l, h)))
                        zi = z_mul("ret_z", l, h, cx, h, -0.5)
                        for tag, o, w in parts(cx):
                            b, free = full("rm", l, h, tag)
                            stt(rnd[:, o:o + w], b[:, 0:w], 1.0 / P, ro[:, o:o + w], ALU.mult, ALU.subtract).then_inc(vector_done, ve.step([free, ("rnd", l, h, tag)]))
                        eng.wait_ge(scalar_done, ve.at(("rstd", ("ret", l, h), "c" if cx else "x")))
                        for tag, o, w in parts(cx):
                            bo = CO if tag == "c" else 0
                            stt(br[:, h, bo:bo + w], rnd[:, o:o + w], V("ret_gn_w_2", 4 * l + h), rstd[:, o:o + w]).then_inc(vector_done, ve.step([("rstd_used", ("ret", l, h))]))
                        z_apply(zi, l, cx, h, -0.5)
                    eng.wait_ge(vector_done, ve.own())
                    v.memset(sc_u[:, :, :], 0.0).then_inc(vector_done, ve.step(("ret_done", l)))
                    eng.wait_ge(vector_done, ve.own())
                    for c in range(4):
                        for tag, o, w in parts(cx):
                            bo = CO if tag == "c" else 0
                            eng.wait_ge(scalar_done, ve.at(("sc_cc", l, c, tag)))
                            b, free = full("sc_x", l, c, tag)
                            tt(sc_u[:, c % 2, 1 + bo:1 + bo + w], b[:, 0:w], sc_c[:, c % 2, o:o + w], ALU.mult).then_inc(vector_done, ve.step([free, ("sc_c_used", l, c)]))
                        wv = lambda k: V("sc_conv_w_2", 12 * l + 4 * k + c)
                        y = br[:, 4 + c, 0:w_]
                        eng.wait_ge(vector_done, ve.own())
                        ts(y, sc_u[:, c % 2, 0:w_], wv(0)).then_inc(vector_done, ve.step())
                        for k in (1, 2):
                            eng.wait_ge(vector_done, ve.own())
                            stt(y, sc_u[:, c % 2, k:k + w_], wv(k), y, ALU.mult, ALU.add).then_inc(vector_done, ve.step())
                        eng.wait_ge(vector_done, ve.own())
                        for tag, o, w in parts(cx):
                            bo = CO if tag == "c" else 0
                            b, free = full("sc_b", l, c, tag)
                            tt(br[:, 4 + c, bo:bo + w], br[:, 4 + c, bo:bo + w], b[:, 0:w], ALU.mult).then_inc(vector_done, ve.step(free))
                        z_apply(z_mul("sc_z", l, c, cx, 4 + c, 0.5), l, cx, 4 + c, 0.5)
                    eng.wait_ge(vector_done, ve.own())
                    for tag, o, w in parts(cx, CO):
                        b, free = full("lm", l, tag)
                        for c in range(4):
                            t_ = br[:, 8 + c, o:o + w]
                            stt(t_, b[:, 0:w], 1.0 / (4 * P), t_, ALU.mult, ALU.subtract).then_inc(vector_done, ve.step([("cf_nd", l, c)] + ([free] if c == 3 else [])))
                    eng.wait_ge(scalar_done, ve.at(("rstd", ("ln", l), "c" if cx else "x")))
                    for c in range(4):
                        for tag, o, w in parts(cx):
                            bo = CO if tag == "c" else 0
                            t_ = br[:, 8 + c, bo:bo + w]
                            stt(t_, t_, V("cf_ln_w_2", 4 * l + c), rstd[:, o:o + w]).then_inc(vector_done, ve.step([("cf_v", l, c), ("rstd_used", ("ln", l))]))
                    for c in range(4):
                        t_ = br[:, 8 + c, 0:w_]
                        eng.wait_ge(scalar_done, ve.at(("cf_tt", l, c)))
                        ts(t_, t_, -1.0, V("cf_ln_b_2", 4 * l + c), ALU.mult, ALU.add).then_inc(vector_done, ve.step())
                        eng.wait_ge(vector_done, ve.own())
                        stt(t_, cf_t[:, c % 2, 0:w_], 1.0, t_, ALU.add, ALU.mult).then_inc(vector_done, ve.step(("cf_y", l, c)))
                    for c in range(4):
                        z_apply(z_mul("cf_z", l, c, cx, 8 + c, 0.25), l, cx, 8 + c, 0.25)
                    eng.wait_ge(vector_done, ve.own())
                    v.memset(col("stat", 0, 1), 0.0).then_inc(vector_done, ve.step(("cf_done", l)))
                    for c in range(8):
                        for i in range(4):
                            m = 4 * c + i
                            for tag, o, w in parts(cx):
                                eng.wait_ge(scalar_done, ve.at(("mt", l, m, tag)))
                                b, free = full("by", l, c, i, tag)
                                dst = mrg[:, c, o:o + w] if i == 0 else mt[:, m % 4, o:o + w]
                                stt(dst, mt[:, m % 4, o:o + w], 1.0, b[:, 0:w], ALU.add, ALU.mult).then_inc(vector_done, ve.step([free, ("mt_used", l, m)]))
                            if i:
                                eng.wait_ge(vector_done, ve.own())
                                w = S + L if cx else S
                                tt(mrg[:, c, 0:w], mrg[:, c, 0:w], mt[:, m % 4, 0:w], ALU.add).then_inc(vector_done, ve.step([("mt_used", l, m)] + ([("mrg", l, c)] if i == 3 else [])))
                    for vv in range(2):
                        ts(col("hg", 8 * vv, 8), M2(2, 0, 8, vv), 0.5).then_inc(vector_done, ve.step())
                    eng.wait_ge(vector_done, ve.own())
                    for c in range(8):
                        for tag, o, w in parts(cx):
                            b, free = full("out2", l, c, tag)
                            t_ = (xT if tag == "x" else cT)[:, c, :]
                            stt(t_, b[:, 0:w], col("hg", c if tag == "x" else 8 + c), t_, ALU.mult, ALU.add).then_inc(vector_done, ve.step([free, ("x_new", l + 1, c)]))
                    eng.wait_ge(vector_done, ve.own())
                    v.memset(col("stat", 0, 1), 0.0).then_inc(vector_done, ve.step(("x_in", l + 1)))
                if upto > 7:
                    eng.wait_ge(scalar_done, ve.at(("rstd", "fin2", "x")))
                    for k in range(KD):
                        stt(xT[:, k, :], xT[:, k, :], V("final_norm_w_2", k), rstd[:, 0:S]).then_inc(vector_done, ve.step([("rstd_used", "fin2"), ("x_out", k)]))
            eng.wait_ge(vector_done, ve.own())
            v.memset(col("stat", 0, 1), 0.0).then_inc(vector_done, ve.step("x_final"))

        @block.gpsimd
        def _(eng):
            po = Count(eng, "gpsimd_done", sems, old, new)
            g = nc.gpsimd

            def mod_load(q):
                i, half = q // 2, q % 2
                kind, l, b = MODS[i]
                if q >= 2:
                    eng.wait_ge(po.doer(("mod_half", q - 2)), po.at(("mod_half", q - 2)))
                eng.dma_start(mod_w[:, half], a[kind][l][512 * half:512 * half + 512, 512 * b:512 * b + 512]
                       .rearrange("(k p) n -> p k n", p=P)).then_inc(mod_w_landed[half], po.landing(f"mod_w_{half}", ("mod_w", q)))

            def moe(l):
                loop = f"moe{l}"
                eng.wait_ge(vector_done, po.at(("xA" if l == 0 else "xM", KD - 1)))
                g.memset(rows, 0.0).then_inc(gpsimd_done, po.step())
                eng.wait_ge(h_rows_stored, 64 * (l + 1))
                eng.wait_ge(vector_done, po.at(("pair_u", l)))
                token_limit, pair_limit = eng.to_reg(S - 1), eng.to_reg(2 * S - 1)

                def fetch(at, s_):
                    eng.indirect_dma_start(rows[:, s_, :], None, h_dram[l],
                                           bass.IndirectOffsetOnAxis(ap=at, axis=0), bounds_check=token_limit,
                                           oob_is_err=False).then_inc(rows_landed[s_], 16)

                eng.wait_ge(gpsimd_done, po.own())
                for b in range(AHEAD):
                    g.tensor_copy(now_u[:, 0, b:b + 1], pair_u[:, 0, b:b + 1]).then_inc(gpsimd_done, po.step())
                    eng.wait_ge(gpsimd_done, po.own())
                    fetch(now_u[:, 0, b:b + 1], b)
                for s_ in range(AHEAD):
                    eng.wait_ge(rows_landed[s_], 16 * (l * (BLOCKS // AHEAD + 1) + 1))
                    eng.indirect_dma_start(y_dram[l], bass.IndirectOffsetOnAxis(ap=pair_u[:, 1, BLOCKS:BLOCKS + 1], axis=0),
                                           rows[:, s_, :], None, bounds_check=pair_limit,
                                           oob_is_err=False).then_inc(y_stored[s_], 16)
                with po.loop(loop, BLOCKS // TURN) as i:
                    for b in range(TURN):
                        s_ = b % AHEAD
                        eng.wait_ge(tensor_done, po.at((loop, "rows_used", b)))
                        g.tensor_copy(now_u[:, 0, s_:s_ + 1], pair_u[:, 0, bass.ds(i * TURN + b + AHEAD, 1)]).then_inc(gpsimd_done, po.step())
                        eng.wait_ge(gpsimd_done, po.own())
                        eng.sem_inc(pool_go, 1)
                        fetch(now_u[:, 0, s_:s_ + 1], s_)
                        eng.wait_ge(y_stored[s_], y_free_at(l, i, b))
                        g.tensor_copy(now_u[:, 1, s_:s_ + 1], pair_u[:, 1, bass.ds(i * TURN + b, 1)]).then_inc(gpsimd_done, po.step())
                        eng.wait_ge(gpsimd_done, po.own())
                        eng.wait_ge(vector_done, po.at((loop, "y_rows", b)))
                        eng.sem_inc(pool_go, 1)
                        eng.indirect_dma_start(y_dram[l], bass.IndirectOffsetOnAxis(ap=now_u[:, 1, s_:s_ + 1], axis=0),
                                               y_rows[:, s_, :], None, bounds_check=pair_limit,
                                               oob_is_err=False).then_inc(y_stored[s_], 16)

            mod_load(0)
            mod_load(1)
            eng.wait_ge(vector_done, po.at("csilu"))
            for i in range(len(MODS)):
                for half in range(2):
                    if i >= DVE_MODS:
                        eng.wait_ge(mod_w_landed[half], po.at(("mod_w", 2 * i + half)))
                        w = mod_w[:, half]
                        for vi, s in enumerate(mod_slots(i)):
                            if half == 0:
                                q = sidx[i][vi]
                                eng.wait_ge(tensor_done, po.at(("full",) + jobname("mod", owner[q - 4])))
                            prod = w if vi == len(mod_slots(i)) - 1 else mod_t
                            c_ = col("csilu", (0 if i < 24 else 8 * (1 + vi)) + 4 * half, 4)
                            if (i, half) != (DVE_MODS, 0):
                                eng.wait_ge(gpsimd_done, po.own())
                            g.tensor_tensor(prod, w, c_.unsqueeze(2).broadcast_to([P, 4, S]), ALU.mult).then_inc(gpsimd_done, po.step())
                            eng.wait_ge(gpsimd_done, po.own())
                            g.tensor_tensor(prod[:, 0:2], prod[:, 0:2], prod[:, 2:4], ALU.add).then_inc(gpsimd_done, po.step())
                            eng.wait_ge(gpsimd_done, po.own())
                            if half:
                                g.tensor_tensor(prod[:, 0], prod[:, 0], prod[:, 1], ALU.add).then_inc(gpsimd_done, po.step())
                                eng.wait_ge(gpsimd_done, po.own())
                                g.tensor_tensor(mod_acc[:, s, :], mod_acc[:, s, :], prod[:, 0], ALU.add).then_inc(gpsimd_done, po.step([("mod_half", 2 * i + 1), ("mod_acc", i)]))
                            else:
                                g.tensor_tensor(mod_acc[:, s, :], prod[:, 0], prod[:, 1], ALU.add).then_inc(gpsimd_done, po.step(("mod_half", 2 * i)))
                    if 2 * (i + 1) + half < 2 * len(MODS):
                        mod_load(2 * (i + 1) + half)
                if i == (19 if stage_on(3) else len(MODS) - 1) and stage_on(2):
                    moe(0)
            if stage_on(4):
                moe(1)


def host_constants():
    import numpy as np
    p = np.arange(P)[:, None]
    t = {}
    t["ident"] = np.eye(P)
    m = np.arange(S)[None, :]
    t["mask_next"] = np.where(m >= p, 0.0, -1e30)
    k = np.arange(P)[None, :]
    t["window"] = np.concatenate([np.where(k >= p, 0, -1e30), np.zeros((P, P)), np.where(k <= p, 0, -1e30)], 1)
    t["rank"] = np.broadcast_to(np.arange(8, 0, -1), (P, 8))
    t["inv_count"] = np.concatenate([np.broadcast_to(np.float32(1) / np.minimum(np.arange(1, 17), w), (P, 16))
                                     for w in (2, 4, 8, 16)], 1)
    rot = np.zeros((P, P))
    for h in range(2):
        for j in range(32):
            rot[64 * h + 32 + j, 64 * h + j] = -1.0
            rot[64 * h + j, 64 * h + 32 + j] = 1.0
    t["rot"] = rot
    inv = np.float32(10000.0) ** (-np.arange(16, dtype=np.float32) / np.float32(16))
    pos = np.arange(S)
    ang = np.concatenate([(pos // 64).astype(np.float32)[:, None] * inv, (pos % 64).astype(np.float32)[:, None] * inv], 1)
    t["cos"] = np.tile(np.cos(ang).T, (4, 1))
    t["sin"] = np.tile(np.sin(ang).T, (4, 1))
    d = np.arange(896)[None, :] - 384 - p
    t["dplus"], t["dminus"] = np.maximum(d, 0), np.maximum(-d, 0)
    i = np.arange(S)[None, :]
    t["to_end"] = i + L - p
    t["to_start"] = S - i + p
    t["prefix"] = (p <= np.arange(32)[None, :]) * 1.0
    t["thresholds"] = np.broadcast_to(np.arange(4) * P, (P, 4))
    t["block_no"] = np.broadcast_to(np.arange(BLOCKS), (P, BLOCKS))
    t["pair_less"] = p + P * np.arange(8)[None, :] - NO_PAIR
    t["block_start"] = np.broadcast_to(P * np.arange(BLOCKS + 1), (P, BLOCKS + 1))
    t["lane"] = np.broadcast_to(np.arange(P), (P, P))
    return np.ascontiguousarray(np.concatenate([np.broadcast_to(t[n], (P, w)) for n, w in CONST_COLS], 1), np.float32)


UPTO = 99


def layout(inputs):
    import numpy as np
    big = ["x", "ctx_2", "ada_w", "mix_w_in", "pool_w", "mix_w_out", "ssm_w_in", "ssm_w_out", "moe_w1", "moe_w3",
           "moe_w2", "w_mod_2", "w_in_2", "w_branch_2", "w_out_2", "ssm_dt_bias", "ssm_A_log"]
    arrays = {n: np.ascontiguousarray(inputs[n]) for n in big}
    rows = []
    for n, k in VEC_ROWS:
        if n.startswith("pad"):
            v = np.zeros((k, P), np.float32)
        elif n == "ssm_D":
            v = np.repeat(np.asarray(inputs[n])[0], 64).reshape(k, P)
        elif n in ("cf_conv_w_2a", "cf_conv_w_2b"):
            v = np.asarray(inputs["cf_conv_w_2"])[int(n[-1] == "b")].reshape(k, P)
        else:
            v = np.asarray(inputs[n]).reshape(k, P)
        rows.append(v)
    arrays["vecs"] = np.concatenate(rows, 0)
    arrays["w_router"] = np.concatenate([np.asarray(inputs["moe_w_group"]),
                                         np.asarray(inputs["moe_w_expert"]).reshape(2, D, 32)], 2)
    arrays["small"] = np.concatenate([np.concatenate([np.asarray(inputs["moe_b_group"]),
                                                      np.asarray(inputs["moe_b_expert"]).reshape(2, 32)], 1).reshape(-1),
                                      np.asarray(inputs["ret_decay_2"]).reshape(-1),
                                      np.asarray(inputs["att_sink_2"]).reshape(-1)])[None, :]
    rel = np.asarray(inputs["rel_bias"])[0][:, ::-1]
    rel = np.concatenate([np.repeat(rel[:, :1], 255, 1), rel[:, :385]], 1)
    arrays["rel_tiles"] = np.stack([rel[:, P - 1 - q:P - 1 - q + S] for q in range(P)], 1)
    arrays["consts"] = host_constants()
    return {n: np.ascontiguousarray(v) for n, v in arrays.items()}


def kernel(**inputs):
    from concourse import bacc
    from concourse.bass_utils import run_bass_kernel_spmd

    arrays = layout(inputs)
    marks = {}
    for _ in range(2):
        nc = bacc.Bacc("TRN2", target_bir_lowering=False, num_devices=1, dynamic_dma_scratch_size=8192)
        aps = {n: nc.dram_tensor(f"in_{n}", v.shape, mybir.dt.from_np(v.dtype), kind="ExternalInput").ap()
               for n, v in arrays.items()}
        result = nc.dram_tensor("result_dram", (1, S, D), F32, kind="ExternalOutput").ap()
        found = {}
        program(nc, aps, result, UPTO, marks, found)
        marks = found
    r = run_bass_kernel_spmd(nc, [{f"in_{n}": v for n, v in arrays.items()}], core_ids=[0])
    return r.results[0]["result_dram"]
```
